# Optimizing a Trainium2 kernel written in Bass

```python
import jax, jax.numpy as jnp
from jax import lax
import numpy as np

D_MODEL = 1024
BATCH = 1
SEQ = 1024
DEPTH = 1

HEAD_DIM = 64
Q_BLOCK = 128
EPS = 1e-6
A_HEADS = 8
A_W = A_HEADS * HEAD_DIM
B_HEADS = 8
B_W = B_HEADS * HEAD_DIM
B_Q_RANK = 256
B_KV_RANK = 128
IDX_HEADS = 8
IDX_DIM = 32
IDX_TOPK_MAX = 256
C_GROUPS = ((128, 1), (512, 4), (2048, 16))
C_HEADS_PER_GROUP = 4
C_HEADS = C_HEADS_PER_GROUP * len(C_GROUPS)
C_W = C_HEADS * HEAD_DIM
IN_WIDTHS = (A_W, A_W, A_W, A_HEADS, A_W,
             B_Q_RANK, B_KV_RANK, IDX_DIM, IDX_HEADS, B_W,
             C_W, C_W, C_W, C_W,
             D_MODEL, D_MODEL, D_MODEL)
D_IN = sum(IN_WIDTHS)

kernel_name = "hybrid_fox_dsa_dilated_gated"

F32 = jnp.float32

def rmsnorm(x, g):
    xf = x.astype(F32)
    y = xf * lax.rsqrt(jnp.mean(xf * xf, axis=-1, keepdims=True) + EPS)
    return (y * g.astype(F32)).astype(x.dtype)

def alibi_slopes(n):
    return jnp.exp2(-8.0 * (jnp.arange(n, dtype=F32) + 1.0) / n)

def _unblock(y, batch, seq):
    return jnp.swapaxes(y, 0, 1).reshape((batch, seq) + y.shape[3:])

def forgetting_attention(q, k, v, log_f):
    B, S, H, Dh = q.shape
    scale = Dh ** -0.5
    c = jnp.cumsum(log_f, axis=1).transpose(0, 2, 1)
    kpos = jnp.arange(S)

    def block(i):
        t0 = i * Q_BLOCK
        qb = lax.dynamic_slice_in_dim(q, t0, Q_BLOCK, 1)
        cb = lax.dynamic_slice_in_dim(c, t0, Q_BLOCK, 2)
        qpos = t0 + jnp.arange(Q_BLOCK)
        logits = jnp.einsum('bqhd,bkhd->bhqk', qb, k, preferred_element_type=F32) * scale
        logits = logits + (cb[..., :, None] - c[..., None, :])
        logits = jnp.where(kpos[None, :] <= qpos[:, None], logits, -jnp.inf)
        p = jax.nn.softmax(logits, axis=-1)
        return jnp.einsum('bhqk,bkhd->bqhd', p.astype(v.dtype), v)

    out = lax.map(block, jnp.arange(S // Q_BLOCK))
    return _unblock(out, B, S)

def dsa_attention(q, k, v, q_idx, k_idx, w_idx, slopes):
    B, S, H, Dh = q.shape
    top_k = min(IDX_TOPK_MAX, S // 4)
    scale = Dh ** -0.5
    kpos = jnp.arange(S)
    bidx = jnp.arange(B)[:, None, None]

    def block(i):
        t0 = i * Q_BLOCK
        qpos = t0 + jnp.arange(Q_BLOCK)
        qib = lax.dynamic_slice_in_dim(q_idx, t0, Q_BLOCK, 1)
        wb = lax.dynamic_slice_in_dim(w_idx, t0, Q_BLOCK, 1)
        dots = jnp.einsum('bqhd,bkd->bqhk', qib, k_idx, preferred_element_type=F32)
        score = jnp.einsum('bqh,bqhk->bqk', wb.astype(F32), jax.nn.relu(dots))
        score = jnp.where(kpos[None, :] <= qpos[:, None], score, -jnp.inf)
        _, sel = lax.top_k(score, top_k)
        ks = k[bidx, sel]
        vs = v[bidx, sel]
        qb = lax.dynamic_slice_in_dim(q, t0, Q_BLOCK, 1)
        logits = jnp.einsum('bqhd,bqkd->bhqk', qb, ks, preferred_element_type=F32) * scale
        dist = (qpos[None, :, None] - sel).astype(F32)
        logits = logits - slopes[None, :, None, None] * dist[:, None]
        valid = sel <= qpos[None, :, None]
        logits = jnp.where(valid[:, None], logits, -jnp.inf)
        p = jax.nn.softmax(logits, axis=-1)
        return jnp.einsum('bhqk,bqkd->bqhd', p.astype(vs.dtype), vs)

    out = lax.map(block, jnp.arange(S // Q_BLOCK))
    return _unblock(out, B, S)

def _dilated_group(q, k, v, slopes, window, dilation):
    B, S, H, Dh = q.shape
    scale = Dh ** -0.5
    n_keys = window // dilation + 1
    kp = jnp.pad(k, ((0, 0), (window, 0), (0, 0), (0, 0)))
    vp = jnp.pad(v, ((0, 0), (window, 0), (0, 0), (0, 0)))
    j = jnp.arange(n_keys)
    rel = jnp.arange(Q_BLOCK)[:, None] + window - j[None, :] * dilation
    dist = (j * dilation).astype(F32)

    def block(i):
        t0 = i * Q_BLOCK
        qpos = t0 + jnp.arange(Q_BLOCK)
        qb = lax.dynamic_slice_in_dim(q, t0, Q_BLOCK, 1)
        kband = lax.dynamic_slice_in_dim(kp, t0, Q_BLOCK + window, 1)
        vband = lax.dynamic_slice_in_dim(vp, t0, Q_BLOCK + window, 1)
        ks = kband[:, rel]
        vs = vband[:, rel]
        logits = jnp.einsum('bqhd,bqjhd->bhqj', qb, ks, preferred_element_type=F32) * scale
        logits = logits - slopes[None, :, None, None] * dist[None, None, None, :]
        valid = (qpos[:, None] - j[None, :] * dilation) >= 0
        logits = jnp.where(valid, logits, -jnp.inf)
        lse = jax.nn.logsumexp(logits, axis=-1)
        p = jnp.exp(logits - lse[..., None])
        o = jnp.einsum('bhqj,bqjhd->bqhd', p.astype(vs.dtype), vs)
        return o, lse.transpose(0, 2, 1)

    o, lse = lax.map(block, jnp.arange(S // Q_BLOCK))
    return _unblock(o, B, S), _unblock(lse, B, S)

def dilated_attention(q, k, v, slopes):
    hg = C_HEADS_PER_GROUP
    outs, lses = [], []
    for g, (window, dilation) in enumerate(C_GROUPS):
        hs = slice(g * hg, (g + 1) * hg)
        o, lse = _dilated_group(q[:, :, hs], k[:, :, hs], v[:, :, hs], slopes[hs], window, dilation)
        outs.append(o)
        lses.append(lse)
    alpha = jax.nn.softmax(jnp.stack(lses, axis=0), axis=0)
    return jnp.concatenate([(alpha[g][..., None] * outs[g]).astype(q.dtype) for g in range(len(C_GROUPS))], axis=2)

def hybrid_layer(x, norm_g, w_in, b_forget, g_cq, w_uq, w_uq_idx, g_ckv, w_ukv, w_a, w_b, w_c, w_o):
    B, S, _ = x.shape
    hd = HEAD_DIM
    h = rmsnorm(x, norm_g)
    proj = h @ w_in
    points = np.cumsum(IN_WIDTHS)[:-1].tolist()
    (qa, ka, va, fa, za, cq, ckv, kidx, widx, zb, qc, kc, vc, zc, ga, gb, gc) = jnp.split(proj, points, axis=-1)

    log_f = jax.nn.log_sigmoid((fa + b_forget).astype(F32))
    ya = forgetting_attention(qa.reshape(B, S, A_HEADS, hd), ka.reshape(B, S, A_HEADS, hd),
                              va.reshape(B, S, A_HEADS, hd), log_f)
    ya = ya.reshape(B, S, A_W) * jax.nn.silu(za)

    cq = rmsnorm(cq, g_cq)
    qb = (cq @ w_uq).reshape(B, S, B_HEADS, hd)
    q_idx = (cq @ w_uq_idx).reshape(B, S, IDX_HEADS, IDX_DIM)
    kv = rmsnorm(ckv, g_ckv) @ w_ukv
    yb = dsa_attention(qb, kv[..., :hd], kv[..., hd:], q_idx, kidx, widx, alibi_slopes(B_HEADS))
    yb = yb.reshape(B, S, B_W) * jax.nn.silu(zb)

    yc = dilated_attention(qc.reshape(B, S, C_HEADS, hd), kc.reshape(B, S, C_HEADS, hd),
                           vc.reshape(B, S, C_HEADS, hd), alibi_slopes(C_HEADS))
    yc = yc.reshape(B, S, C_W) * jax.nn.silu(zc)

    merged = (jax.nn.sigmoid(ga) * (ya @ w_a) + jax.nn.sigmoid(gb) * (yb @ w_b)
              + jax.nn.sigmoid(gc) * (yc @ w_c))
    return (x + merged @ w_o).astype(x.dtype)

def setup_inputs(seed: int = 0) -> dict:
    key = jax.random.key(seed)
    ks = jax.random.split(key, 16)
    nrm = lambda k, shape, fan_in: jax.random.normal(k, shape, F32) * (fan_in ** -0.5)
    return {
        "x": jax.random.normal(ks[0], (BATCH, SEQ, D_MODEL), F32),
        "norm_g": 1.0 + 0.05 * jax.random.normal(ks[1], (DEPTH, D_MODEL), F32),
        "w_in": nrm(ks[2], (DEPTH, D_MODEL, D_IN), D_MODEL),
        "b_forget": 1.0 + 0.5 * jax.random.normal(ks[3], (DEPTH, A_HEADS), F32),
        "g_cq": 1.0 + 0.05 * jax.random.normal(ks[4], (DEPTH, B_Q_RANK), F32),
        "w_uq": nrm(ks[5], (DEPTH, B_Q_RANK, B_W), B_Q_RANK),
        "w_uq_idx": nrm(ks[6], (DEPTH, B_Q_RANK, IDX_HEADS * IDX_DIM), B_Q_RANK),
        "g_ckv": 1.0 + 0.05 * jax.random.normal(ks[7], (DEPTH, B_KV_RANK), F32),
        "w_ukv": nrm(ks[8], (DEPTH, B_KV_RANK, 2 * HEAD_DIM), B_KV_RANK),
        "w_a": nrm(ks[9], (DEPTH, A_W, D_MODEL), A_W),
        "w_b": nrm(ks[10], (DEPTH, B_W, D_MODEL), B_W),
        "w_c": nrm(ks[11], (DEPTH, C_W, D_MODEL), C_W),
        "w_o": nrm(ks[12], (DEPTH, D_MODEL, D_MODEL), D_MODEL),
        "final_g": 1.0 + 0.05 * jax.random.normal(ks[13], (D_MODEL,), F32),
    }

def reference(x, norm_g, w_in, b_forget, g_cq, w_uq, w_uq_idx, g_ckv, w_ukv, w_a, w_b, w_c, w_o, final_g):
    for l in range(DEPTH):
        x = hybrid_layer(x, norm_g[l], w_in[l], b_forget[l], g_cq[l], w_uq[l], w_uq_idx[l],
                         g_ckv[l], w_ukv[l], w_a[l], w_b[l], w_c[l], w_o[l])
    return rmsnorm(x, final_g)


_drawn_inputs = setup_inputs


def setup_inputs(seed=0):
    import zlib

    import numpy as np

    out = dict(_drawn_inputs(seed))
    spreads = {}
    factors = {'g_ckv': 6.884}
    for name, (base, spread) in spreads.items():
        noise = np.random.default_rng([zlib.crc32(name.encode()), seed]).standard_normal(out[name].shape)
        drawn = base * np.exp(spread * noise) if base else spread * noise
        out[name] = __import__('jax').numpy.asarray(drawn.astype(out[name].dtype))
    for name, factor in factors.items():
        out[name] = (out[name] * factor).astype(out[name].dtype)
    return out
```

```python
from contextlib import ExitStack

import numpy as np

import concourse.bass as bass
from concourse import mybir

P = 128
D = 1024
T = 1024
KC = D // P
TB = T // P
HALF = 512
HD = 64
A_HEADS, B_HEADS, C_HEADS, IDX_HEADS = 8, 8, 12, 8
IDX_DIM = 32
TOPK = 256
ROUNDS = TOPK // 8
EPS = 1e-6
SCALE = HD ** -0.5
C_GROUPS = ((128, 1), (512, 4), (2048, 16))
NEG = -1e30
CAUSAL = -1e38
TAKEN = -3e38

WIDTHS = (("qa", 512), ("ka", 512), ("va", 512), ("fa", 8), ("za", 512), ("cq", 256), ("ckv", 128), ("kidx", 32),
          ("widx", 8), ("zb", 512), ("qc", 768), ("kc", 768), ("vc", 768), ("zc", 768), ("ga", D), ("gb", D), ("gc", D))
COL, at = {}, 0
for _n, _w in WIDTHS:
    COL[_n] = at
    at += _w
D_IN = at

F32, F32R, BF16 = mybir.dt.float32, mybir.dt.float32r, mybir.dt.bfloat16
ALU = mybir.AluOpType
ACTF = mybir.ActivationFunctionType
AX = mybir.AxisListType

RAW = 3
SPL = 3
PTS = 4
NCH = {"a": 4, "b": 4, "c": 6}


def c_slope(h):
    return float(np.float32(2.0 ** (-8.0 * (h + 1) / C_HEADS)))


def build_plan():
    plan, uses, blocks = [], [0] * 4, []
    count = {"ring": 0, "tp": 0, "hs": 0, "S": 0, "unit": 0, "stage": 0}
    tiles, unit_of_tp, units_seen, y_turn_of = {}, [], [], []

    def use(b):
        uses[b] += 1
        return b, uses[b] - 1

    def ring():
        count["ring"] += 1
        return use(2 + count["ring"] % 2)

    def nxt(name, n=1):
        count[name] += n
        return count[name] - n

    def step(kind, **kw):
        plan.append((kind, kw))
        return kw

    def tile(kind, c, src, chunks=KC, split=False, **kw):
        u = [use(0), use(1)]
        for base in range(0, chunks, 4):
            nk = min(4, chunks - base)
            last = base + nk == chunks
            blocks.append(dict(kind=kind, nk=nk, c=c, base=base, last=last, done=u[1]))
            step("block", n=len(blocks) - 1, base=base, nk=nk, u=u, first=base == 0, last=last, src=src)
        if split:
            kw["hs"] = nxt("hs", 2)
        tiles[kind, c] = u
        return step(kind[0] if kind[0] in "zgw" and len(kind) == 2 else kind, c=c, u=u, **kw)

    def softmax_run(units, tail=None):
        n = len(units)
        for s in range(n + 2):
            if s < n:
                units[s].update(S=nxt("S"), unit=nxt("unit"))
                units_seen.append(units[s])
                plan.append(("logits", units[s]))
            if s == n and tail:
                tail()
            if 1 <= s <= n:
                x = units[s - 1]
                chunks = x["W"] // P
                x["groups"] = []
                for c0 in range(0, chunks, 4):
                    x["groups"].append(dict(use=ring(), tp=nxt("tp"), c0=c0, nc=min(4, chunks - c0)))
                    unit_of_tp.append(x)
                plan.append(("turn", x))
            if s >= 2:
                x = units[s - 2]
                if x["b"] % 4 == 0:
                    count["stage"] += 1
                x["pv"], x["stage"] = ring(), count["stage"] - 1
                plan.append(("pv", x))
                if x["b"] % 4 == 3:
                    y_turn_of.append(ring())
                    step("y_turn", use=y_turn_of[-1], x=x)

    def attend(br, ch, tail):
        for half in range(2):
            tiles["V" + br, ch, half] = ring()
            step("v_turn", br=br, ch=ch, half=half, use=tiles["V" + br, ch, half])
        units = []
        for hh in range(2):
            if br == "a":
                tiles["negc", 2 * ch + hh] = [ring(), ring()]
                step("c_bcast", h=2 * ch + hh, u=tiles["negc", 2 * ch + hh])
            for b in range(TB):
                W = {0: P * min(b + 1, 2), 1: P * (b % 2 + 1), 2: P}[ch // 2] if br == "c" else P * (b + 1)
                units.append(dict(br=br, ch=ch, hh=hh, b=b, W=W, qk=[tiles["q" + br, ch], tiles["k" + br, ch]],
                                  vt=tiles["V" + br, ch, 1]))
        softmax_run(units, tail)

    def merge(br):
        n = NCH[br]
        for c in range(n):
            share = [ring(), ring()] if br == "c" else None
            if br == "c":
                step("share", c=c, u=share)
            tile("z" + br, c, "h", split=True, br=br, share=share)
        for c in range(KC):
            tile("g" + br, c, "h", br=br)
            tile("w" + br, c, "y", chunks=n, br=br, gate=tiles["g" + br, c])

    step("phase", name="x")
    for kc in range(KC):
        for th in range(2):
            step("x_turn", kc=kc, th=th, use=ring(), hs=nxt("hs"))
    step("phase", name="small")
    tile("cq", 0, "h")
    tile("cq", 1, "h")
    tile("ckv", 2, "h")
    tile("small", 0, "h")
    for name, first, n in (("cq", 0, 2), ("ckv", 2, 1)):
        step("rms", name=name, first_chunk=first, n=n, u=[use(0), use(1)], hs=nxt("hs", 2 * n))
    step("forget")
    step("natural", u=[ring(), ring()])
    step("phase", name="index")
    step("b_k", u=[use(0), use(1)], hs=nxt("hs", 2))
    step("b_v", u=[use(0)])
    for h in range(B_HEADS):
        step("b_q", h=h, u=[use(0), use(1)], hs=nxt("hs", 2))
    for h in range(IDX_HEADS + 1):
        if h < IDX_HEADS:
            step("i_q", h=h, u=[use(0), use(1)], hs=nxt("hs", 2))
            low_of = count["hs"]
        if h:
            for i in range(2, TB):
                step("i_dots", h=h - 1, i=i, S=nxt("S"), n=(h - 1) * 6 + i - 2, low=low_of - (2 if h < IDX_HEADS else 0))
    step("phase", name="c")
    tile("qc", 0, "h")
    for ch in range(6):
        tile("kc", ch, "h")
        tile("vc", ch, "h")
        attend("c", ch, (lambda: tile("qc", ch + 1, "h")) if ch < 5 else None)
    step("phase", name="c_stats")
    for g in range(3):
        for half in range(2):
            step("stat_turn", g=g, half=half, use=ring())
    step("stat_back", use=ring())
    for half in range(2):
        step("share_turn", half=half, use=ring())
    step("phase", name="c_merge")
    merge("c")
    step("phase", name="a")
    tile("qa", 0, "h")
    for ch in range(4):
        tile("ka", ch, "h")
        tile("va", ch, "h")
        attend("a", ch, (lambda: tile("qa", ch + 1, "h")) if ch < 3 else None)
    step("phase", name="a_merge")
    merge("a")
    step("phase", name="b")
    softmax_run([dict(br="b", ch=h // 2, hh=h % 2, b=b, W=(b + 1) * P, h=h, qk=[], vt=None)
                 for h in range(B_HEADS) for b in range(TB)])
    step("phase", name="b_merge")
    merge("b")
    step("phase", name="o")
    first_wo = len(blocks)
    for half in range(2):
        for cc in range(KC):
            blocks.append(dict(kind="wo", nk=4, c=cc, half=half))
    step("final", first=first_wo, uses=list(uses), S=count["S"])
    return plan, blocks, dict(unit_of_tp=unit_of_tp, units=units_seen, y_turns=y_turn_of, tiles=tiles, first_wo=first_wo)


def hybrid_layer_kernel(nc, x, norm_g, w_in, b_forget, g_cq, w_uq, w_uq_idx, g_ckv, w_ukv, w_a, w_b, w_c, w_o, final_g,
                        out):
    plan, blocks, info = build_plan()
    tiles, units = info["tiles"], info["units"]
    with ExitStack() as ctx:
        def sb(name, shape, dt=F32, es=ctx):
            return es.enter_context(nc.sbuf_tensor(name, shape, dt))

        def psum(name, cols):
            return ctx.enter_context(nc.psum_tensor(name, [P, cols], F32))

        def sem(name):
            return ctx.enter_context(nc.semaphore(name))

        hs = sb("hs", [P, 2, KC, T], F32R)
        w_raw = sb("w_raw", [P, RAW, 4, P])
        w_hl = sb("w_hl", [P, SPL, 2, 4, P], F32R)
        score = sb("score", [P, P * TB * (TB + 1) // 2])
        cumT = sb("cumT", [A_HEADS, T])
        ident = sb("ident", [P, P])
        ones = sb("ones", [P, P])
        ident_b = sb("ident_b", [P, P], BF16)
        tri_b = sb("tri_b", [P, P], BF16)
        band = sb("band", [P, 2 * P])
        pairs = sb("pairs", [P, P])
        gn = sb("gn", [P, KC])
        gq = sb("gq", [P, 3])
        bf = sb("bf", [A_HEADS, 1])
        wnat = sb("wnat", [P, TB, IDX_HEADS])
        top8 = sb("top8", [P, 8])
        stat = sb("stat", [P, 3, TB, 2, 4])
        nmax = sb("nmax", [P, 8])
        den = sb("den", [P, 8])
        rden = sb("rden", [P, 8])
        ssq = sb("ssq", [P, TB])
        rstd = sb("rstd", [P, 3, TB])
        stage = sb("stage", [P, 2, 4, HD])

        def at(kib, name, shape, dt=F32):
            with ExitStack() as es:
                if kib:
                    sb(name + "_below", [P, int(kib * 256)], F32, es)
                return sb(name, shape, dt, es)

        xn, junk = at(0, "xn", [P, TB, D]), at(32, "junk", [P, D])
        cq_hl, ckv_hl = at(0, "cq_hl", [P, 2, 2, T], F32R), at(16, "ckv_hl", [P, 2, T], F32R)
        uq_hl = at(24, "uq_hl", [P, 2, 2, B_HEADS, 2, HD], F32R)
        ix_hl = at(40, "ix_hl", [P, 2, 2, IDX_HEADS, 4, IDX_DIM], F32R)
        ukv_hl, kidx_hl = at(56, "ukv_hl", [P, 2, 3, HD], F32R), at(58, "kidx_hl", [P, T], F32R)
        uq_raw, ix_raw = at(62, "uq_raw", [P, 2, B_HEADS, HD]), at(66, "ix_raw", [P, 2, IDX_HEADS, IDX_DIM])
        ukv_raw, c_raw = at(68, "ukv_raw", [P, 2, HD]), at(69, "c_raw", [P, 3, T])
        c_tmp, small = at(81, "c_tmp", [P, 2, T]), at(89, "small", [P, T])
        q_st, relu_t, v_st = at(69, "q_st", [P, 2, T], F32R), at(77, "relu_t", [P, 2, T]), at(85, "v_st", [P, TB, HD])
        Y = {"c": at(0, "yc", [P, 6, T]), "a": at(0, "ya", [P, 4, T]), "b": at(0, "yb", [P, 4, T])}
        Q = {"c": at(24, "qc", [P, T]), "a": at(16, "qa", [P, T])}
        K = {"c": at(28, "kc", [P, T]), "a": at(20, "ka", [P, T])}
        VT = {"c": at(32, "vtc", [P, T]), "a": at(24, "vta", [P, T])}
        V = {"c": at(36, "vc", [P, TB, P]), "a": at(28, "va", [P, TB, P]), "b": at(24, "vb", [P, TB, HD])}
        PR = {"c": at(40, "pc", [P, 2, 2 * P]), "a": at(32, "pa", [P, 2, T]), "b": at(34, "pb", [P, 2, T])}
        PT = {"c": at(42, "ptc", [P, PTS, 4, P]), "a": at(40, "pta", [P, PTS, 4, P]), "b": at(42, "ptb", [P, PTS, 4, P])}
        bmc = at(50, "bmc", [P, 2, 2 * P])
        negc, selA = at(48, "negc", [P, 2, T]), at(88, "selA", [A_HEADS, A_HEADS, P])
        khb, qb, srow = at(16, "khb", [P, 2, T], F32R), at(26, "qb", [P, 2, T], F32R), at(50, "srow", [P, T])
        statT, natS = at(24, "statT", [8, 3, T]), at(36, "natS", [P, TB, 3, 2, 4])
        eS, wS, shareN = at(37, "eS", [P, 3, TB, 4]), at(38, "wS", [P, 3, TB, 4]), at(39, "shareN", [P, TB, 3, 4])
        mxS = at(40, "mxS", [P, TB, 4])
        shareT, selC = at(88, "shareT", [C_HEADS, T]), at(92, "selC", [C_HEADS, C_HEADS, HD])
        YH = {"c": at(0, "ych", [P, 6, T], F32R), "a": at(0, "yah", [P, 4, T], F32R), "b": at(0, "ybh", [P, 4, T], F32R)}
        YL = {"c": at(24, "ycl", [P, 6, T], F32R), "a": at(16, "yal", [P, 4, T], F32R), "b": at(16, "ybl", [P, 4, T], F32R)}
        tm = at(48, "tm", [P, 4, HALF])
        mT = at(56, "mT", [P, KC, T])
        wo_hl = [at(0, "wo0", [P, 2, KC, HALF], F32R), at(56, "wo1", [P, 2, KC, HALF], F32R)]
        xo_lo = at(32, "xo_lo", [P, 6, D])
        xo = [xo_lo[:, b, :] if b < 6 else score[:, (b - 6) * D:(b - 5) * D] for b in range(TB)]
        fg = score[:, 2 * D:3 * D]
        junk_o = score[:, 3 * D:4 * D]

        bank = [psum(f"bank{i}", HALF) for i in range(4)]
        slot = [psum(f"slot{i}", T) for i in range(2)]
        banks8 = [bank[0][:], bank[1][:], bank[2][:], bank[3][:], slot[0][:, 0:HALF], slot[0][:, HALF:T],
                  slot[1][:, 0:HALF], slot[1][:, HALF:T]]

        qb_dram = nc.dram_tensor("qb_scratch", [B_HEADS, P, T], F32R, kind="Internal").ap()
        kb_dram = nc.dram_tensor("kb_scratch", [P, 2, T], F32R, kind="Internal").ap()
        vb_dram = nc.dram_tensor("vb_scratch", [P, TB, HD], F32, kind="Internal").ap()

        consts_in, x_in, fg_in, xo_in = sem("consts_in"), sem("x_in"), sem("fg_in"), sem("xo_in")
        pw_in = sem("pw_in")
        raw_in = [sem(f"raw_in{i}") for i in range(RAW)]
        w_high, w_low, w_used = sem("w_high"), sem("w_low"), sem("w_used")
        bank_full = [sem(f"bank_full{i}") for i in range(4)]
        bank_free = [sem(f"bank_free{i}") for i in range(4)]
        s_full, s_free, logit_ready = sem("s_full"), sem("s_free"), sem("logit_ready")
        high_ready, low_ready = sem("high_ready"), sem("low_ready")
        pool_consts, pool_causal, pool_srow = sem("pool_consts"), sem("pool_causal"), sem("pool_srow")
        ones_ready, ssq_ready, var_ready, sd_ready, xs_ready = (sem(n) for n in
            ("ones_ready", "ssq_ready", "var_ready", "sd_ready", "xs_ready"))
        pw_high, pw_low = sem("pw_high"), sem("pw_low")
        rms_sq, rms_var, rms_sd, rms_y = sem("rms_sq"), sem("rms_var"), sem("rms_sd"), sem("rms_y")
        fg_l, cum_ready, kidx_high, kidx_low = sem("fg_l"), sem("cum_ready"), sem("kidx_high"), sem("kidx_low")
        v_ready, kv_spilled, spilled = sem("v_ready"), sem("kv_spilled"), [sem(f"spilled{i}") for i in range(2)]
        relu_used, score_done = sem("relu_used"), sem("score_done")
        bm_ready, sel_ready = sem("bm_ready"), sem("sel_ready")
        st_d, st_e, share_ready = sem("st_d"), sem("st_e"), sem("share_ready")
        z_mul, mixed = sem("z_mul"), sem("mixed")
        kv_in, qb_in = sem("kv_in"), [sem(f"qb_in{i}") for i in range(2)]
        bias_b = sem("bias_b")
        m_high, m_low, o_full, o_free, res_ready = (sem(n) for n in ("m_high", "m_low", "o_full", "o_free", "res_ready"))
        o_ssq, o_var, o_sd, out_ready, stored = (sem(n) for n in ("o_ssq", "o_var", "o_sd", "out_ready", "stored"))
        act_chain, dve_chain = sem("act_chain"), sem("dve_chain")
        ended = {e: sem(f"ended_{e}") for e in ("pe", "act", "dve", "pool")}

        def full(eng, u):
            eng.wait_ge(bank_full[u[0]], u[1] + 1)

        def freed(eng, u):
            eng.wait_ge(bank_free[u[0]], u[1] + 1)

        def claim(pe, u):
            if u[1]:
                pe.wait_ge(bank_free[u[0]], u[1])

        def phase_end(eng, name, k):
            eng.drain().then_inc(ended[name], 1)
            if name != "pe":
                for other in ended:
                    if other != name:
                        eng.wait_ge(ended[other], k)

        def block_done(eng, n):
            if blocks[n]["last"]:
                full(eng, blocks[n]["done"])
            else:
                eng.wait_ge(w_used, sum(not b["last"] for b in blocks[:n + 1]))

        loads, arrived = [], [0] * RAW
        for n, b in enumerate(blocks):
            rows = slice(b.get("base", 0) * P, (b.get("base", 0) + b["nk"]) * P)
            kind, c = b["kind"], b["c"]

            def cols(w, col, width=P):
                return w[rows, col:col + width].rearrange("(k p) c -> p k c", p=P)
            if kind == "wo":
                src = [(None, w_o[0][c * P:(c + 1) * P, b["half"] * HALF:(b["half"] + 1) * HALF])]
            elif kind == "small":
                src = [(0, cols(w_in[0], COL["fa"], 32)), (32, cols(w_in[0], COL["widx"], 32)),
                       (64, cols(w_in[0], COL["kidx"], 32)), (96, cols(w_in[0], COL["kidx"], 32))]
            elif kind in ("wa", "wb", "wc"):
                src = [(0, cols({"wa": w_a, "wb": w_b, "wc": w_c}[kind][0], c * P))]
            else:
                src = [(0, cols(w_in[0], COL[kind] + (c if kind != "ckv" else 0) * P))]
            arrived[n % RAW] += 16 * len(src)
            loads.append((src, arrived[n % RAW]))

        def v_tokens(br, ch, t, b):
            g = ch // 2 if br == "c" else 0
            if g == 1:
                return t.rearrange("q (x r) -> q r x", r=4)[:, b // 2, (b % 2) * P:(b % 2 + 1) * P]
            return t[:, b * P:(b + 1) * P]

        def score_of(i):
            o = P * i * (i + 1) // 2
            return score[:, o:o + P * (i + 1)]

        def logit_bias(u):
            if u["br"] == "a":
                return negc[:, u["hh"], 0:u["W"]]
            if u["br"] == "b":
                return score_of(u["b"])
            return bmc[:, u["hh"], 0:P] if u["ch"] // 2 == 2 else bmc[:, u["hh"], 2 * P - u["W"]:2 * P]

        def stats_of(u):
            if u["br"] == "c":
                h4 = 2 * (u["ch"] % 2) + u["hh"]
                return stat[:, u["ch"] // 2, u["b"], 0, h4:h4 + 1], stat[:, u["ch"] // 2, u["b"], 1, h4:h4 + 1]
            k = u["unit"] % 8
            return nmax[:, k:k + 1], den[:, k:k + 1]

        steps = {}
        for kind, a in plan:
            steps.setdefault(kind, []).append(a)
        last_low = {"w" + br: max(z["hs"] for z in steps["z"] if z["br"] == br) + 2 for br in "cab"}
        z_base = {br: min(z["hs"] for z in steps["z"] if z["br"] == br) for br in "cab"}
        z_count = {"c": 0, "a": 2 * NCH["c"], "b": 2 * (NCH["c"] + NCH["a"])}
        mix_base = {"a": 0, "b": 2 * KC}
        b_low = max(r["hs"] for r in steps["rms"]) + 2
        last_S, last_pv, last_unit = {}, {}, {}
        for u in units:
            last_S[u["br"], u["ch"]] = u["S"]
            last_pv[u["br"], u["ch"]] = u["pv"]
            last_unit[u["br"], 2 * u["ch"] + u["hh"]] = u["unit"]
        units_c = [u for u in units if u["br"] == "c"]
        stat_uses = [a["use"] for a in steps["stat_turn"]]
        share_uses = [a["use"] for a in steps["share_turn"]]

        def turned_room(eng, grp):
            if grp["tp"] >= PTS:
                full(eng, info["unit_of_tp"][grp["tp"] - PTS]["pv"])

        def stage_room(eng, u):
            if u["b"] % 4 == 0 and u["stage"] >= 2:
                full(eng, info["y_turns"][u["stage"] - 2])

        block = ctx.enter_context(nc.Block())

        @block.sync
        def _(sp):
            with nc.allow_non_contiguous_dma(reason="parameters, one value per partition"):
                sp.dma_start(gn[:], norm_g[0].rearrange("(k p) -> p k", p=P)).then_inc(consts_in, 16)
                sp.dma_start(gq[:, 0:2], g_cq[0].rearrange("(k p) -> p k", p=P)).then_inc(consts_in, 16)
                sp.dma_start(gq[:, 2:3], g_ckv[0].rearrange("(k p) -> p k", p=P)).then_inc(consts_in, 16)
                sp.dma_start(bf[:], b_forget[0].rearrange("(h o) -> h o", o=1)).then_inc(consts_in, 16)
            for i in range(TB):
                sp.dma_start(xn[:, i, :], x[0, i * P:(i + 1) * P, :]).then_inc(x_in, 16)
            sp.dma_start(uq_raw[:].rearrange("p k h d -> p k (h d)"),
                         w_uq[0].rearrange("(k p) n -> p k n", p=P)).then_inc(pw_in, 16)
            sp.dma_start(ix_raw[:].rearrange("p k h d -> p k (h d)"),
                         w_uq_idx[0].rearrange("(k p) n -> p k n", p=P)).then_inc(pw_in, 16)
            sp.dma_start(ukv_raw[:].rearrange("p a d -> p (a d)"), w_ukv[0]).then_inc(pw_in, 16)
            for n, (src, _) in enumerate(loads):
                if n >= RAW:
                    sp.wait_ge(w_low, n - RAW + 1)
                for col, ap in src:
                    if col is None:
                        dst = w_raw[:, n % RAW].rearrange("p k c -> p (k c)")
                    else:
                        dst = w_raw[:, n % RAW, 0:blocks[n]["nk"], col:col + ap.shape[2]]
                    sp.dma_start(dst, ap).then_inc(raw_in[n % RAW], 16)
            for b in range(TB):
                sp.wait_ge(out_ready, b + 1)
                sp.dma_start(out[0, b * P:(b + 1) * P, :], xo[b]).then_inc(stored, 16)
            sp.wait_ge(stored, 16 * TB)

        @block.gpsimd
        def _(pool):
            g = nc.gpsimd
            chain = [0]

            def then(ins):
                chain[0] += 1
                ins.then_inc(pool_consts, 1)
                pool.wait_ge(pool_consts, chain[0])

            then(g.memset(ident[:], 0.0))
            then(g.affine_select(ident[:], ident[:], [[-1, P]], ALU.not_equal, 1.0, base=0, channel_multiplier=1))
            then(g.memset(ident_b[:], 0.0))
            then(g.affine_select(ident_b[:], ident_b[:], [[-1, P]], ALU.not_equal, 1.0, base=0, channel_multiplier=1))
            then(g.memset(tri_b[:], 0.0))
            then(g.affine_select(tri_b[:], tri_b[:], [[-1, P]], ALU.is_ge, NEG, base=0, channel_multiplier=1))
            then(g.iota(band[:], [[1, 2 * P]], base=-P, channel_multiplier=-1, allow_small_or_imprecise_dtypes=True))
            then(g.affine_select(band[:], band[:], [[-1, 2 * P]], ALU.is_ge, NEG, base=P, channel_multiplier=1))
            then(g.affine_select(band[:], band[:], [[1, 2 * P]], ALU.is_ge, NEG, base=0, channel_multiplier=-1))
            then(g.memset(pairs[:], NEG))
            for a in range(2):
                sub = pairs[HD * a:HD * a + HD, HD * a:HD * a + HD]
                then(g.iota(sub, [[1, HD]], base=0, channel_multiplier=-1, allow_small_or_imprecise_dtypes=True))
                then(g.affine_select(sub, sub, [[-1, HD]], ALU.is_ge, NEG, base=0, channel_multiplier=1))
            for i in range(2):
                m = score_of(i)
                then(g.iota(m, [[1, P * (i + 1)]], base=-P * i, channel_multiplier=-1,
                            allow_small_or_imprecise_dtypes=True))
                then(g.affine_select(m, m, [[-1, P * (i + 1)]], ALU.is_ge, NEG, base=P * i, channel_multiplier=1))
            k = 0
            for kind, a in plan:
                if kind == "phase":
                    k += 1
                    if k > 1:
                        if a["name"] == "c":
                            pool.wait_ge(kv_spilled, 32)
                            for s in range(2):
                                pool.wait_ge(spilled[s], 16 * (B_HEADS // 2))
                            for i in range(2, TB):
                                pool.wait_ge(score_done, i - 1)
                                m = score_of(i)[:, P * i:P * (i + 1)]
                                g.affine_select(m, m, [[-1, P]], ALU.is_ge, CAUSAL, base=0,
                                                channel_multiplier=1).then_inc(pool_causal, 1)
                        phase_end(pool, "pool", k - 1)
                    if a["name"] == "b":
                        pool.dma_start(khb[:], kb_dram).then_inc(kv_in, 16)
                        pool.dma_start(V["b"][:], vb_dram).then_inc(kv_in, 16)
                        g.iota(srow[:], [[1, T]], base=0, channel_multiplier=-1,
                               allow_small_or_imprecise_dtypes=True).then_inc(pool_srow, 1)
                    if a["name"] == "o":
                        pool.dma_start(fg, final_g.rearrange("(o d) -> o d", o=1).to_broadcast([P, D])).then_inc(fg_in, 16)
                        for b in range(TB):
                            pool.dma_start(xo[b], x[0, b * P:(b + 1) * P, :]).then_inc(xo_in, 16)
                            pool.wait_ge(xo_in, 16 * (b + 1))
                elif kind == "b_k":
                    pool.wait_ge(low_ready, a["hs"] + 2)
                    pool.dma_start(kb_dram, q_st[:]).then_inc(kv_spilled, 16)
                elif kind == "b_v":
                    pool.wait_ge(v_ready, 1)
                    pool.dma_start(vb_dram, v_st[:]).then_inc(kv_spilled, 16)
                elif kind == "b_q":
                    pool.wait_ge(low_ready, a["hs"] + 2)
                    pool.dma_start(qb_dram[a["h"]], q_st[:, a["h"] % 2, :]).then_inc(spilled[a["h"] % 2], 16)
                elif kind == "logits" and a["br"] == "b" and a["b"] == 0:
                    for h in ([0, 1] if a["h"] == 0 else [a["h"] + 1] if a["h"] + 1 < B_HEADS else []):
                        if h >= 2:
                            pool.wait_ge(s_full, a["S"])
                        pool.dma_start(qb[:, h % 2, :], qb_dram[h]).then_inc(qb_in[h % 2], 16)

        @block.tensor
        def _(pe):
            def h_ready(low):
                pe.wait_ge(low_ready, low)

            def split_product(out_, wh, wl, mh, ml, start, stop):
                pe.matmul(out_, wh, mh, start=start, stop=False)
                pe.matmul(out_, wh, ml, start=False, stop=False)
                return pe.matmul(out_, wl, mh, start=False, stop=stop)

            k = 0
            for kind, a in plan:
                if kind == "phase":
                    k += 1
                    if k > 1:
                        phase_end(pe, "pe", k - 1)
                elif kind == "x_turn":
                    if a["kc"] == 0:
                        pe.wait_ge(xs_ready, 4 * a["th"] + 4)
                        pe.wait_ge(pool_consts, 2)
                    claim(pe, a["use"])
                    for j in range(4):
                        ins = pe.transpose(bank[a["use"][0]][:, j * P:(j + 1) * P],
                                           xn[:, 4 * a["th"] + j, a["kc"] * P:(a["kc"] + 1) * P], ident[:])
                    ins.then_inc(bank_full[a["use"][0]], 1)
                elif kind == "block":
                    n, b = a["n"], blocks[a["n"]]
                    pe.wait_ge(w_low, n + 1)
                    if a["first"]:
                        if a["src"] == "h":
                            h_ready(2 * KC)
                        elif b["c"] == 0:
                            pe.wait_ge(low_ready, last_low[b["kind"]])
                    br = b["kind"][1]
                    w = w_hl[:, n % SPL]
                    for th in range(2):
                        if a["first"]:
                            claim(pe, a["u"][th])
                        for kk in range(a["nk"]):
                            c = a["base"] + kk
                            ts = slice(th * HALF, (th + 1) * HALF)
                            mh, ml = ((hs[:, 0, c, ts], hs[:, 1, c, ts]) if a["src"] == "h" else
                                      (YH[br][:, c, ts], YL[br][:, c, ts]))
                            ins = split_product(bank[th][:], w[:, 0, kk, :], w[:, 1, kk, :], mh, ml,
                                                a["first"] and kk == 0, a["last"] and kk == a["nk"] - 1)
                        if a["last"]:
                            ins.then_inc(bank_full[th], 1)
                        elif th == 1:
                            ins.then_inc(w_used, 1)
                elif kind == "rms":
                    pe.wait_ge(rms_sq, 1 if a["name"] == "cq" else 2)
                    pe.wait_ge(ones_ready, 1)
                    for th in range(2):
                        claim(pe, a["u"][th])
                        for c in range(a["n"]):
                            ins = pe.matmul(bank[th][:], ones[:], c_tmp[:, c, th * HALF:(th + 1) * HALF],
                                            start=c == 0, stop=c == a["n"] - 1)
                        ins.then_inc(bank_full[th], 1)
                elif kind == "natural":
                    freed(pe, tiles["small", 0][0])
                    freed(pe, tiles["small", 0][1])
                    for half, u in enumerate(a["u"]):
                        claim(pe, u)
                        for j in range(4):
                            i = 4 * half + j
                            ins = pe.transpose(bank[u[0]][:, j * P:(j + 1) * P], small[:, i * P:(i + 1) * P], ident[:])
                        ins.then_inc(bank_full[u[0]], 1)
                elif kind == "b_k":
                    pe.wait_ge(pw_low, 3)
                    pe.wait_ge(low_ready, b_low)
                    for th in range(2):
                        claim(pe, a["u"][th])
                        ts = slice(th * HALF, (th + 1) * HALF)
                        split_product(bank[th][:], ukv_hl[:, 0, 0:2, :], ukv_hl[:, 1, 0:2, :], ckv_hl[:, 0, ts],
                                      ckv_hl[:, 1, ts], True, True).then_inc(bank_full[th], 1)
                elif kind == "b_v":
                    u = a["u"][0]
                    claim(pe, u)
                    for b in range(TB):
                        tk = slice(b * P, (b + 1) * P)
                        ins = split_product(bank[0][:, b * HD:(b + 1) * HD], ckv_hl[:, 0, tk], ckv_hl[:, 1, tk],
                                            ukv_hl[:, 0, 2, :], ukv_hl[:, 1, 2, :], True, True)
                    ins.then_inc(bank_full[0], 1)
                elif kind in ("b_q", "i_q"):
                    w = (uq_hl if kind == "b_q" else ix_hl)
                    for th in range(2):
                        claim(pe, a["u"][th])
                        ts = slice(th * HALF, (th + 1) * HALF)
                        for c in range(2):
                            ins = split_product(bank[th][:], w[:, 0, c, a["h"]], w[:, 1, c, a["h"]],
                                                cq_hl[:, 0, c, ts], cq_hl[:, 1, c, ts], c == 0, c == 1)
                        ins.then_inc(bank_full[th], 1)
                elif kind == "i_dots":
                    if a["i"] == 2:
                        pe.wait_ge(low_ready, a["low"])
                        pe.wait_ge(kidx_low, 1)
                    if a["S"] >= 2:
                        pe.wait_ge(s_free, a["S"] - 1)
                    W = (a["i"] + 1) * P
                    for c0 in range(0, W, HALF):
                        c1 = min(W, c0 + HALF)
                        ins = pe.matmul(slot[a["S"] % 2][:, c0:c1], q_st[:, a["h"] % 2, a["i"] * P:(a["i"] + 1) * P],
                                        kidx_hl[:, c0:c1], start=True, stop=True)
                    ins.then_inc(s_full, 1)
                elif kind == "v_turn":
                    br = a["br"]
                    for u in tiles["v" + br, a["ch"]]:
                        freed(pe, u)
                    claim(pe, a["use"])
                    for j in range(4):
                        ins = pe.transpose(bank[a["use"][0]][:, j * P:(j + 1) * P],
                                           v_tokens(br, a["ch"], VT[br][:], 4 * a["half"] + j), ident[:])
                    ins.then_inc(bank_full[a["use"][0]], 1)
                elif kind == "c_bcast":
                    pe.wait_ge(cum_ready, 1)
                    pe.wait_ge(sel_ready, 2)
                    for th, u in enumerate(a["u"]):
                        claim(pe, u)
                        pe.matmul(bank[u[0]][:], selA[:, a["h"], :], cumT[:, th * HALF:(th + 1) * HALF],
                                  start=True, stop=True).then_inc(bank_full[u[0]], 1)
                elif kind == "logits":
                    br, W = a["br"], a["W"]
                    for tile_uses in a["qk"]:
                        for u in tile_uses:
                            freed(pe, u)
                    if br == "b" and a["b"] == 0:
                        pe.wait_ge(kv_in, 32)
                        pe.wait_ge(qb_in[a["h"] % 2], 16 * (a["h"] // 2 + 1))
                    if a["S"] >= 2:
                        pe.wait_ge(s_free, a["S"] - 1)
                    o = slot[a["S"] % 2]
                    if br == "b":
                        q = qb[:, a["h"] % 2, a["b"] * P:(a["b"] + 1) * P]
                        for c0 in range(0, W, HALF):
                            c1 = min(W, c0 + HALF)
                            pe.matmul(o[:, c0:c1], q, khb[:, 0, c0:c1], start=True, stop=False)
                            ins = pe.matmul(o[:, c0:c1], q, khb[:, 1, c0:c1], start=False, stop=True)
                    else:
                        rows = slice(HD * a["hh"], HD * a["hh"] + HD)
                        q = v_tokens(br, a["ch"], Q[br][rows, :], a["b"])
                        g = a["ch"] // 2 if br == "c" else 0
                        if br == "c" and g == 0:
                            keys = K[br][rows, (a["b"] + 1) * P - W:(a["b"] + 1) * P]
                        elif g == 1:
                            keys = K[br][rows, :].rearrange("q (x r) -> q r x", r=4)[:, a["b"] // 2, 0:W]
                        elif g == 2:
                            keys = v_tokens(br, a["ch"], K[br][rows, :], a["b"])
                        if br == "c":
                            ins = pe.matmul(o[:, 0:W], q, keys, start=True, stop=True)
                        else:
                            for c0 in range(0, W, HALF):
                                c1 = min(W, c0 + HALF)
                                pe.matmul(o[:, c0:c1], q, K[br][rows, c0:c1], start=True, stop=c1 < W)
                            ins = pe.matmul(o[:, W - P:W], ident_b[:], tri_b[:], start=False, stop=True)
                    ins.then_inc(s_full, 1)
                elif kind == "turn":
                    pe.wait_ge(s_free, a["S"] + 1)
                    pr = PR[a["br"]][:, a["unit"] % 2]
                    for grp in a["groups"]:
                        claim(pe, grp["use"])
                        for j in range(grp["nc"]):
                            c = grp["c0"] + j
                            ins = pe.transpose(bank[grp["use"][0]][:, j * P:(j + 1) * P], pr[:, c * P:(c + 1) * P], ident[:])
                        ins.then_inc(bank_full[grp["use"][0]], 1)
                elif kind == "pv":
                    for grp in a["groups"]:
                        freed(pe, grp["use"])
                    if a["vt"]:
                        freed(pe, a["vt"])
                    claim(pe, a["pv"])
                    n = a["W"] // P
                    first = a["b"] + 1 - n
                    if a["br"] == "c" and a["ch"] // 2 == 1:
                        first = a["b"] // 2 * 2
                    for grp in a["groups"]:
                        for j in range(grp["nc"]):
                            c = grp["c0"] + j
                            v = (V["b"][:, c, :] if a["br"] == "b" else
                                 V[a["br"]][:, first + c, HD * a["hh"]:HD * a["hh"] + HD])
                            ins = pe.matmul(bank[a["pv"][0]][:, 0:HD], PT[a["br"]][:, grp["tp"] % PTS, j, :], v,
                                            start=c == 0, stop=c == n - 1)
                    ins.then_inc(bank_full[a["pv"][0]], 1)
                elif kind == "y_turn":
                    x = a["x"]
                    freed(pe, x["pv"])
                    claim(pe, a["use"])
                    for j in range(4):
                        ins = pe.transpose(bank[a["use"][0]][0:HD, j * P:(j + 1) * P], stage[:, x["stage"] % 2, j, :], ident[:])
                    ins.then_inc(bank_full[a["use"][0]], 1)
                elif kind == "stat_turn":
                    claim(pe, a["use"])
                    if a["g"] == 0 and a["half"] == 0:
                        pe.wait_ge(s_free, units_c[-1]["S"] + 1)
                    for j in range(4):
                        b = 4 * a["half"] + j
                        ins = pe.transpose(bank[a["use"][0]][0:8, j * P:(j + 1) * P],
                                           stat[:, a["g"], b].rearrange("p a h -> p (a h)"), ident[:])
                    ins.then_inc(bank_full[a["use"][0]], 1)
                elif kind == "stat_back":
                    for u in stat_uses:
                        freed(pe, u)
                    claim(pe, a["use"])
                    for i in range(TB):
                        for g in range(3):
                            o = (i * 3 + g) * 8
                            ins = pe.transpose(bank[a["use"][0]][:, o:o + 8], statT[:, g, i * P:(i + 1) * P], ident[0:8, 0:8])
                    ins.then_inc(bank_full[a["use"][0]], 1)
                elif kind == "share_turn":
                    pe.wait_ge(share_ready, 1)
                    claim(pe, a["use"])
                    for j in range(4):
                        ins = pe.transpose(bank[a["use"][0]][0:C_HEADS, j * P:(j + 1) * P],
                                           shareN[:, 4 * a["half"] + j].rearrange("p g h -> p (g h)"), ident[:])
                    ins.then_inc(bank_full[a["use"][0]], 1)
                elif kind == "share":
                    for u in share_uses:
                        freed(pe, u)
                    pe.wait_ge(sel_ready, 1)
                    for th, u in enumerate(a["u"]):
                        claim(pe, u)
                        pe.matmul(bank[u[0]][:], selC[:, 2 * a["c"]:2 * a["c"] + 2, :].rearrange("p h d -> p (h d)"),
                                  shareT[:, th * HALF:(th + 1) * HALF], start=True, stop=True).then_inc(bank_full[u[0]], 1)
                elif kind == "final":
                    for b in range(4):
                        pe.wait_ge(bank_free[b], a["uses"][b])
                    pe.wait_ge(s_free, a["S"])
                    for half in range(2):
                        if half == 0:
                            order = [(cc, tb) for cc in range(KC) for tb in range(TB)]
                        else:
                            order = [(cc, tb) for tb in range(TB) for cc in range(KC)]
                        for cc, tb in order:
                            if half == 0 and tb == 0:
                                pe.wait_ge(m_low, cc + 1)
                                pe.wait_ge(w_low, a["first"] + cc + 1)
                            if half == 1 and cc == 0:
                                pe.wait_ge(o_free, tb + 1)
                                if tb == 0:
                                    pe.wait_ge(w_low, a["first"] + 2 * KC)
                            tk = slice(tb * P, (tb + 1) * P)
                            w = wo_hl[half]
                            ins = split_product(banks8[tb], hs[:, 0, cc, tk], hs[:, 1, cc, tk], w[:, 0, cc, :], w[:, 1, cc, :],
                                                cc == 0, cc == KC - 1)
                            if cc == KC - 1:
                                ins.then_inc(o_full, 1)

        @block.scalar
        def _(act):
            A = nc.scalar.activation
            chain = [0]
            done = [0]

            def then(ins):
                chain[0] += 1
                ins.then_inc(act_chain, 1)
                act.wait_ge(act_chain, chain[0])

            def split_high(upto):
                while done[0] < min(upto, len(blocks)):
                    n = done[0]
                    b = blocks[n]
                    done[0] += 1
                    act.wait_ge(raw_in[n % RAW], loads[n][1])
                    if b["kind"] == "wo":
                        dst = wo_hl[b["half"]][:, 0, b["c"], :]
                        src = w_raw[:, n % RAW].rearrange("p k c -> p (k c)")
                    else:
                        if n >= SPL:
                            block_done(act, n - SPL)
                        dst, src = w_hl[:, n % SPL, 0, 0:b["nk"], :], w_raw[:, n % RAW, 0:b["nk"], :]
                    A(dst, src, ACTF.Copy).then_inc(w_high, 1)

            k = 0
            for kind, a in plan:
                if kind == "phase":
                    k += 1
                    if k > 1:
                        phase_end(act, "act", k - 1)
                    if a["name"] == "x":
                        act.wait_ge(x_in, 16 * TB)
                        for i in range(TB):
                            ins = A(junk[:], xn[:, i, :], ACTF.Square, accum_out=ssq[:, i:i + 1])
                            then(ins)
                        act.wait_ge(var_ready, 1)
                        A(rstd[:, 1], rstd[:, 0], ACTF.Sqrt).then_inc(sd_ready, 1)
                    if a["name"] == "small":
                        act.wait_ge(pw_in, 48)
                        for r in range(2):
                            A(uq_hl[:, 0, :, :, r, :], uq_raw[:], ACTF.Copy)
                        for r in range(4):
                            ins = A(ix_hl[:, 0, :, :, r, :], ix_raw[:], ACTF.Copy)
                        for r, s in ((0, 0), (1, 0), (2, 1)):
                            ins = A(ukv_hl[:, 0, r, :], ukv_raw[:, s, :], ACTF.Copy)
                        ins.then_inc(pw_high, 1)
                elif kind == "x_turn":
                    full(act, a["use"])
                    A(hs[:, 0, a["kc"], a["th"] * HALF:(a["th"] + 1) * HALF], bank[a["use"][0]][:], ACTF.Copy,
                      scale=gn[:, a["kc"]:a["kc"] + 1]).then_inc(high_ready, 1)
                elif kind == "block":
                    split_high(min(a["n"] + SPL, info["first_wo"]))
                elif kind in ("cq", "ckv", "small"):
                    for th in range(2):
                        full(act, a["u"][th])
                        dst = small[:] if kind == "small" else c_raw[:, a["c"], :]
                        A(dst[:, th * HALF:(th + 1) * HALF], bank[th][:], ACTF.Copy).then_inc(bank_free[th], 1)
                elif kind == "rms":
                    for c in range(a["n"]):
                        ch = a["first_chunk"] + c
                        for u in tiles["cq" if ch < 2 else "ckv", ch]:
                            freed(act, u)
                        if a["name"] == "ckv" and c == 0:
                            act.wait_ge(rms_y, 2)
                        ins = A(c_tmp[:, c, :], c_raw[:, ch, :], ACTF.Square)
                    ins.then_inc(rms_sq, 1)
                    for th in range(2):
                        kk = 2 * (a["name"] == "ckv") + th
                        act.wait_ge(rms_var, kk + 1)
                        v = c_tmp[:, 0, th * HALF:(th + 1) * HALF]
                        A(v, v, ACTF.Sqrt).then_inc(rms_sd, 1)
                    for c in range(a["n"]):
                        ch = a["first_chunk"] + c
                        act.wait_ge(rms_y, ch + 1)
                        dst = ckv_hl[:, 0, :] if ch == 2 else cq_hl[:, 0, ch, :]
                        for th in range(2):
                            ts = slice(th * HALF, (th + 1) * HALF)
                            A(dst[:, ts], c_raw[:, ch, ts], ACTF.Copy).then_inc(high_ready, 1)
                elif kind == "forget":
                    act.wait_ge(rms_y, 3)
                    act.wait_ge(consts_in, 64)
                    for u in tiles["small", 0]:
                        freed(act, u)
                    e = c_tmp[0:A_HEADS, 0, :]
                    then(A(e, small[0:A_HEADS, :], ACTF.Abs, bias=bf[:]))
                    then(A(e, e, ACTF.Exp, scale=-1.0))
                    A(e, e, ACTF.Ln, bias=1.0).then_inc(fg_l, 1)
                    A(kidx_hl[0:32, :], small[64:96, :], ACTF.Copy)
                    A(kidx_hl[32:64, :], small[64:96, :], ACTF.Copy)
                    A(kidx_hl[64:128, :], small[64:128, :], ACTF.Copy).then_inc(kidx_high, 1)
                elif kind == "b_k":
                    for th in range(2):
                        full(act, a["u"][th])
                        A(q_st[:, 0, th * HALF:(th + 1) * HALF], bank[th][:], ACTF.Copy).then_inc(high_ready, 1)
                elif kind == "b_v":
                    full(act, a["u"][0])
                    A(v_st[:].rearrange("p b d -> p (b d)"), bank[0][:], ACTF.Copy).then_inc(bank_free[0], 1)
                elif kind in ("b_q", "i_q"):
                    s = a["h"] % 2
                    if kind == "b_q":
                        act.wait_ge(kv_spilled, 32) if a["h"] < 2 else act.wait_ge(spilled[s], 16 * (a["h"] // 2))
                        scale = SCALE * 2.0 ** (a["h"] + 1)
                    else:
                        if a["h"] < 2:
                            act.wait_ge(spilled[s], 16 * (B_HEADS // 2))
                        else:
                            act.wait_ge(s_full, 6 * (a["h"] - 1))
                        scale = 1.0
                    for th in range(2):
                        full(act, a["u"][th])
                        A(q_st[:, s, th * HALF:(th + 1) * HALF], bank[th][:], ACTF.Copy,
                          scale=scale).then_inc(high_ready, 1)
                elif kind == "i_dots":
                    act.wait_ge(s_full, a["S"] + 1)
                    if a["n"] >= 2:
                        act.wait_ge(relu_used, a["n"] - 1)
                    W = (a["i"] + 1) * P
                    A(relu_t[:, a["n"] % 2, 0:W], slot[a["S"] % 2][:, 0:W], ACTF.Relu).then_inc(s_free, 1)
                elif kind in ("qc", "qa", "kc", "ka", "vc", "va"):
                    br, what = kind[1], kind[0]
                    dst = {"q": Q, "k": K, "v": VT}[what][br]
                    if a["c"]:
                        if what == "v":
                            full(act, tiles["V" + br, a["c"] - 1, 1])
                        else:
                            act.wait_ge(s_full, last_S[br, a["c"] - 1] + 1)
                    for th in range(2):
                        full(act, a["u"][th])
                        d, src = dst[:, th * HALF:(th + 1) * HALF], bank[th][:]
                        if br == "c" and a["c"] // 2 == 2:
                            d = dst[:].rearrange("p (c u) -> p u c", c=16)[:, 32 * th:32 * th + 32, :]
                            src = src.rearrange("p (u c) -> p u c", c=16)
                        A(d, src, ACTF.Copy, scale=SCALE if what == "q" else 1.0).then_inc(bank_free[th], 1)
                elif kind == "v_turn":
                    br = a["br"]
                    if a["ch"] and a["half"] == 0:
                        full(act, last_pv[br, a["ch"] - 1])
                    full(act, a["use"])
                    A(V[br][:, 4 * a["half"]:4 * a["half"] + 4, :].rearrange("p b c -> p (b c)"), bank[a["use"][0]][:],
                      ACTF.Copy).then_inc(bank_free[a["use"][0]], 1)
                elif kind == "c_bcast":
                    if a["h"] >= 2:
                        act.wait_ge(logit_ready, last_unit["a", a["h"] - 2] + 1)
                    for th, u in enumerate(a["u"]):
                        full(act, u)
                        A(negc[:, a["h"] % 2, th * HALF:(th + 1) * HALF], bank[u[0]][:], ACTF.Copy,
                          scale=-1.0).then_inc(bank_free[u[0]], 1)
                elif kind == "logits":
                    if a["br"] == "c" and a["b"] == 0:
                        h, g = 2 * a["ch"] + a["hh"], a["ch"] // 2
                        if h >= 2:
                            act.wait_ge(logit_ready, last_unit["c", h - 2] + 1)
                        m = band[:] if g < 2 else pairs[:]
                        if h == 0:
                            act.wait_ge(pool_consts, 14)
                        A(bmc[:, a["hh"], 0:m.shape[1]], m, ACTF.Copy,
                          scale=float(np.float32(c_slope(h)) * np.float32(C_GROUPS[g][1]))).then_inc(bm_ready, 1)
                elif kind == "turn":
                    act.wait_ge(logit_ready, a["unit"] + 1)
                    if a["unit"] >= 2:
                        full(act, units[a["unit"] - 2]["groups"][-1]["use"])
                    mx, dn = stats_of(a)
                    A(PR[a["br"]][:, a["unit"] % 2, 0:a["W"]], slot[a["S"] % 2][:, 0:a["W"]], ACTF.Exp, bias=mx,
                      scale=-1.0, accum_out=dn).then_inc(s_free, 1)
                    for grp in a["groups"]:
                        if grp["tp"] % 2:
                            full(act, grp["use"])
                            turned_room(act, grp)
                            b = grp["use"][0]
                            A(PT[a["br"]][:, grp["tp"] % PTS, 0:grp["nc"], :].rearrange("p c q -> p (c q)"),
                              bank[b][:, 0:grp["nc"] * P], ACTF.Copy).then_inc(bank_free[b], 1)
                elif kind == "pv" and a["br"] == "c":
                    full(act, a["pv"])
                    stage_room(act, a)
                    b = a["pv"][0]
                    A(stage[:, a["stage"] % 2, a["b"] % 4, :], bank[b][:, 0:HD], ACTF.Copy).then_inc(bank_free[b], 1)
                elif kind == "y_turn":
                    x = a["x"]
                    br, ch, b0 = x["br"], x["ch"], x["b"] - 3
                    full(act, a["use"])
                    y = Y[br][HD * x["hh"]:HD * x["hh"] + HD, ch, :]
                    src = bank[a["use"][0]][0:HD, :]
                    g = ch // 2 if br == "c" else 0
                    if g == 0:
                        y = y[:, b0 * P:(b0 + 4) * P]
                    elif g == 1:
                        y = y.rearrange("q (x r) -> q r x", r=4)[:, b0 // 2:b0 // 2 + 2, :]
                        src = src.rearrange("q (r x) -> q r x", r=2)
                    else:
                        y = y.rearrange("q (u c) -> q c u", c=16)[:, 2 * b0:2 * b0 + 8, :]
                        src = src.rearrange("q (c u) -> q c u", c=8)
                    A(y, src, ACTF.Copy).then_inc(bank_free[a["use"][0]], 1)
                elif kind == "stat_turn":
                    full(act, a["use"])
                    g, half = a["g"], a["half"]
                    y, src = statT[:, g, :], bank[a["use"][0]][0:8, :]
                    if g == 0:
                        y = y[:, half * HALF:(half + 1) * HALF]
                    elif g == 1:
                        y = y.rearrange("q (x r) -> q r x", r=4)[:, 2 * half:2 * half + 2, :]
                        src = src.rearrange("q (r x) -> q r x", r=2)
                    else:
                        y = y.rearrange("q (u c) -> q c u", c=16)[:, 8 * half:8 * half + 8, :]
                        src = src.rearrange("q (c u) -> q c u", c=8)
                    A(y, src, ACTF.Copy).then_inc(bank_free[a["use"][0]], 1)
                elif kind == "stat_back":
                    full(act, a["use"])
                    A(natS[:].rearrange("p i g a h -> p (i g a h)"), bank[a["use"][0]][:, 0:TB * 24],
                      ACTF.Copy).then_inc(bank_free[a["use"][0]], 1)
                    act.wait_ge(st_d, 1)
                    A(eS[:], eS[:], ACTF.Exp).then_inc(st_e, 1)
                elif kind == "share_turn":
                    full(act, a["use"])
                    A(shareT[:, a["half"] * HALF:(a["half"] + 1) * HALF], bank[a["use"][0]][0:C_HEADS, :],
                      ACTF.Copy).then_inc(bank_free[a["use"][0]], 1)
                elif kind == "z":
                    br, c = a["br"], a["c"]
                    for th in range(2):
                        full(act, a["u"][th])
                        if c:
                            act.wait_ge(low_ready, a["hs"] + th - 1)
                        A(tm[:, 2 * th, :], bank[th][:], ACTF.Silu).then_inc(bank_free[th], 1)
                    for th in range(2):
                        act.wait_ge(z_mul, a["hs"] - z_base[br] + z_count[br] + th + 1)
                        A(YH[br][:, c, th * HALF:(th + 1) * HALF], tm[:, 2 * th + 1, :], ACTF.Copy).then_inc(high_ready, 1)
                elif kind == "g":
                    br, c = a["br"], a["c"]
                    for th in range(2):
                        full(act, a["u"][th])
                        if c < 2:
                            act.wait_ge(low_ready, last_low["w" + br])
                        elif br == "c":
                            freed(act, tiles["w" + br, c - 2][th])
                        else:
                            act.wait_ge(mixed, mix_base[br] + 2 * (c - 2) + th + 1)
                        A(tm[:, 2 * (c % 2) + th, :], bank[th][:], ACTF.Sigmoid).then_inc(bank_free[th], 1)
                elif kind == "final":
                    for cc in range(KC):
                        A(hs[:, 0, cc, :], mT[:, cc, :], ACTF.Copy).then_inc(m_high, 1)
                        split_high(a["first"] + cc + 1)
                    act.wait_ge(m_low, KC)
                    split_high(a["first"] + 2 * KC)
                    for b in range(TB):
                        act.wait_ge(res_ready, b + 1)
                        A(junk_o, xo[b], ACTF.Square, accum_out=ssq[:, b:b + 1]).then_inc(o_ssq, 1)
                        act.wait_ge(o_var, b + 1)
                        A(rstd[:, 1, b:b + 1], rstd[:, 0, b:b + 1], ACTF.Sqrt).then_inc(o_sd, 1)

        @block.vector
        def _(dve):
            v = nc.vector
            chain = [0]
            done = [0]

            def then(ins):
                chain[0] += 1
                ins.then_inc(dve_chain, 1)
                dve.wait_ge(dve_chain, chain[0])

            def split_low(upto):
                while done[0] < min(upto, len(blocks)):
                    n = done[0]
                    b = blocks[n]
                    done[0] += 1
                    dve.wait_ge(w_high, n + 1)
                    if b["kind"] == "wo":
                        hi, lo = wo_hl[b["half"]][:, 0, b["c"], :], wo_hl[b["half"]][:, 1, b["c"], :]
                        src = w_raw[:, n % RAW].rearrange("p k c -> p (k c)")
                    else:
                        hi, lo = w_hl[:, n % SPL, 0, 0:b["nk"], :], w_hl[:, n % SPL, 1, 0:b["nk"], :]
                        src = w_raw[:, n % RAW, 0:b["nk"], :]
                    v.tensor_tensor(lo, src, hi.bitcast(F32), ALU.subtract).then_inc(w_low, 1)

            rounds = [(i, r) for i in range(2, TB) for r in range(ROUNDS)]
            credit, at_round = [0.0], [0]

            def select(us):
                credit[0] += us
                while at_round[0] < len(rounds):
                    i, r = rounds[at_round[0]]
                    cost = 2 * P * (i + 1) / 960 + 0.2
                    if credit[0] < cost:
                        return
                    credit[0] -= cost
                    at_round[0] += 1
                    if r == 0:
                        dve.wait_ge(pool_causal, i - 1)
                    then(v.max(top8[:], score_of(i)))
                    then(v.match_replace(score_of(i), top8[:], score_of(i), TAKEN))
                    if r == ROUNDS - 1:
                        then(v.tensor_scalar(score_of(i), score_of(i), 0.66 * TAKEN, NEG, ALU.is_ge, ALU.mult))

            def low_of(dst, src, hi):
                v.tensor_tensor(dst, src, hi.bitcast(F32), ALU.subtract).then_inc(low_ready, 1)

            selecting = False
            k = 0
            for kind, a in plan:
                if kind == "phase":
                    k += 1
                    if a["name"] == "b":
                        select(1e9)
                    if k > 1:
                        phase_end(dve, "dve", k - 1)
                    if a["name"] == "x":
                        v.memset(ones[:], 1.0).then_inc(ones_ready, 1)
                        dve.wait_ge(act_chain, TB)
                        v.tensor_scalar(rstd[:, 0], ssq[:], 1.0 / D, EPS, ALU.mult, ALU.add).then_inc(var_ready, 1)
                        dve.wait_ge(sd_ready, 1)
                        then(v.reciprocal(rstd[:, 2], rstd[:, 1]))
                        for i in range(TB):
                            v.tensor_scalar(xn[:, i, :], xn[:, i, :], rstd[:, 2, i:i + 1], None,
                                            ALU.mult).then_inc(xs_ready, 1)
                        dve.wait_ge(consts_in, 64)
                    if a["name"] == "small":
                        dve.wait_ge(pw_high, 1)
                        for r in range(2):
                            ins = v.tensor_tensor(uq_hl[:, 1, :, :, r, :], uq_raw[:], uq_hl[:, 0, :, :, r, :].bitcast(F32),
                                                  ALU.subtract)
                        ins.then_inc(pw_low, 1)
                        for r in range(4):
                            ins = v.tensor_tensor(ix_hl[:, 1, :, :, r, :], ix_raw[:], ix_hl[:, 0, :, :, r, :].bitcast(F32),
                                                  ALU.subtract)
                        ins.then_inc(pw_low, 1)
                        for r, s in ((0, 0), (1, 0), (2, 1)):
                            ins = v.tensor_tensor(ukv_hl[:, 1, r, :], ukv_raw[:, s, :], ukv_hl[:, 0, r, :].bitcast(F32),
                                                  ALU.subtract)
                        ins.then_inc(pw_low, 1)
                    if a["name"] == "c":
                        selecting = True
                    if a["name"] == "a":
                        dve.wait_ge(pool_consts, 2)
                        v.tensor_copy(selA[:], ident[0:A_HEADS, 0:A_HEADS].unsqueeze(2).to_broadcast([A_HEADS, A_HEADS, P])
                                      ).then_inc(sel_ready, 1)
                    if a["name"] == "b":
                        dve.wait_ge(pool_srow, 1)
                        for i in range(2, TB):
                            ins = v.scalar_tensor_tensor(score_of(i), score_of(i), float(-P * i), srow[:, 0:P * (i + 1)],
                                                         ALU.add, ALU.add)
                            then(ins)
                        dve.wait_ge(pool_consts, 18)
                elif kind == "x_turn":
                    dve.wait_ge(high_ready, a["hs"] + 1)
                    ts = slice(a["th"] * HALF, (a["th"] + 1) * HALF)
                    b = a["use"][0]
                    v.scalar_tensor_tensor(hs[:, 1, a["kc"], ts], bank[b][:], gn[:, a["kc"]:a["kc"] + 1],
                                           hs[:, 0, a["kc"], ts].bitcast(F32), ALU.mult,
                                           ALU.subtract).then_inc(low_ready, 1)
                    dve.wait_ge(low_ready, a["hs"] + 1)
                    dve.sem_inc(bank_free[b], 1)
                elif kind == "block":
                    split_low(min(a["n"] + SPL, info["first_wo"]))
                    if selecting:
                        select(2.6)
                elif kind == "rms":
                    width = P * a["n"]
                    for th in range(2):
                        full(dve, a["u"][th])
                        v.tensor_scalar(c_tmp[:, 0, th * HALF:(th + 1) * HALF], bank[th][:], 1.0 / width, EPS, ALU.mult,
                                        ALU.add).then_inc(rms_var, 1)
                    n0 = 2 * (a["name"] == "ckv")
                    dve.wait_ge(rms_sd, n0 + 2)
                    then(v.reciprocal(c_tmp[:, 0, :], c_tmp[:, 0, :]))
                    for th in range(2):
                        dve.wait_ge(rms_var, n0 + th + 1)
                        dve.sem_inc(bank_free[th], 1)
                    for c in range(a["n"]):
                        ch = a["first_chunk"] + c
                        v.scalar_tensor_tensor(c_raw[:, ch, :], c_raw[:, ch, :], gq[:, ch:ch + 1], c_tmp[:, 0, :], ALU.mult,
                                               ALU.mult).then_inc(rms_y, 1)
                    dve.wait_ge(rms_y, a["first_chunk"] + a["n"])
                    for c in range(a["n"]):
                        ch = a["first_chunk"] + c
                        hl = ckv_hl if ch == 2 else cq_hl[:, :, ch, :]
                        for th in range(2):
                            ts = slice(th * HALF, (th + 1) * HALF)
                            dve.wait_ge(high_ready, a["hs"] + 2 * c + th + 1)
                            low_of(hl[:, 1, ts], c_raw[:, ch, ts], hl[:, 0, ts])
                elif kind == "forget":
                    mn = c_tmp[0:A_HEADS, 1, :]
                    then(v.tensor_scalar(mn, small[0:A_HEADS, :], bf[:], 0.0, ALU.add, ALU.min))
                    dve.wait_ge(fg_l, 1)
                    v.tensor_tensor_scan(cumT[:], mn, c_tmp[0:A_HEADS, 0, :], 0.0, ALU.add,
                                         ALU.subtract).then_inc(cum_ready, 1)
                    dve.wait_ge(kidx_high, 1)
                    v.tensor_tensor(kidx_hl[64:128, :], small[64:128, :], kidx_hl[64:128, :].bitcast(F32),
                                    ALU.subtract).then_inc(kidx_low, 1)
                elif kind == "natural":
                    for half, u in enumerate(a["u"]):
                        full(dve, u)
                        v.tensor_copy(wnat[:, 4 * half:4 * half + 4, :],
                                      bank[u[0]][:].rearrange("p (j c) -> p j c", j=4)[:, :, 32:32 + IDX_HEADS]
                                      ).then_inc(bank_free[u[0]], 1)
                elif kind == "b_k":
                    for th in range(2):
                        ts = slice(th * HALF, (th + 1) * HALF)
                        dve.wait_ge(high_ready, a["hs"] + th + 1)
                        low_of(q_st[:, 1, ts], bank[th][:], q_st[:, 0, ts])
                    dve.wait_ge(low_ready, a["hs"] + 2)
                    for th in range(2):
                        dve.sem_inc(bank_free[th], 1)
                elif kind == "b_v":
                    freed(dve, a["u"][0])
                    dve.sem_inc(v_ready, 1)
                elif kind in ("b_q", "i_q"):
                    s = a["h"] % 2
                    spans = ((64, 128),) if kind == "b_q" else ((32, 64), (96, 128))
                    scale = SCALE * 2.0 ** (a["h"] + 1) if kind == "b_q" else 1.0
                    for th in range(2):
                        ts = slice(th * HALF, (th + 1) * HALF)
                        dve.wait_ge(high_ready, a["hs"] + th + 1)
                        for p0, p1 in spans:
                            ins = v.scalar_tensor_tensor(q_st[p0:p1, s, ts], bank[th][p0:p1, :], scale,
                                                         q_st[p0:p1, s, ts].bitcast(F32), ALU.mult, ALU.subtract)
                        ins.then_inc(low_ready, 1)
                    dve.wait_ge(low_ready, a["hs"] + 2)
                    for th in range(2):
                        dve.sem_inc(bank_free[th], 1)
                elif kind == "i_dots":
                    W, i = (a["i"] + 1) * P, a["i"]
                    dve.wait_ge(s_free, a["S"] + 1)
                    w = wnat[:, i, a["h"]:a["h"] + 1]
                    if a["h"] == 0:
                        v.tensor_scalar(score_of(i), relu_t[:, a["n"] % 2, 0:W], w, None, ALU.mult).then_inc(relu_used, 1)
                    else:
                        dve.wait_ge(relu_used, a["n"] - 5)
                        v.scalar_tensor_tensor(score_of(i), relu_t[:, a["n"] % 2, 0:W], w, score_of(i), ALU.mult,
                                               ALU.add).then_inc(relu_used, 1)
                    if a["h"] == IDX_HEADS - 1:
                        dve.wait_ge(relu_used, a["n"] + 1)
                        dve.sem_inc(score_done, 1)
                elif kind == "logits":
                    dve.wait_ge(s_full, a["S"] + 1)
                    if a["br"] == "a" and a["b"] == 0:
                        for u in tiles["negc", 2 * a["ch"] + a["hh"]]:
                            freed(dve, u)
                    if a["br"] == "c":
                        dve.wait_ge(bm_ready, 2 * a["ch"] + a["hh"] + 1)
                    o = slot[a["S"] % 2][:, 0:a["W"]]
                    slope = 2.0 ** (-(a["h"] + 1)) if a["br"] == "b" else 1.0
                    v.tensor_tensor_reduce(o, o, logit_bias(a), -slope, 0.0, ALU.add, ALU.min,
                                           stats_of(a)[0]).then_inc(logit_ready, 1)
                elif kind == "turn":
                    for grp in a["groups"]:
                        if grp["tp"] % 2 == 0:
                            full(dve, grp["use"])
                            turned_room(dve, grp)
                            b = grp["use"][0]
                            v.tensor_copy(PT[a["br"]][:, grp["tp"] % PTS, 0:grp["nc"], :].rearrange("p c q -> p (c q)"),
                                          bank[b][:, 0:grp["nc"] * P]).then_inc(bank_free[b], 1)
                elif kind == "pv" and a["br"] != "c":
                    r = a["unit"] % 8
                    then(v.reciprocal(rden[:, r:r + 1], den[:, r:r + 1]))
                    full(dve, a["pv"])
                    stage_room(dve, a)
                    b = a["pv"][0]
                    v.tensor_scalar(stage[:, a["stage"] % 2, a["b"] % 4, :], bank[b][:, 0:HD], rden[:, r:r + 1], None,
                                    ALU.mult).then_inc(bank_free[b], 1)
                elif kind == "stat_back":
                    freed(dve, a["use"])
                    nm = [natS[:, :, g, 0, :] for g in range(3)]
                    dn = [natS[:, :, g, 1, :] for g in range(3)]
                    then(v.tensor_tensor(mxS[:], nm[0], nm[1], ALU.min))
                    then(v.tensor_tensor(mxS[:], mxS[:], nm[2], ALU.min))
                    for g in range(3):
                        ins = v.tensor_tensor(eS[:, g], mxS[:], nm[g], ALU.subtract)
                    ins.then_inc(st_d, 1)
                    dve.wait_ge(st_e, 1)
                    for g in range(3):
                        then(v.tensor_tensor(wS[:, g], eS[:, g], dn[g], ALU.mult))
                    then(v.tensor_tensor(wS[:, 0], wS[:, 0], wS[:, 1], ALU.add))
                    then(v.tensor_tensor(wS[:, 0], wS[:, 0], wS[:, 2], ALU.add))
                    then(v.reciprocal(wS[:, 1], wS[:, 0]))
                    for g in range(3):
                        then(v.tensor_tensor(shareN[:, :, g, :], eS[:, g], wS[:, 1], ALU.mult))
                    v.tensor_copy(selC[:], ident[0:C_HEADS, 0:C_HEADS].unsqueeze(2).to_broadcast([C_HEADS, C_HEADS, HD])
                                  ).then_inc(sel_ready, 1)
                    dve.wait_ge(sel_ready, 1)
                    dve.sem_inc(share_ready, 1)
                elif kind == "z":
                    br, c = a["br"], a["c"]
                    for th in range(2):
                        ts = slice(th * HALF, (th + 1) * HALF)
                        freed(dve, a["u"][th])
                        if br == "c":
                            sh = a["share"][th]
                            full(dve, sh)
                            then(v.tensor_tensor(tm[:, 2 * th, :], tm[:, 2 * th, :], bank[sh[0]][:], ALU.mult))
                            dve.sem_inc(bank_free[sh[0]], 1)
                        v.tensor_tensor(tm[:, 2 * th + 1, :], tm[:, 2 * th, :], Y[br][:, c, ts], ALU.mult).then_inc(z_mul, 1)
                    dve.wait_ge(z_mul, z_count[br] + a["hs"] - z_base[br] + 2)
                    for th in range(2):
                        ts = slice(th * HALF, (th + 1) * HALF)
                        dve.wait_ge(high_ready, a["hs"] + th + 1)
                        low_of(YL[br][:, c, ts], tm[:, 2 * th + 1, :], YH[br][:, c, ts])
                elif kind == "w":
                    br, c = a["br"], a["c"]
                    for th in range(2):
                        ts = slice(th * HALF, (th + 1) * HALF)
                        full(dve, a["u"][th])
                        freed(dve, a["gate"][th])
                        gate = tm[:, 2 * (c % 2) + th, :]
                        if br == "c":
                            v.tensor_tensor(mT[:, c, ts], bank[th][:], gate, ALU.mult).then_inc(bank_free[th], 1)
                        else:
                            v.tensor_tensor(gate, bank[th][:], gate, ALU.mult).then_inc(bank_free[th], 1)
                            freed(dve, a["u"][th])
                            v.tensor_tensor(mT[:, c, ts], mT[:, c, ts], gate, ALU.add).then_inc(mixed, 1)
                elif kind == "final":
                    for cc in range(KC):
                        dve.wait_ge(m_high, cc + 1)
                        v.tensor_tensor(hs[:, 1, cc, :], mT[:, cc, :], hs[:, 0, cc, :].bitcast(F32),
                                        ALU.subtract).then_inc(m_low, 1)
                        split_low(a["first"] + cc + 1)
                    split_low(a["first"] + 2 * KC)
                    dve.wait_ge(xo_in, 16 * TB)
                    for b in range(TB):
                        dve.wait_ge(o_full, b + 1)
                        v.tensor_tensor(xo[b][:, 0:HALF], banks8[b], xo[b][:, 0:HALF], ALU.add).then_inc(o_free, 1)
                    for b in range(TB):
                        dve.wait_ge(o_full, TB + b + 1)
                        v.tensor_tensor(xo[b][:, HALF:D], banks8[b], xo[b][:, HALF:D], ALU.add).then_inc(res_ready, 1)
                        dve.wait_ge(o_ssq, b + 1)
                        v.tensor_scalar(rstd[:, 0, b:b + 1], ssq[:, b:b + 1], 1.0 / D, EPS, ALU.mult,
                                        ALU.add).then_inc(o_var, 1)
                        dve.wait_ge(o_sd, b + 1)
                        then(v.reciprocal(rstd[:, 2, b:b + 1], rstd[:, 1, b:b + 1]))
                        if b == 0:
                            dve.wait_ge(fg_in, 16)
                        v.scalar_tensor_tensor(xo[b], xo[b], rstd[:, 2, b:b + 1], fg, ALU.mult, ALU.mult).then_inc(out_ready, 1)


_INS = ["x", "norm_g", "w_in", "b_forget", "g_cq", "w_uq", "w_uq_idx", "g_ckv", "w_ukv", "w_a", "w_b", "w_c", "w_o",
        "final_g"]
_OUTS = [((1, T, D), "float32")]


def kernel(**inputs):
    import numpy as _np
    import concourse.bacc as _bacc
    from concourse import mybir as _mybir
    from concourse.bass_utils import run_bass_kernel_spmd as _run

    nc = _bacc.Bacc("TRN2", target_bir_lowering=False, num_devices=1)
    arrays, args = {}, []
    for name in _INS:
        a = _np.ascontiguousarray(inputs[name])
        arrays[f"in_{name}_dram"] = a
        args.append(nc.dram_tensor(f"in_{name}_dram", a.shape, _mybir.dt.from_np(a.dtype), kind="ExternalInput").ap())
    for i, (shape, dtype) in enumerate(_OUTS):
        dt = _mybir.dt.from_np(_np.dtype(dtype))
        args.append(nc.dram_tensor(f"out_{i}_dram", shape, dt, kind="ExternalOutput").ap())
    hybrid_layer_kernel(nc, *args)
    r = _run(nc, [arrays], core_ids=[0])
    return r.results[0]["out_0_dram"]
```

```python
from contextlib import ExitStack

import numpy as np

import concourse.bass as bass
from concourse import mybir

P = 128
D = 1024
T = 1024
KC = D // P
TB = T // P
HALF = 512
HD = 64
A_HEADS, B_HEADS, C_HEADS, IDX_HEADS = 8, 8, 12, 8
IDX_DIM = 32
TOPK = 256
ROUNDS = TOPK // 8
EPS = 1e-6
SCALE = HD ** -0.5
C_GROUPS = ((128, 1), (512, 4), (2048, 16))
NEG = -1e30
CAUSAL = -1e38
TAKEN = -3e38
SELECT_US = {"c": (0.8, 0.8), "c_merge": (0.6, 0.0), "a": (0.0, 2.4)}

WIDTHS = (("qa", 512), ("ka", 512), ("va", 512), ("fa", 8), ("za", 512), ("cq", 256), ("ckv", 128), ("kidx", 32),
          ("widx", 8), ("zb", 512), ("qc", 768), ("kc", 768), ("vc", 768), ("zc", 768), ("ga", D), ("gb", D), ("gc", D))
COL, at = {}, 0
for _n, _w in WIDTHS:
    COL[_n] = at
    at += _w
D_IN = at

F32, F32R, BF16 = mybir.dt.float32, mybir.dt.float32r, mybir.dt.bfloat16
ALU = mybir.AluOpType
ACTF = mybir.ActivationFunctionType
AX = mybir.AxisListType

RAW = 3
SPL = 3
PTS = 4
NCH = {"a": 4, "b": 4, "c": 6}


def c_slope(h):
    return float(np.float32(2.0 ** (-8.0 * (h + 1) / C_HEADS)))


def build_plan():
    plan, uses, blocks = [], [0] * 4, []
    count = {"ring": 0, "tp": 0, "hs": 0, "S": 0, "unit": 0, "stage": 0, "z": 0}
    tiles, unit_of_tp, units_seen, y_turn_of = {}, [], [], []

    def use(b):
        uses[b] += 1
        return b, uses[b] - 1

    def ring():
        count["ring"] += 1
        return use(2 + count["ring"] % 2)

    def nxt(name, n=1):
        count[name] += n
        return count[name] - n

    def step(kind, **kw):
        plan.append((kind, kw))
        return kw

    later, defer = [], [False]

    def flush_later():
        while later:
            later.pop(0)()

    def tile_pieces(kind, c, src, chunks=KC, **kw):
        u = [use(0), use(1)]
        tiles[kind, c] = u

        def read(th):
            name = kind[0] if kind[0] in "zgw" and len(kind) == 2 else kind
            if name == "z":
                step("z", c=c, u=u, th=th, zn=nxt("z"), **kw)
                if th:
                    for t in range(2):
                        step("z_split", c=c, th=t, zn=count["z"] - 2 + t, hs=nxt("hs"), br=kw["br"])
            else:
                step(name, c=c, u=u, th=th, **kw)

        for base in range(0, chunks, 4):
            nk = min(4, chunks - base)
            last = base + nk == chunks
            blocks.append(dict(kind=kind, nk=nk, c=c, base=base, last=last, done=u[1]))
            n = len(blocks) - 1
            for th in range(2):
                step("block", n=n, base=base, nk=nk, u=u[th], th=th, first=base == 0, last=last, src=src)
                if last:
                    later.append(lambda th=th: read(th))
                    if not defer[0]:
                        flush_later()
                yield

    def tile(*args, **kw):
        for _ in tile_pieces(*args, **kw):
            pass

    fill, owed = [], [0.0]

    def pump(pieces):
        owed[0] += pieces
        while owed[0] >= 1 and fill:
            owed[0] -= 1
            flush_later()
            try:
                next(fill[0])
            except StopIteration:
                fill.pop(0)
                owed[0] += 1
        if not fill:
            owed[0] = 0.0

    def flush():
        while fill:
            pump(1)
        flush_later()

    def softmax_run(units, before, rate):
        n = len(units)
        defer[0] = True
        for s in range(n + 4):
            for f in before.get(s, []):
                f()
            if s < n:
                units[s].update(S=nxt("S"), unit=nxt("unit"))
                units_seen.append(units[s])
                plan.append(("logits", units[s]))
            if 1 <= s <= n:
                plan.append(("exp", units[s - 1]))
            pump(rate)
            if 3 <= s <= n + 2:
                x = units[s - 3]
                if x["b"] % 4 == 0:
                    count["stage"] += 1
                x["pv"], x["stage"] = ring(), count["stage"] - 1
                plan.append(("pv", x))
            if 2 <= s <= n + 1:
                x = units[s - 2]
                chunks = x["W"] // P
                x["groups"] = []
                for c0 in range(0, chunks, 4):
                    x["groups"].append(dict(use=ring(), tp=nxt("tp"), c0=c0, nc=min(4, chunks - c0)))
                    unit_of_tp.append(x)
                plan.append(("turn", x))
            if s >= 4 and units[s - 4]["b"] % 4 == 3:
                y_turn_of.append(ring())
                step("y_turn", use=y_turn_of[-1], x=units[s - 4])
            flush_later()
        defer[0] = False

    def attend(br, after):
        units, before = [], {}
        for ch in range(NCH[br]):
            def v_turns(ch=ch):
                flush()
                for half in range(2):
                    tiles["V" + br, ch, half] = ring()
                    step("v_turn", br=br, ch=ch, half=half, use=tiles["V" + br, ch, half])
                fill.extend(qkv(br, ch + 1) if ch + 1 < NCH[br] else after())
            at = len(units)
            before.setdefault(at, []).append(v_turns)
            for hh in range(2):
                if br == "a":
                    def bcast(h=2 * ch + hh):
                        tiles["negc", h] = [ring(), ring()]
                        step("c_bcast", h=h, u=tiles["negc", h])
                    before.setdefault(max(0, len(units) - 1), []).append(bcast)
                for b in range(TB):
                    W = {0: P * min(b + 1, 2), 1: P * (b % 2 + 1), 2: P}[ch // 2] if br == "c" else P * (b + 1)
                    units.append(dict(br=br, ch=ch, hh=hh, b=b, W=W))
        softmax_run(units, before, 0.8)
        flush()

    def qkv(br, ch):
        return [tile_pieces(w + br, ch, "h") for w in "qkv"]

    def merge(br):
        n = NCH[br]
        for c in range(n):
            share = []
            pieces = tile_pieces("z" + br, c, "h", br=br, share=share)
            for k, _ in enumerate(pieces):
                yield
                if k == 1 and br == "c":
                    share.extend([ring(), ring()])
                    step("share", c=c, u=share)
        yield from tile_pieces("g" + br, 0, "h", br=br)
        for c in range(KC):
            if c + 1 < KC:
                yield from tile_pieces("g" + br, c + 1, "h", br=br)
            yield from tile_pieces("w" + br, c, "y", chunks=n, br=br, gate=tiles["g" + br, c])
            if br == "b" and c == KC - 2:
                step("m_split", chunks=range(KC - 2))

    step("phase", name="x")
    for th in range(2):
        for kc in range(KC):
            step("x_turn", kc=kc, th=th, use=use(kc % 4), hs=nxt("hs"))
    step("phase", name="small")
    tile("cq", 0, "h")
    tile("cq", 1, "h")
    fill.extend([tile_pieces("ckv", 2, "h"), tile_pieces("small", 0, "h")] + qkv("c", 0))
    for name, first, n in (("cq", 0, 2), ("ckv", 2, 1)):
        step("rms_sum", name=name, first_chunk=first, n=n, u=[ring(), ring()])
        pump(4)
        step("rms_norm", name=name, first_chunk=first, n=n, hs=nxt("hs", 2 * n))
    step("forget")
    step("natural", u=[ring(), ring()])
    pump(4)
    step("phase", name="index")
    step("b_k", u=[ring(), ring()], hs=nxt("hs", 2))
    step("b_v", u=[ring()])
    low = {}
    for h in range(IDX_HEADS + 1):
        def project(kind, th):
            if h < IDX_HEADS:
                step(kind, h=h, th=th, u=ring(), hs=nxt("hs"))
                if kind == "i_q":
                    low[h] = count["hs"]
        beside = [lambda: project("i_q", 0), lambda: project("i_q", 1), lambda: pump(1), lambda: project("b_q", 0),
                  lambda: project("b_q", 1), lambda: None]
        for i, other in zip(range(2, TB), beside):
            if h:
                step("i_dots", h=h - 1, i=i, S=nxt("S"), n=(h - 1) * 6 + i - 2, low=low[h - 1])
            other()
    step("phase", name="c")
    attend("c", lambda: qkv("a", 0))
    step("phase", name="c_stats")
    for g in range(3):
        for half in range(2):
            step("stat_turn", g=g, half=half, use=ring())
    fill.append(merge("c"))
    pump(1)
    step("stat_back", use=ring())
    pump(1)
    for half in range(2):
        step("share_turn", half=half, use=ring())
    step("phase", name="c_merge")
    flush()
    step("phase", name="a")
    attend("a", lambda: [])
    step("phase", name="b")
    fill.append(merge("a"))
    pump(3)
    softmax_run([dict(br="b", ch=h // 2, hh=h % 2, b=b, W=(b + 1) * P, h=h)
                 for h in range(B_HEADS) for b in range(TB)], {}, 1.0)
    flush()
    step("phase", name="b_merge")
    for _ in merge("b"):
        pass
    step("phase", name="o")
    first_wo = len(blocks)
    for half in range(2):
        for cc in range(KC):
            blocks.append(dict(kind="wo", nk=4, c=cc, half=half))
    step("final", first=first_wo, uses=list(uses), S=count["S"])
    return plan, blocks, dict(unit_of_tp=unit_of_tp, units=units_seen, y_turns=y_turn_of, tiles=tiles, first_wo=first_wo)


def hybrid_layer_kernel(nc, x, norm_g, w_in, b_forget, g_cq, w_uq, w_uq_idx, g_ckv, w_ukv, w_a, w_b, w_c, w_o, final_g,
                        out):
    plan, blocks, info = build_plan()
    tiles, units = info["tiles"], info["units"]
    with ExitStack() as ctx:
        def sb(name, shape, dt=F32, es=ctx):
            return es.enter_context(nc.sbuf_tensor(name, shape, dt))

        def psum(name, cols):
            return ctx.enter_context(nc.psum_tensor(name, [P, cols], F32))

        def sem(name):
            return ctx.enter_context(nc.semaphore(name))

        hs = sb("hs", [P, 2, KC, T], F32R)
        w_raw = sb("w_raw", [P, RAW, 4, P])
        w_hl = sb("w_hl", [P, SPL, 2, 4, P], F32R)
        score = sb("score", [P, P * TB * (TB + 1) // 2])
        cumT = sb("cumT", [A_HEADS, T])
        ident = sb("ident", [P, P])
        ident_b = sb("ident_b", [P, P], BF16)
        tri_b = sb("tri_b", [P, P], BF16)
        band = sb("band", [P, 2 * P])
        pairs = sb("pairs", [P, P])
        gn = sb("gn", [P, KC])
        gq = sb("gq", [P, 3])
        bf = sb("bf", [A_HEADS, 1])
        wnat = sb("wnat", [P, TB, IDX_HEADS])
        top8 = sb("top8", [P, 8])
        stat = sb("stat", [P, 3, TB, 2, 4])
        nmax = sb("nmax", [P, 8])
        den = sb("den", [P, 8])
        rden = sb("rden", [P, 8])
        ssq = sb("ssq", [P, TB])
        rstd = sb("rstd", [P, 3, TB])
        stage = sb("stage", [P, 2, 4, HD])

        def at(kib, name, shape, dt=F32):
            with ExitStack() as es:
                if kib:
                    sb(name + "_below", [P, int(kib * 256)], F32, es)
                return sb(name, shape, dt, es)

        xn, junk = at(0, "xn", [P, TB, D]), at(36, "junk", [P, D])
        cq_hl, ckv_hl = at(0, "cq_hl", [P, 2, 2, T], F32R), at(16, "ckv_hl", [P, 2, T], F32R)
        ix_hl = at(52, "ix_hl", [P, 2, 2, IDX_HEADS, 4, IDX_DIM], F32R)
        uq_hl = at(68, "uq_hl", [P, 2, 2, B_HEADS, 2, HD], F32R)
        ukv_hl, kidx_hl = at(84, "ukv_hl", [P, 2, 3, HD], F32R), at(36, "kidx_hl", [P, T], F32R)
        c_raw = [at(k, f"c_raw{n}", [P, T]) for n, k in enumerate((28, 32, 48))]
        c_tmp, small = at(40, "c_tmp", [P, 2, T]), at(86, "small", [P, T])
        uq_raw, ix_raw = at(90, "uq_raw", [P, 2, B_HEADS, HD]), at(94, "ix_raw", [P, 2, IDX_HEADS, IDX_DIM])
        ukv_raw, ones = at(96, "ukv_raw", [P, 2, HD]), at(96.5, "ones", [P, P])
        iq_st, bq_st, relu_t = at(40, "iq_st", [P, 2, T], F32R), at(32, "bq_st", [P, T], F32R), at(86, "relu_t", [P, 2, T])
        v_st = at(94, "v_st", [P, TB, HD])
        Y = {"c": at(0, "yc", [P, 6, T]), "a": at(0, "ya", [P, 4, T]), "b": at(64, "yb", [P, 4, T])}
        Q = {"c": [at(k, f"qc{k}", [P, T]) for k in (24, 36)], "a": [at(k, f"qa{k}", [P, T]) for k in (80, 16)]}
        K = {"c": [at(k, f"kc{k}", [P, T]) for k in (28, 40)], "a": [at(k, f"ka{k}", [P, T]) for k in (84, 20)]}
        V = {"c": [at(k, f"vc{k}", [P, TB, P]) for k in (32, 44)], "a": [at(k, f"va{k}", [P, TB, P]) for k in (88, 24)],
             "b": at(96, "vb", [P, TB, HD])}
        VT = {"c": at(48, "vtc", [P, T]), "a": at(92, "vta", [P, T])}
        PR = {"c": at(52, "pc", [P, 2, 2 * P]), "a": at(28, "pa", [P, 2, T]), "b": at(32, "pb", [P, 2, T])}
        PT = {"c": at(54, "ptc", [P, PTS, 4, P]), "a": at(36, "pta", [P, PTS, 4, P]), "b": at(40, "ptb", [P, PTS, 4, P])}
        bmc = at(62, "bmc", [P, 2, 2 * P])
        negc, selA = at(44, "negc", [P, 2, T]), at(52, "selA", [A_HEADS, A_HEADS, P])
        khb, qb, srow = at(80, "khb", [P, 2, T], F32R), at(88, "qb", [P, 2, T], F32R), at(76, "srow", [P, T])
        statT, natS = at(24, "statT", [8, 3, T]), at(36, "natS", [P, TB, 3, 2, 4])
        eS, wS, shareN = at(37, "eS", [P, 3, TB, 4]), at(38, "wS", [P, 3, TB, 4]), at(39, "shareN", [P, TB, 3, 4])
        mxS = at(40, "mxS", [P, TB, 4])
        shareT, selC = at(64, "shareT", [C_HEADS, T]), at(68, "selC", [C_HEADS, C_HEADS, HD])
        YH = {"c": at(0, "ych", [P, 6, T], F32R), "a": at(0, "yah", [P, 4, T], F32R), "b": at(64, "ybh", [P, 4, T], F32R)}
        YL = {"c": at(24, "ycl", [P, 6, T], F32R), "a": at(16, "yal", [P, 4, T], F32R), "b": at(0, "ybl", [P, 4, T], F32R)}
        tm = at(48, "tm", [P, 4, HALF])
        ms = at(56, "ms", [P, 2, T])
        mT = at(16, "mT", [P, KC, T])
        wo_hl = [at(64, "wo0", [P, 2, KC, HALF], F32R), at(16, "wo1", [P, 2, KC, HALF], F32R)]
        xo_a, xo_b = at(48, "xo_a", [P, 4, D]), at(0, "xo_b", [P, 4, D])
        xo = [(xo_a if b < 4 else xo_b)[:, b % 4, :] for b in range(TB)]
        fg, junk_o = score[:, 0:D], score[:, D:2 * D]

        bank = [psum(f"bank{i}", HALF) for i in range(4)]
        slot = [psum(f"slot{i}", T) for i in range(2)]
        banks8 = [bank[0][:], bank[1][:], bank[2][:], bank[3][:], slot[0][:, 0:HALF], slot[0][:, HALF:T],
                  slot[1][:, 0:HALF], slot[1][:, HALF:T]]

        qb_dram = nc.dram_tensor("qb_scratch", [B_HEADS, P, T], F32R, kind="Internal").ap()
        kb_dram = nc.dram_tensor("kb_scratch", [P, 2, T], F32R, kind="Internal").ap()
        vb_dram = nc.dram_tensor("vb_scratch", [P, TB, HD], F32, kind="Internal").ap()
        m_dram = nc.dram_tensor("merged_scratch", [KC, P, T], F32, kind="Internal").ap()

        consts_in, fg_in, xo_in = sem("consts_in"), sem("fg_in"), sem("xo_in")
        x_in = [sem(f"x_in{i}") for i in range(2)]
        m_stored, m_loaded = [sem(f"m_stored{i}") for i in range(2)], [sem(f"m_loaded{i}") for i in range(2)]
        pw_in = sem("pw_in")
        raw_in = [sem(f"raw_in{i}") for i in range(RAW)]
        w_high, w_low, w_used = sem("w_high"), sem("w_low"), sem("w_used")
        bank_full = [sem(f"bank_full{i}") for i in range(4)]
        bank_free = [sem(f"bank_free{i}") for i in range(4)]
        s_full, s_free, logit_ready = sem("s_full"), sem("s_free"), sem("logit_ready")
        high_ready, low_ready = sem("high_ready"), sem("low_ready")
        pool_consts, pool_causal, pool_srow = sem("pool_consts"), sem("pool_causal"), sem("pool_srow")
        ones_ready, ssq_ready, var_ready, sd_ready, xs_ready = (sem(n) for n in
            ("ones_ready", "ssq_ready", "var_ready", "sd_ready", "xs_ready"))
        pw_high, pw_low = sem("pw_high"), sem("pw_low")
        rms_sq, rms_var, rms_sd, rms_y = sem("rms_sq"), sem("rms_var"), sem("rms_sd"), sem("rms_y")
        fg_l, cum_ready, kidx_high, kidx_low = sem("fg_l"), sem("cum_ready"), sem("kidx_high"), sem("kidx_low")
        kv_spilled, spilled = sem("kv_spilled"), sem("spilled")
        relu_used, score_done = sem("relu_used"), sem("score_done")
        bm_ready, sel_ready = sem("bm_ready"), sem("sel_ready")
        st_d, st_e, share_ready = sem("st_d"), sem("st_e"), sem("share_ready")
        z_tanh, z_mul, mixed = sem("z_tanh"), sem("z_mul"), sem("mixed")
        kv_in, qb_in = sem("kv_in"), [sem(f"qb_in{i}") for i in range(2)]
        bias_b = sem("bias_b")
        m_high, m_low, o_full, o_free, res_ready = (sem(n) for n in ("m_high", "m_low", "o_full", "o_free", "res_ready"))
        o_ssq, o_var, o_sd, out_ready, stored = (sem(n) for n in ("o_ssq", "o_var", "o_sd", "out_ready", "stored"))
        act_chain, dve_chain = sem("act_chain"), sem("dve_chain")
        ended = {e: sem(f"ended_{e}") for e in ("pe", "act", "dve", "pool")}

        def full(eng, u):
            eng.wait_ge(bank_full[u[0]], u[1] + 1)

        def freed(eng, u):
            eng.wait_ge(bank_free[u[0]], u[1] + 1)

        def claim(pe, u):
            if u[1]:
                pe.wait_ge(bank_free[u[0]], u[1])

        def phase_end(eng, name, k):
            eng.drain().then_inc(ended[name], 1)
            if name != "pe":
                for other in ended:
                    if other != name:
                        eng.wait_ge(ended[other], k)

        def block_done(eng, n):
            if blocks[n]["last"]:
                full(eng, blocks[n]["done"])
            else:
                eng.wait_ge(w_used, sum(not b["last"] for b in blocks[:n + 1]))

        loads, arrived = [], [0] * RAW
        for n, b in enumerate(blocks):
            rows = slice(b.get("base", 0) * P, (b.get("base", 0) + b["nk"]) * P)
            kind, c = b["kind"], b["c"]

            def cols(w, col, width=P):
                return w[rows, col:col + width].rearrange("(k p) c -> p k c", p=P)
            if kind == "wo":
                src = [(None, w_o[0][c * P:(c + 1) * P, b["half"] * HALF:(b["half"] + 1) * HALF])]
            elif kind == "small":
                src = [(0, cols(w_in[0], COL["fa"], 32)), (32, cols(w_in[0], COL["widx"], 32)),
                       (64, cols(w_in[0], COL["kidx"], 32)), (96, cols(w_in[0], COL["kidx"], 32))]
            elif kind in ("wa", "wb", "wc"):
                src = [(0, cols({"wa": w_a, "wb": w_b, "wc": w_c}[kind][0], c * P))]
            else:
                src = [(0, cols(w_in[0], COL[kind] + (c if kind != "ckv" else 0) * P))]
            arrived[n % RAW] += 16 * len(src)
            loads.append((src, arrived[n % RAW]))

        def v_tokens(br, ch, t, b):
            g = ch // 2 if br == "c" else 0
            if g == 1:
                return t.rearrange("q (x r) -> q r x", r=4)[:, b // 2, (b % 2) * P:(b % 2 + 1) * P]
            return t[:, b * P:(b + 1) * P]

        def score_of(i):
            o = P * i * (i + 1) // 2
            return score[:, o:o + P * (i + 1)]

        def logit_bias(u):
            if u["br"] == "a":
                return negc[:, u["hh"], 0:u["W"]]
            if u["br"] == "b":
                return score_of(u["b"])
            return bmc[:, u["hh"], 0:P] if u["ch"] // 2 == 2 else bmc[:, u["hh"], 2 * P - u["W"]:2 * P]

        def stats_of(u):
            if u["br"] == "c":
                h4 = 2 * (u["ch"] % 2) + u["hh"]
                return stat[:, u["ch"] // 2, u["b"], 0, h4:h4 + 1], stat[:, u["ch"] // 2, u["b"], 1, h4:h4 + 1]
            k = u["unit"] % 8
            return nmax[:, k:k + 1], den[:, k:k + 1]

        steps = {}
        for kind, a in plan:
            steps.setdefault(kind, []).append(a)
        last_low = {"w" + br: max(z["hs"] for z in steps["z_split"] if z["br"] == br) + 1 for br in "cab"}
        split_of = {(z["br"], z["c"], z["th"]): z["hs"] for z in steps["z_split"]}
        mix_base = {"a": 0, "b": 2 * KC}
        b_low = max(r["hs"] for r in steps["rms_norm"]) + 2
        last_S, last_pv, last_unit = {}, {}, {}
        for u in units:
            last_S[u["br"], u["ch"]] = u["S"]
            last_pv[u["br"], u["ch"]] = u["pv"]
            last_unit[u["br"], 2 * u["ch"] + u["hh"]] = u["unit"]
        units_c = [u for u in units if u["br"] == "c"]
        stat_uses = [a["use"] for a in steps["stat_turn"]]
        share_uses = [a["use"] for a in steps["share_turn"]]

        def turned_room(eng, grp):
            if grp["tp"] >= PTS:
                full(eng, info["unit_of_tp"][grp["tp"] - PTS]["pv"])

        def stage_room(eng, u):
            if u["b"] % 4 == 0 and u["stage"] >= 2:
                full(eng, info["y_turns"][u["stage"] - 2])

        block = ctx.enter_context(nc.Block())

        @block.sync
        def _(sp):
            with nc.allow_non_contiguous_dma(reason="parameters, one value per partition"):
                sp.dma_start(gn[:], norm_g[0].rearrange("(k p) -> p k", p=P)).then_inc(consts_in, 16)
                sp.dma_start(gq[:, 0:2], g_cq[0].rearrange("(k p) -> p k", p=P)).then_inc(consts_in, 16)
                sp.dma_start(gq[:, 2:3], g_ckv[0].rearrange("(k p) -> p k", p=P)).then_inc(consts_in, 16)
                sp.dma_start(bf[:], b_forget[0].rearrange("(h o) -> h o", o=1)).then_inc(consts_in, 16)
            for i in range(TB):
                sp.dma_start(xn[:, i, :], x[0, i * P:(i + 1) * P, :]).then_inc(x_in[i // 4], 16)
            sp.dma_start(uq_raw[:].rearrange("p k h d -> p k (h d)"),
                         w_uq[0].rearrange("(k p) n -> p k n", p=P)).then_inc(pw_in, 16)
            sp.dma_start(ix_raw[:].rearrange("p k h d -> p k (h d)"),
                         w_uq_idx[0].rearrange("(k p) n -> p k n", p=P)).then_inc(pw_in, 16)
            sp.dma_start(ukv_raw[:].rearrange("p a d -> p (a d)"), w_ukv[0]).then_inc(pw_in, 16)
            for n, (src, _) in enumerate(loads):
                if n >= RAW:
                    sp.wait_ge(w_low, n - RAW + 1)
                for col, ap in src:
                    if col is None:
                        dst = w_raw[:, n % RAW].rearrange("p k c -> p (k c)")
                    else:
                        dst = w_raw[:, n % RAW, 0:blocks[n]["nk"], col:col + ap.shape[2]]
                    sp.dma_start(dst, ap).then_inc(raw_in[n % RAW], 16)
            for b in range(TB):
                sp.wait_ge(out_ready, b + 1)
                sp.dma_start(out[0, b * P:(b + 1) * P, :], xo[b]).then_inc(stored, 16)
            sp.wait_ge(stored, 16 * TB)

        @block.gpsimd
        def _(pool):
            g = nc.gpsimd
            chain = [0]

            def then(ins):
                chain[0] += 1
                ins.then_inc(pool_consts, 1)
                pool.wait_ge(pool_consts, chain[0])

            then(g.memset(ident[:], 0.0))
            then(g.affine_select(ident[:], ident[:], [[-1, P]], ALU.not_equal, 1.0, base=0, channel_multiplier=1))
            then(g.memset(ident_b[:], 0.0))
            then(g.affine_select(ident_b[:], ident_b[:], [[-1, P]], ALU.not_equal, 1.0, base=0, channel_multiplier=1))
            then(g.memset(tri_b[:], 0.0))
            then(g.affine_select(tri_b[:], tri_b[:], [[-1, P]], ALU.is_ge, NEG, base=0, channel_multiplier=1))
            then(g.iota(band[:], [[1, 2 * P]], base=-P, channel_multiplier=-1, allow_small_or_imprecise_dtypes=True))
            then(g.affine_select(band[:], band[:], [[-1, 2 * P]], ALU.is_ge, NEG, base=P, channel_multiplier=1))
            then(g.affine_select(band[:], band[:], [[1, 2 * P]], ALU.is_ge, NEG, base=0, channel_multiplier=-1))
            then(g.memset(pairs[:], NEG))
            for a in range(2):
                sub = pairs[HD * a:HD * a + HD, HD * a:HD * a + HD]
                then(g.iota(sub, [[1, HD]], base=0, channel_multiplier=-1, allow_small_or_imprecise_dtypes=True))
                then(g.affine_select(sub, sub, [[-1, HD]], ALU.is_ge, NEG, base=0, channel_multiplier=1))
            for i in range(2):
                m = score_of(i)
                then(g.iota(m, [[1, P * (i + 1)]], base=-P * i, channel_multiplier=-1,
                            allow_small_or_imprecise_dtypes=True))
                then(g.affine_select(m, m, [[-1, P * (i + 1)]], ALU.is_ge, NEG, base=P * i, channel_multiplier=1))
            k = 0
            for kind, a in plan:
                if kind == "phase":
                    k += 1
                    if a["name"] == "c":
                        pool.wait_ge(kv_spilled, 32)
                        pool.wait_ge(spilled, 16 * B_HEADS)
                        for i in range(2, TB):
                            pool.wait_ge(score_done, i - 1)
                            m = score_of(i)[:, P * i:P * (i + 1)]
                            g.affine_select(m, m, [[-1, P]], ALU.is_ge, CAUSAL, base=0,
                                            channel_multiplier=1).then_inc(pool_causal, 1)
                    if a["name"] in ("a", "b_merge"):
                        for s in range(2):
                            pool.wait_ge(m_stored[s], 16 * (KC // 2) * (1 if a["name"] == "a" else 2))
                    if k > 1:
                        phase_end(pool, "pool", k - 1)
                    if a["name"] == "c":
                        g.iota(srow[:], [[1, T]], base=0, channel_multiplier=-1,
                               allow_small_or_imprecise_dtypes=True).then_inc(pool_srow, 1)
                    if a["name"] == "b":
                        pool.dma_start(khb[:], kb_dram).then_inc(kv_in, 16)
                        pool.dma_start(V["b"][:], vb_dram).then_inc(kv_in, 16)
                    if a["name"] in ("b", "b_merge"):
                        for c in range(2):
                            pool.dma_start(ms[:, c, :], m_dram[c]).then_inc(m_loaded[c], 16)
                    if a["name"] == "o":
                        pool.dma_start(fg, final_g.rearrange("(o d) -> o d", o=1).to_broadcast([P, D])).then_inc(fg_in, 16)
                        for b in range(TB):
                            pool.dma_start(xo[b], x[0, b * P:(b + 1) * P, :]).then_inc(xo_in, 16)
                            pool.wait_ge(xo_in, 16 * (b + 1))
                elif kind == "b_k":
                    pool.wait_ge(low_ready, a["hs"] + 2)
                    pool.dma_start(kb_dram, iq_st[:]).then_inc(kv_spilled, 16)
                elif kind == "b_v":
                    freed(pool, a["u"][0])
                    pool.dma_start(vb_dram, v_st[:]).then_inc(kv_spilled, 16)
                elif kind == "b_q" and a["th"]:
                    pool.wait_ge(low_ready, a["hs"] + 1)
                    pool.dma_start(qb_dram[a["h"]], bq_st[:]).then_inc(spilled, 16)
                elif kind == "logits" and a["br"] == "b" and a["b"] == 0:
                    for h in ([0, 1] if a["h"] == 0 else [a["h"] + 1] if a["h"] + 1 < B_HEADS else []):
                        if h >= 2:
                            pool.wait_ge(s_full, a["S"])
                        pool.dma_start(qb[:, h % 2, :], qb_dram[h]).then_inc(qb_in[h % 2], 16)
                elif kind == "w" and a["th"]:
                    br, c = a["br"], a["c"]
                    if br == "c":
                        for u in a["u"]:
                            freed(pool, u)
                    else:
                        pool.wait_ge(mixed, mix_base[br] + 2 * c + 2)
                    if br != "b":
                        pool.dma_start(m_dram[c], ms[:, c % 2, :]).then_inc(m_stored[c % 2], 16)
                    if br != "c" and c + 2 < KC:
                        if br == "a":
                            pool.wait_ge(m_stored[c % 2], 16 * (KC // 2 + c // 2 + 1))
                        pool.dma_start(ms[:, c % 2, :], m_dram[c + 2]).then_inc(m_loaded[c % 2], 16)

        @block.tensor
        def _(pe):
            def split_product(out_, wh, wl, mh, ml, start, stop):
                pe.matmul(out_, wh, mh, start=start, stop=False)
                pe.matmul(out_, wh, ml, start=False, stop=False)
                return pe.matmul(out_, wl, mh, start=False, stop=stop)

            k = 0
            for kind, a in plan:
                if kind == "phase":
                    k += 1
                    if k > 1:
                        phase_end(pe, "pe", k - 1)
                elif kind == "x_turn":
                    if a["kc"] == 0:
                        pe.wait_ge(xs_ready, 4 * a["th"] + 4)
                        pe.wait_ge(pool_consts, 2)
                    claim(pe, a["use"])
                    for j in range(4):
                        ins = pe.transpose(bank[a["use"][0]][:, j * P:(j + 1) * P],
                                           xn[:, 4 * a["th"] + j, a["kc"] * P:(a["kc"] + 1) * P], ident[:])
                    ins.then_inc(bank_full[a["use"][0]], 1)
                elif kind == "block":
                    n, b, th = a["n"], blocks[a["n"]], a["th"]
                    pe.wait_ge(w_low, n + 1)
                    if a["first"]:
                        if a["src"] == "h":
                            pe.wait_ge(low_ready, 2 * KC)
                        elif b["c"] == 0:
                            pe.wait_ge(low_ready, last_low[b["kind"]])
                        claim(pe, a["u"])
                    br, w = b["kind"][1], w_hl[:, n % SPL]
                    ts = slice(th * HALF, (th + 1) * HALF)
                    for kk in range(a["nk"]):
                        c = a["base"] + kk
                        mh, ml = ((hs[:, 0, c, ts], hs[:, 1, c, ts]) if a["src"] == "h" else
                                  (YH[br][:, c, ts], YL[br][:, c, ts]))
                        ins = split_product(bank[th][:], w[:, 0, kk, :], w[:, 1, kk, :], mh, ml,
                                            a["first"] and kk == 0, a["last"] and kk == a["nk"] - 1)
                    if a["last"]:
                        ins.then_inc(bank_full[th], 1)
                    elif th == 1:
                        ins.then_inc(w_used, 1)
                elif kind == "rms_sum":
                    pe.wait_ge(rms_sq, 1 if a["name"] == "cq" else 2)
                    pe.wait_ge(ones_ready, 1)
                    for th, u in enumerate(a["u"]):
                        claim(pe, u)
                        for c in range(a["n"]):
                            ins = pe.matmul(bank[u[0]][:], ones[:], c_tmp[:, c, th * HALF:(th + 1) * HALF],
                                            start=c == 0, stop=c == a["n"] - 1)
                        ins.then_inc(bank_full[u[0]], 1)
                elif kind == "natural":
                    for u in tiles["small", 0]:
                        freed(pe, u)
                    for half, u in enumerate(a["u"]):
                        claim(pe, u)
                        for j in range(4):
                            i = 4 * half + j
                            ins = pe.transpose(bank[u[0]][:, j * P:(j + 1) * P], small[:, i * P:(i + 1) * P], ident[:])
                        ins.then_inc(bank_full[u[0]], 1)
                elif kind == "b_k":
                    pe.wait_ge(pw_low, 3)
                    pe.wait_ge(low_ready, b_low)
                    for th, u in enumerate(a["u"]):
                        claim(pe, u)
                        ts = slice(th * HALF, (th + 1) * HALF)
                        split_product(bank[u[0]][:], ukv_hl[:, 0, 0:2, :], ukv_hl[:, 1, 0:2, :], ckv_hl[:, 0, ts],
                                      ckv_hl[:, 1, ts], True, True).then_inc(bank_full[u[0]], 1)
                elif kind == "b_v":
                    u = a["u"][0]
                    claim(pe, u)
                    for b in range(TB):
                        tk = slice(b * P, (b + 1) * P)
                        ins = split_product(bank[u[0]][:, b * HD:(b + 1) * HD], ckv_hl[:, 0, tk], ckv_hl[:, 1, tk],
                                            ukv_hl[:, 0, 2, :], ukv_hl[:, 1, 2, :], True, True)
                    ins.then_inc(bank_full[u[0]], 1)
                elif kind in ("b_q", "i_q"):
                    w, u, th = (uq_hl if kind == "b_q" else ix_hl), a["u"], a["th"]
                    claim(pe, u)
                    ts = slice(th * HALF, (th + 1) * HALF)
                    for c in range(2):
                        ins = split_product(bank[u[0]][:], w[:, 0, c, a["h"]], w[:, 1, c, a["h"]],
                                            cq_hl[:, 0, c, ts], cq_hl[:, 1, c, ts], c == 0, c == 1)
                    ins.then_inc(bank_full[u[0]], 1)
                elif kind == "i_dots":
                    if a["i"] == 2:
                        pe.wait_ge(low_ready, a["low"])
                        pe.wait_ge(kidx_low, 1)
                    if a["S"] >= 2:
                        pe.wait_ge(s_free, a["S"] - 1)
                    W = (a["i"] + 1) * P
                    for c0 in range(0, W, HALF):
                        c1 = min(W, c0 + HALF)
                        ins = pe.matmul(slot[a["S"] % 2][:, c0:c1], iq_st[:, a["h"] % 2, a["i"] * P:(a["i"] + 1) * P],
                                        kidx_hl[:, c0:c1], start=True, stop=True)
                    ins.then_inc(s_full, 1)
                elif kind == "v_turn":
                    br = a["br"]
                    for u in tiles["v" + br, a["ch"]]:
                        freed(pe, u)
                    claim(pe, a["use"])
                    for j in range(4):
                        ins = pe.transpose(bank[a["use"][0]][:, j * P:(j + 1) * P],
                                           v_tokens(br, a["ch"], VT[br][:], 4 * a["half"] + j), ident[:])
                    ins.then_inc(bank_full[a["use"][0]], 1)
                elif kind == "c_bcast":
                    pe.wait_ge(cum_ready, 1)
                    pe.wait_ge(sel_ready, 2)
                    for th, u in enumerate(a["u"]):
                        claim(pe, u)
                        pe.matmul(bank[u[0]][:], selA[:, a["h"], :], cumT[:, th * HALF:(th + 1) * HALF],
                                  start=True, stop=True).then_inc(bank_full[u[0]], 1)
                elif kind == "logits":
                    br, W = a["br"], a["W"]
                    if br != "b" and a["b"] == 0 and a["hh"] == 0:
                        for w in "qk":
                            for u in tiles[w + br, a["ch"]]:
                                freed(pe, u)
                    if br == "b" and a["b"] == 0:
                        pe.wait_ge(kv_in, 32)
                        pe.wait_ge(qb_in[a["h"] % 2], 16 * (a["h"] // 2 + 1))
                    if a["S"] >= 2:
                        pe.wait_ge(s_free, a["S"] - 1)
                    o = slot[a["S"] % 2]
                    if br == "b":
                        q = qb[:, a["h"] % 2, a["b"] * P:(a["b"] + 1) * P]
                        for c0 in range(0, W, HALF):
                            c1 = min(W, c0 + HALF)
                            pe.matmul(o[:, c0:c1], q, khb[:, 0, c0:c1], start=True, stop=False)
                            ins = pe.matmul(o[:, c0:c1], q, khb[:, 1, c0:c1], start=False, stop=True)
                    else:
                        rows = slice(HD * a["hh"], HD * a["hh"] + HD)
                        qt, kt = Q[br][a["ch"] % 2], K[br][a["ch"] % 2]
                        q = v_tokens(br, a["ch"], qt[rows, :], a["b"])
                        g = a["ch"] // 2 if br == "c" else 0
                        if br == "c" and g == 0:
                            keys = kt[rows, (a["b"] + 1) * P - W:(a["b"] + 1) * P]
                        elif g == 1:
                            keys = kt[rows, :].rearrange("q (x r) -> q r x", r=4)[:, a["b"] // 2, 0:W]
                        elif g == 2:
                            keys = v_tokens(br, a["ch"], kt[rows, :], a["b"])
                        if br == "c":
                            ins = pe.matmul(o[:, 0:W], q, keys, start=True, stop=True)
                        else:
                            for c0 in range(0, W, HALF):
                                c1 = min(W, c0 + HALF)
                                pe.matmul(o[:, c0:c1], q, kt[rows, c0:c1], start=True, stop=c1 < W)
                            ins = pe.matmul(o[:, W - P:W], ident_b[:], tri_b[:], start=False, stop=True)
                    ins.then_inc(s_full, 1)
                elif kind == "turn":
                    pe.wait_ge(s_free, a["S"] + 1)
                    pr = PR[a["br"]][:, a["unit"] % 2]
                    for grp in a["groups"]:
                        claim(pe, grp["use"])
                        for j in range(grp["nc"]):
                            c = grp["c0"] + j
                            ins = pe.transpose(bank[grp["use"][0]][:, j * P:(j + 1) * P], pr[:, c * P:(c + 1) * P], ident[:])
                        ins.then_inc(bank_full[grp["use"][0]], 1)
                elif kind == "pv":
                    for grp in a["groups"]:
                        freed(pe, grp["use"])
                    if a["br"] != "b":
                        freed(pe, tiles["V" + a["br"], a["ch"], 1])
                    claim(pe, a["pv"])
                    n = a["W"] // P
                    first = a["b"] + 1 - n
                    if a["br"] == "c" and a["ch"] // 2 == 1:
                        first = a["b"] // 2 * 2
                    for grp in a["groups"]:
                        for j in range(grp["nc"]):
                            c = grp["c0"] + j
                            v = (V["b"][:, c, :] if a["br"] == "b" else
                                 V[a["br"]][a["ch"] % 2][:, first + c, HD * a["hh"]:HD * a["hh"] + HD])
                            ins = pe.matmul(bank[a["pv"][0]][:, 0:HD], PT[a["br"]][:, grp["tp"] % PTS, j, :], v,
                                            start=c == 0, stop=c == n - 1)
                    ins.then_inc(bank_full[a["pv"][0]], 1)
                elif kind == "y_turn":
                    x = a["x"]
                    freed(pe, x["pv"])
                    claim(pe, a["use"])
                    for j in range(4):
                        ins = pe.transpose(bank[a["use"][0]][0:HD, j * P:(j + 1) * P], stage[:, x["stage"] % 2, j, :], ident[:])
                    ins.then_inc(bank_full[a["use"][0]], 1)
                elif kind == "stat_turn":
                    claim(pe, a["use"])
                    if a["g"] == 0 and a["half"] == 0:
                        pe.wait_ge(s_free, units_c[-1]["S"] + 1)
                    for j in range(4):
                        b = 4 * a["half"] + j
                        ins = pe.transpose(bank[a["use"][0]][0:8, j * P:(j + 1) * P],
                                           stat[:, a["g"], b].rearrange("p a h -> p (a h)"), ident[:])
                    ins.then_inc(bank_full[a["use"][0]], 1)
                elif kind == "stat_back":
                    for u in stat_uses:
                        freed(pe, u)
                    claim(pe, a["use"])
                    for i in range(TB):
                        for g in range(3):
                            o = (i * 3 + g) * 8
                            ins = pe.transpose(bank[a["use"][0]][:, o:o + 8], statT[:, g, i * P:(i + 1) * P], ident[0:8, 0:8])
                    ins.then_inc(bank_full[a["use"][0]], 1)
                elif kind == "share_turn":
                    pe.wait_ge(share_ready, 1)
                    claim(pe, a["use"])
                    for j in range(4):
                        ins = pe.transpose(bank[a["use"][0]][0:C_HEADS, j * P:(j + 1) * P],
                                           shareN[:, 4 * a["half"] + j].rearrange("p g h -> p (g h)"), ident[:])
                    ins.then_inc(bank_full[a["use"][0]], 1)
                elif kind == "share":
                    for u in share_uses:
                        freed(pe, u)
                    pe.wait_ge(sel_ready, 1)
                    for th, u in enumerate(a["u"]):
                        claim(pe, u)
                        pe.matmul(bank[u[0]][:], selC[:, 2 * a["c"]:2 * a["c"] + 2, :].rearrange("p h d -> p (h d)"),
                                  shareT[:, th * HALF:(th + 1) * HALF], start=True, stop=True).then_inc(bank_full[u[0]], 1)
                elif kind == "final":
                    for b in range(4):
                        pe.wait_ge(bank_free[b], a["uses"][b])
                    pe.wait_ge(s_free, a["S"])
                    for half in range(2):
                        if half == 0:
                            order = [(cc, tb) for cc in range(KC) for tb in range(TB)]
                        else:
                            order = [(cc, tb) for tb in range(TB) for cc in range(KC)]
                        for cc, tb in order:
                            if half == 0 and tb == 0:
                                pe.wait_ge(m_low, cc + 1)
                                pe.wait_ge(w_low, a["first"] + cc + 1)
                            if half == 1 and cc == 0:
                                pe.wait_ge(o_free, tb + 1)
                                if tb == 0:
                                    pe.wait_ge(w_low, a["first"] + 2 * KC)
                            tk = slice(tb * P, (tb + 1) * P)
                            w = wo_hl[half]
                            ins = split_product(banks8[tb], hs[:, 0, cc, tk], hs[:, 1, cc, tk], w[:, 0, cc, :], w[:, 1, cc, :],
                                                cc == 0, cc == KC - 1)
                            if cc == KC - 1:
                                ins.then_inc(o_full, 1)

        @block.scalar
        def _(act):
            A = nc.scalar.activation
            chain = [0]
            done = [0]

            def then(ins):
                chain[0] += 1
                ins.then_inc(act_chain, 1)
                act.wait_ge(act_chain, chain[0])

            def split_high(upto):
                while done[0] < min(upto, len(blocks)):
                    n = done[0]
                    b = blocks[n]
                    done[0] += 1
                    act.wait_ge(raw_in[n % RAW], loads[n][1])
                    if b["kind"] == "wo":
                        dst = wo_hl[b["half"]][:, 0, b["c"], :]
                        src = w_raw[:, n % RAW].rearrange("p k c -> p (k c)")
                    else:
                        if n >= SPL:
                            block_done(act, n - SPL)
                        dst, src = w_hl[:, n % SPL, 0, 0:b["nk"], :], w_raw[:, n % RAW, 0:b["nk"], :]
                    A(dst, src, ACTF.Copy).then_inc(w_high, 1)

            k = 0
            for kind, a in plan:
                if kind == "phase":
                    k += 1
                    if k > 1:
                        phase_end(act, "act", k - 1)
                    if a["name"] == "x":
                        for th in range(2):
                            act.wait_ge(x_in[th], 16 * 4)
                            for i in range(4 * th, 4 * th + 4):
                                then(A(junk[:], xn[:, i, :], ACTF.Square, accum_out=ssq[:, i:i + 1]))
                            act.sem_inc(ssq_ready, 1)
                            act.wait_ge(var_ready, th + 1)
                            hb = slice(4 * th, 4 * th + 4)
                            A(rstd[:, 1, hb], rstd[:, 0, hb], ACTF.Sqrt).then_inc(sd_ready, 1)
                        split_high(SPL)
                elif kind == "x_turn":
                    full(act, a["use"])
                    A(hs[:, 0, a["kc"], a["th"] * HALF:(a["th"] + 1) * HALF], bank[a["use"][0]][:], ACTF.Copy,
                      scale=gn[:, a["kc"]:a["kc"] + 1]).then_inc(high_ready, 1)
                elif kind == "block":
                    if a["th"] == 0:
                        split_high(min(a["n"] + SPL, info["first_wo"]))
                elif kind in ("cq", "ckv", "small"):
                    th = a["th"]
                    full(act, a["u"][th])
                    dst = small[:] if kind == "small" else c_raw[a["c"]][:]
                    A(dst[:, th * HALF:(th + 1) * HALF], bank[th][:], ACTF.Copy).then_inc(bank_free[th], 1)
                elif kind == "rms_sum":
                    for c in range(a["n"]):
                        ch = a["first_chunk"] + c
                        for u in tiles["cq" if ch < 2 else "ckv", ch]:
                            freed(act, u)
                        if a["name"] == "ckv" and c == 0:
                            act.wait_ge(rms_y, 2)
                        ins = A(c_tmp[:, c, :], c_raw[ch][:], ACTF.Square)
                    ins.then_inc(rms_sq, 1)
                    for th in range(2):
                        kk = 2 * (a["name"] == "ckv") + th
                        act.wait_ge(rms_var, kk + 1)
                        v = c_tmp[:, 0, th * HALF:(th + 1) * HALF]
                        A(v, v, ACTF.Sqrt).then_inc(rms_sd, 1)
                    if a["name"] == "cq":
                        act.wait_ge(pw_in, 48)
                        for r in range(2):
                            A(uq_hl[:, 0, :, :, r, :], uq_raw[:], ACTF.Copy)
                        for r in range(4):
                            ins = A(ix_hl[:, 0, :, :, r, :], ix_raw[:], ACTF.Copy)
                        for r, s in ((0, 0), (1, 0), (2, 1)):
                            ins = A(ukv_hl[:, 0, r, :], ukv_raw[:, s, :], ACTF.Copy)
                        ins.then_inc(pw_high, 1)
                elif kind == "rms_norm":
                    for c in range(a["n"]):
                        ch = a["first_chunk"] + c
                        act.wait_ge(rms_y, ch + 1)
                        dst = ckv_hl[:, 0, :] if ch == 2 else cq_hl[:, 0, ch, :]
                        for th in range(2):
                            ts = slice(th * HALF, (th + 1) * HALF)
                            A(dst[:, ts], c_raw[ch][:, ts], ACTF.Copy).then_inc(high_ready, 1)
                elif kind == "forget":
                    act.wait_ge(rms_y, 3)
                    act.wait_ge(consts_in, 64)
                    for u in tiles["small", 0]:
                        freed(act, u)
                    e = c_tmp[0:A_HEADS, 0, :]
                    then(A(e, small[0:A_HEADS, :], ACTF.Abs, bias=bf[:]))
                    then(A(e, e, ACTF.Exp, scale=-1.0))
                    A(e, e, ACTF.Ln, bias=1.0).then_inc(fg_l, 1)
                    A(kidx_hl[0:32, :], small[64:96, :], ACTF.Copy)
                    A(kidx_hl[32:64, :], small[64:96, :], ACTF.Copy)
                    A(kidx_hl[64:128, :], small[64:128, :], ACTF.Copy).then_inc(kidx_high, 1)
                elif kind == "b_k":
                    for th, u in enumerate(a["u"]):
                        full(act, u)
                        A(iq_st[:, 0, th * HALF:(th + 1) * HALF], bank[u[0]][:], ACTF.Copy).then_inc(high_ready, 1)
                elif kind == "b_v":
                    u = a["u"][0]
                    full(act, u)
                    A(v_st[:].rearrange("p b d -> p (b d)"), bank[u[0]][:], ACTF.Copy).then_inc(bank_free[u[0]], 1)
                elif kind in ("b_q", "i_q"):
                    h = a["h"]
                    th, u = a["th"], a["u"]
                    if kind == "b_q":
                        if h and th == 0:
                            act.wait_ge(spilled, 16 * h)
                        dst, scale = bq_st[:], SCALE * 2.0 ** (h + 1)
                    else:
                        if h < 2:
                            act.wait_ge(kv_spilled, 32)
                        else:
                            act.wait_ge(s_full, 6 * (h - 1))
                        dst, scale = iq_st[:, h % 2, :], 1.0
                    full(act, u)
                    A(dst[:, th * HALF:(th + 1) * HALF], bank[u[0]][:], ACTF.Copy, scale=scale).then_inc(high_ready, 1)
                elif kind == "i_dots":
                    act.wait_ge(s_full, a["S"] + 1)
                    if a["n"] >= 2:
                        act.wait_ge(relu_used, a["n"] - 1)
                    W = (a["i"] + 1) * P
                    A(relu_t[:, a["n"] % 2, 0:W], slot[a["S"] % 2][:, 0:W], ACTF.Relu).then_inc(s_free, 1)
                elif kind in ("qc", "qa", "kc", "ka", "vc", "va"):
                    br, what, th = kind[1], kind[0], a["th"]
                    dst = {"q": Q, "k": K}[what][br][a["c"] % 2] if what != "v" else VT[br]
                    if what == "v" and a["c"] and th == 0:
                        full(act, tiles["V" + br, a["c"] - 1, 1])
                    elif what != "v" and a["c"] >= 2 and th == 0:
                        act.wait_ge(s_full, last_S[br, a["c"] - 2] + 1)
                    full(act, a["u"][th])
                    d, src = dst[:, th * HALF:(th + 1) * HALF], bank[th][:]
                    if br == "c" and a["c"] // 2 == 2:
                        d = dst[:].rearrange("p (c u) -> p u c", c=16)[:, 32 * th:32 * th + 32, :]
                        src = src.rearrange("p (u c) -> p u c", c=16)
                    A(d, src, ACTF.Copy, scale=SCALE if what == "q" else 1.0).then_inc(bank_free[th], 1)
                elif kind == "v_turn":
                    br = a["br"]
                    if a["ch"] >= 2 and a["half"] == 0:
                        full(act, last_pv[br, a["ch"] - 2])
                    full(act, a["use"])
                    A(V[br][a["ch"] % 2][:, 4 * a["half"]:4 * a["half"] + 4, :].rearrange("p b c -> p (b c)"), bank[a["use"][0]][:],
                      ACTF.Copy).then_inc(bank_free[a["use"][0]], 1)
                elif kind == "c_bcast":
                    if a["h"] >= 2:
                        act.wait_ge(logit_ready, last_unit["a", a["h"] - 2] + 1)
                    for th, u in enumerate(a["u"]):
                        full(act, u)
                        A(negc[:, a["h"] % 2, th * HALF:(th + 1) * HALF], bank[u[0]][:], ACTF.Copy,
                          scale=-1.0).then_inc(bank_free[u[0]], 1)
                elif kind == "logits":
                    if a["br"] == "c" and a["b"] == 0:
                        h, g = 2 * a["ch"] + a["hh"], a["ch"] // 2
                        if h >= 2:
                            act.wait_ge(logit_ready, last_unit["c", h - 2] + 1)
                        m = band[:] if g < 2 else pairs[:]
                        if h == 0:
                            act.wait_ge(pool_consts, 14)
                        A(bmc[:, a["hh"], 0:m.shape[1]], m, ACTF.Copy,
                          scale=float(np.float32(c_slope(h)) * np.float32(C_GROUPS[g][1]))).then_inc(bm_ready, 1)
                elif kind == "exp":
                    act.wait_ge(logit_ready, a["unit"] + 1)
                    if a["unit"] >= 2:
                        full(act, units[a["unit"] - 2]["groups"][-1]["use"])
                    mx, dn = stats_of(a)
                    A(PR[a["br"]][:, a["unit"] % 2, 0:a["W"]], slot[a["S"] % 2][:, 0:a["W"]], ACTF.Exp, bias=mx,
                      scale=-1.0, accum_out=dn).then_inc(s_free, 1)
                elif kind == "turn":
                    for grp in a["groups"]:
                        if grp["tp"] % 2 or a["br"] == "a":
                            full(act, grp["use"])
                            turned_room(act, grp)
                            b = grp["use"][0]
                            A(PT[a["br"]][:, grp["tp"] % PTS, 0:grp["nc"], :].rearrange("p c q -> p (c q)"),
                              bank[b][:, 0:grp["nc"] * P], ACTF.Copy).then_inc(bank_free[b], 1)
                elif kind == "pv" and a["br"] == "c":
                    full(act, a["pv"])
                    stage_room(act, a)
                    b = a["pv"][0]
                    A(stage[:, a["stage"] % 2, a["b"] % 4, :], bank[b][:, 0:HD], ACTF.Copy).then_inc(bank_free[b], 1)
                elif kind == "y_turn":
                    x = a["x"]
                    br, ch, b0 = x["br"], x["ch"], x["b"] - 3
                    full(act, a["use"])
                    y = Y[br][HD * x["hh"]:HD * x["hh"] + HD, ch, :]
                    src = bank[a["use"][0]][0:HD, :]
                    g = ch // 2 if br == "c" else 0
                    if g == 0:
                        y = y[:, b0 * P:(b0 + 4) * P]
                    elif g == 1:
                        y = y.rearrange("q (x r) -> q r x", r=4)[:, b0 // 2:b0 // 2 + 2, :]
                        src = src.rearrange("q (r x) -> q r x", r=2)
                    else:
                        y = y.rearrange("q (u c) -> q c u", c=16)[:, 2 * b0:2 * b0 + 8, :]
                        src = src.rearrange("q (c u) -> q c u", c=8)
                    A(y, src, ACTF.Copy).then_inc(bank_free[a["use"][0]], 1)
                elif kind == "stat_turn":
                    full(act, a["use"])
                    g, half = a["g"], a["half"]
                    y, src = statT[:, g, :], bank[a["use"][0]][0:8, :]
                    if g == 0:
                        y = y[:, half * HALF:(half + 1) * HALF]
                    elif g == 1:
                        y = y.rearrange("q (x r) -> q r x", r=4)[:, 2 * half:2 * half + 2, :]
                        src = src.rearrange("q (r x) -> q r x", r=2)
                    else:
                        y = y.rearrange("q (u c) -> q c u", c=16)[:, 8 * half:8 * half + 8, :]
                        src = src.rearrange("q (c u) -> q c u", c=8)
                    A(y, src, ACTF.Copy).then_inc(bank_free[a["use"][0]], 1)
                elif kind == "stat_back":
                    full(act, a["use"])
                    A(natS[:].rearrange("p i g a h -> p (i g a h)"), bank[a["use"][0]][:, 0:TB * 24],
                      ACTF.Copy).then_inc(bank_free[a["use"][0]], 1)
                    act.wait_ge(st_d, 1)
                    A(eS[:], eS[:], ACTF.Exp).then_inc(st_e, 1)
                elif kind == "share_turn":
                    full(act, a["use"])
                    A(shareT[:, a["half"] * HALF:(a["half"] + 1) * HALF], bank[a["use"][0]][0:C_HEADS, :],
                      ACTF.Copy).then_inc(bank_free[a["use"][0]], 1)
                elif kind == "z":
                    br, c, th = a["br"], a["c"], a["th"]
                    full(act, a["u"][th])
                    if c:
                        act.wait_ge(low_ready, split_of[br, c - 1, th] + 1)
                    A(tm[:, 2 * th, :], bank[th][:], ACTF.Tanh, scale=0.5).then_inc(z_tanh, 1)
                elif kind == "z_split":
                    th = a["th"]
                    act.wait_ge(z_mul, a["zn"] + 1)
                    A(YH[a["br"]][:, a["c"], th * HALF:(th + 1) * HALF], tm[:, 2 * th + 1, :], ACTF.Copy).then_inc(high_ready, 1)
                elif kind == "g":
                    br, c, th = a["br"], a["c"], a["th"]
                    full(act, a["u"][th])
                    if c < 2:
                        act.wait_ge(low_ready, last_low["w" + br])
                    elif br == "c":
                        freed(act, tiles["w" + br, c - 2][th])
                    else:
                        act.wait_ge(mixed, mix_base[br] + 2 * (c - 2) + th + 1)
                    A(tm[:, 2 * (c % 2) + th, :], bank[th][:], ACTF.Tanh, scale=0.5).then_inc(bank_free[th], 1)
                elif kind == "m_split":
                    for u in tiles["gb", KC - 1]:
                        full(act, u)
                    for cc in a["chunks"]:
                        act.wait_ge(mixed, mix_base["b"] + 2 * cc + 2)
                        A(hs[:, 0, cc, :], mT[:, cc, :], ACTF.Copy, scale=0.25).then_inc(m_high, 1)
                elif kind == "final":
                    for cc in range(KC):
                        if cc >= KC - 2:
                            A(hs[:, 0, cc, :], mT[:, cc, :], ACTF.Copy, scale=0.25).then_inc(m_high, 1)
                        split_high(a["first"] + cc + 1)
                    act.wait_ge(m_low, KC)
                    split_high(a["first"] + 2 * KC)
                    for b in range(TB):
                        act.wait_ge(res_ready, b + 1)
                        A(junk_o, xo[b], ACTF.Square, accum_out=ssq[:, b:b + 1]).then_inc(o_ssq, 1)
                        act.wait_ge(o_var, b + 1)
                        A(rstd[:, 1, b:b + 1], rstd[:, 0, b:b + 1], ACTF.Sqrt).then_inc(o_sd, 1)

        @block.vector
        def _(dve):
            v = nc.vector
            chain = [0]
            done = [0]

            def then(ins):
                chain[0] += 1
                ins.then_inc(dve_chain, 1)
                dve.wait_ge(dve_chain, chain[0])

            def split_low(upto):
                while done[0] < min(upto, len(blocks)):
                    n = done[0]
                    b = blocks[n]
                    done[0] += 1
                    dve.wait_ge(w_high, n + 1)
                    if b["kind"] == "wo":
                        hi, lo = wo_hl[b["half"]][:, 0, b["c"], :], wo_hl[b["half"]][:, 1, b["c"], :]
                        src = w_raw[:, n % RAW].rearrange("p k c -> p (k c)")
                    else:
                        hi, lo = w_hl[:, n % SPL, 0, 0:b["nk"], :], w_hl[:, n % SPL, 1, 0:b["nk"], :]
                        src = w_raw[:, n % RAW, 0:b["nk"], :]
                    v.tensor_tensor(lo, src, hi.bitcast(F32), ALU.subtract).then_inc(w_low, 1)

            rounds = [(i, r) for i in range(2, TB) for r in range(ROUNDS)]
            credit, at_round = [0.0], [0]

            def select(us):
                credit[0] += us
                while at_round[0] < len(rounds):
                    i, r = rounds[at_round[0]]
                    cost = 2 * P * (i + 1) / 960 + 0.2
                    if credit[0] < cost:
                        return
                    credit[0] -= cost
                    at_round[0] += 1
                    if r == 0:
                        dve.wait_ge(pool_causal, i - 1)
                    then(v.max(top8[:], score_of(i)))
                    then(v.match_replace(score_of(i), top8[:], score_of(i), TAKEN))
                    if r == ROUNDS - 1:
                        then(v.tensor_scalar(score_of(i), score_of(i), 0.66 * TAKEN, NEG, ALU.is_ge, ALU.mult))
                        dve.wait_ge(pool_srow, 1)
                        then(v.scalar_tensor_tensor(score_of(i), score_of(i), float(-P * i), srow[:, 0:P * (i + 1)],
                                                    ALU.add, ALU.add))

            def low_of(dst, src, hi):
                v.tensor_tensor(dst, src, hi.bitcast(F32), ALU.subtract).then_inc(low_ready, 1)

            def m_split_low(cc):
                dve.wait_ge(m_high, cc + 1)
                v.scalar_tensor_tensor(hs[:, 1, cc, :], mT[:, cc, :], 0.25, hs[:, 0, cc, :].bitcast(F32), ALU.mult,
                                       ALU.subtract).then_inc(m_low, 1)

            rate = (0.0, 0.0)
            k = 0
            for kind, a in plan:
                if kind == "phase":
                    k += 1
                    if a["name"] == "b":
                        select(1e9)
                    if k > 1:
                        phase_end(dve, "dve", k - 1)
                    if a["name"] == "x":
                        v.memset(ones[:], 1.0).then_inc(ones_ready, 1)
                        for th in range(2):
                            hb = slice(4 * th, 4 * th + 4)
                            dve.wait_ge(ssq_ready, th + 1)
                            v.tensor_scalar(rstd[:, 0, hb], ssq[:, hb], 1.0 / D, EPS, ALU.mult, ALU.add).then_inc(var_ready, 1)
                            dve.wait_ge(sd_ready, th + 1)
                            then(v.reciprocal(rstd[:, 2, hb], rstd[:, 1, hb]))
                            for i in range(4 * th, 4 * th + 4):
                                v.tensor_scalar(xn[:, i, :], xn[:, i, :], rstd[:, 2, i:i + 1], None,
                                                ALU.mult).then_inc(xs_ready, 1)
                        dve.wait_ge(consts_in, 64)
                    rate = SELECT_US.get(a["name"], (0.0, 0.0))
                    if a["name"] == "a":
                        dve.wait_ge(pool_consts, 2)
                        v.tensor_copy(selA[:], ident[0:A_HEADS, 0:A_HEADS].unsqueeze(2).to_broadcast([A_HEADS, A_HEADS, P])
                                      ).then_inc(sel_ready, 1)
                    if a["name"] == "b":
                        dve.wait_ge(pool_consts, 18)
                elif kind == "x_turn":
                    dve.wait_ge(high_ready, a["hs"] + 1)
                    ts = slice(a["th"] * HALF, (a["th"] + 1) * HALF)
                    b = a["use"][0]
                    v.scalar_tensor_tensor(hs[:, 1, a["kc"], ts], bank[b][:], gn[:, a["kc"]:a["kc"] + 1],
                                           hs[:, 0, a["kc"], ts].bitcast(F32), ALU.mult,
                                           ALU.subtract).then_inc(low_ready, 1)
                    dve.wait_ge(low_ready, a["hs"] + 1)
                    dve.sem_inc(bank_free[b], 1)
                elif kind == "block":
                    if a["th"] == 0:
                        split_low(min(a["n"] + SPL, info["first_wo"]))
                    select(rate[0])
                elif kind == "rms_sum":
                    width = P * a["n"]
                    for th, u in enumerate(a["u"]):
                        full(dve, u)
                        v.tensor_scalar(c_tmp[:, 0, th * HALF:(th + 1) * HALF], bank[u[0]][:], 1.0 / width, EPS, ALU.mult,
                                        ALU.add).then_inc(rms_var, 1)
                    n0 = 2 * (a["name"] == "ckv")
                    dve.wait_ge(rms_sd, n0 + 2)
                    then(v.reciprocal(c_tmp[:, 0, :], c_tmp[:, 0, :]))
                    for th, u in enumerate(a["u"]):
                        dve.wait_ge(rms_var, n0 + th + 1)
                        dve.sem_inc(bank_free[u[0]], 1)
                    if a["name"] == "cq":
                        dve.wait_ge(pw_high, 1)
                        for r in range(2):
                            ins = v.tensor_tensor(uq_hl[:, 1, :, :, r, :], uq_raw[:], uq_hl[:, 0, :, :, r, :].bitcast(F32),
                                                  ALU.subtract)
                        ins.then_inc(pw_low, 1)
                        for r in range(4):
                            ins = v.tensor_tensor(ix_hl[:, 1, :, :, r, :], ix_raw[:], ix_hl[:, 0, :, :, r, :].bitcast(F32),
                                                  ALU.subtract)
                        ins.then_inc(pw_low, 1)
                        for r, s in ((0, 0), (1, 0), (2, 1)):
                            ins = v.tensor_tensor(ukv_hl[:, 1, r, :], ukv_raw[:, s, :], ukv_hl[:, 0, r, :].bitcast(F32),
                                                  ALU.subtract)
                        ins.then_inc(pw_low, 1)
                elif kind == "rms_norm":
                    for c in range(a["n"]):
                        ch = a["first_chunk"] + c
                        v.scalar_tensor_tensor(c_raw[ch][:], c_raw[ch][:], gq[:, ch:ch + 1], c_tmp[:, 0, :], ALU.mult,
                                               ALU.mult).then_inc(rms_y, 1)
                    dve.wait_ge(rms_y, a["first_chunk"] + a["n"])
                    for c in range(a["n"]):
                        ch = a["first_chunk"] + c
                        hl = ckv_hl if ch == 2 else cq_hl[:, :, ch, :]
                        for th in range(2):
                            ts = slice(th * HALF, (th + 1) * HALF)
                            dve.wait_ge(high_ready, a["hs"] + 2 * c + th + 1)
                            low_of(hl[:, 1, ts], c_raw[ch][:, ts], hl[:, 0, ts])
                elif kind == "forget":
                    mn = c_tmp[0:A_HEADS, 1, :]
                    then(v.tensor_scalar(mn, small[0:A_HEADS, :], bf[:], 0.0, ALU.add, ALU.min))
                    dve.wait_ge(fg_l, 1)
                    v.tensor_tensor_scan(cumT[:], mn, c_tmp[0:A_HEADS, 0, :], 0.0, ALU.add,
                                         ALU.subtract).then_inc(cum_ready, 1)
                    dve.wait_ge(kidx_high, 1)
                    v.tensor_tensor(kidx_hl[64:128, :], small[64:128, :], kidx_hl[64:128, :].bitcast(F32),
                                    ALU.subtract).then_inc(kidx_low, 1)
                elif kind == "natural":
                    for half, u in enumerate(a["u"]):
                        full(dve, u)
                        v.tensor_copy(wnat[:, 4 * half:4 * half + 4, :],
                                      bank[u[0]][:].rearrange("p (j c) -> p j c", j=4)[:, :, 32:32 + IDX_HEADS]
                                      ).then_inc(bank_free[u[0]], 1)
                elif kind == "b_k":
                    for th, u in enumerate(a["u"]):
                        ts = slice(th * HALF, (th + 1) * HALF)
                        dve.wait_ge(high_ready, a["hs"] + th + 1)
                        low_of(iq_st[:, 1, ts], bank[u[0]][:], iq_st[:, 0, ts])
                    for th, u in enumerate(a["u"]):
                        dve.wait_ge(low_ready, a["hs"] + th + 1)
                        dve.sem_inc(bank_free[u[0]], 1)
                elif kind in ("b_q", "i_q"):
                    q_t = bq_st[:] if kind == "b_q" else iq_st[:, a["h"] % 2, :]
                    spans = ((64, 128),) if kind == "b_q" else ((32, 64), (96, 128))
                    scale = SCALE * 2.0 ** (a["h"] + 1) if kind == "b_q" else 1.0
                    th, u = a["th"], a["u"]
                    ts = slice(th * HALF, (th + 1) * HALF)
                    dve.wait_ge(high_ready, a["hs"] + 1)
                    for p0, p1 in spans:
                        ins = v.scalar_tensor_tensor(q_t[p0:p1, ts], bank[u[0]][p0:p1, :], scale,
                                                     q_t[p0:p1, ts].bitcast(F32), ALU.mult, ALU.subtract)
                    ins.then_inc(low_ready, 1)
                    dve.wait_ge(low_ready, a["hs"] + 1)
                    dve.sem_inc(bank_free[u[0]], 1)
                elif kind == "i_dots":
                    W, i = (a["i"] + 1) * P, a["i"]
                    dve.wait_ge(s_free, a["S"] + 1)
                    w = wnat[:, i, a["h"]:a["h"] + 1]
                    if a["h"] == 0:
                        v.tensor_scalar(score_of(i), relu_t[:, a["n"] % 2, 0:W], w, None, ALU.mult).then_inc(relu_used, 1)
                    else:
                        dve.wait_ge(relu_used, a["n"] - 5)
                        v.scalar_tensor_tensor(score_of(i), relu_t[:, a["n"] % 2, 0:W], w, score_of(i), ALU.mult,
                                               ALU.add).then_inc(relu_used, 1)
                    if a["h"] == IDX_HEADS - 1:
                        dve.wait_ge(relu_used, a["n"] + 1)
                        dve.sem_inc(score_done, 1)
                elif kind == "logits":
                    dve.wait_ge(s_full, a["S"] + 1)
                    if a["br"] == "a" and a["b"] == 0:
                        for u in tiles["negc", 2 * a["ch"] + a["hh"]]:
                            freed(dve, u)
                    if a["br"] == "c":
                        dve.wait_ge(bm_ready, 2 * a["ch"] + a["hh"] + 1)
                    o = slot[a["S"] % 2][:, 0:a["W"]]
                    slope = 2.0 ** (-(a["h"] + 1)) if a["br"] == "b" else 1.0
                    v.tensor_tensor_reduce(o, o, logit_bias(a), -slope, 0.0, ALU.add, ALU.min,
                                           stats_of(a)[0]).then_inc(logit_ready, 1)
                elif kind == "turn":
                    for grp in a["groups"]:
                        if grp["tp"] % 2 == 0 and a["br"] != "a":
                            full(dve, grp["use"])
                            turned_room(dve, grp)
                            b = grp["use"][0]
                            v.tensor_copy(PT[a["br"]][:, grp["tp"] % PTS, 0:grp["nc"], :].rearrange("p c q -> p (c q)"),
                                          bank[b][:, 0:grp["nc"] * P]).then_inc(bank_free[b], 1)
                    select(rate[1])
                elif kind == "pv" and a["br"] != "c":
                    r = a["unit"] % 8
                    then(v.reciprocal(rden[:, r:r + 1], den[:, r:r + 1]))
                    full(dve, a["pv"])
                    stage_room(dve, a)
                    b = a["pv"][0]
                    v.tensor_scalar(stage[:, a["stage"] % 2, a["b"] % 4, :], bank[b][:, 0:HD], rden[:, r:r + 1], None,
                                    ALU.mult).then_inc(bank_free[b], 1)
                elif kind == "stat_back":
                    freed(dve, a["use"])
                    nm = [natS[:, :, g, 0, :] for g in range(3)]
                    dn = [natS[:, :, g, 1, :] for g in range(3)]
                    then(v.tensor_tensor(mxS[:], nm[0], nm[1], ALU.min))
                    then(v.tensor_tensor(mxS[:], mxS[:], nm[2], ALU.min))
                    for g in range(3):
                        ins = v.tensor_tensor(eS[:, g], mxS[:], nm[g], ALU.subtract)
                    ins.then_inc(st_d, 1)
                    dve.wait_ge(st_e, 1)
                    for g in range(3):
                        then(v.tensor_tensor(wS[:, g], eS[:, g], dn[g], ALU.mult))
                    then(v.tensor_tensor(wS[:, 0], wS[:, 0], wS[:, 1], ALU.add))
                    then(v.tensor_tensor(wS[:, 0], wS[:, 0], wS[:, 2], ALU.add))
                    then(v.reciprocal(wS[:, 1], wS[:, 0]))
                    for g in range(3):
                        then(v.tensor_tensor(shareN[:, :, g, :], eS[:, g], wS[:, 1], ALU.mult))
                    v.tensor_copy(selC[:], ident[0:C_HEADS, 0:C_HEADS].unsqueeze(2).to_broadcast([C_HEADS, C_HEADS, HD])
                                  ).then_inc(sel_ready, 1)
                    dve.wait_ge(sel_ready, 1)
                    dve.sem_inc(share_ready, 1)
                elif kind == "z":
                    br, c, th = a["br"], a["c"], a["th"]
                    ts = slice(th * HALF, (th + 1) * HALF)
                    z = tm[:, 2 * th, :]
                    dve.wait_ge(z_tanh, a["zn"] + 1)
                    v.scalar_tensor_tensor(z, z, 1.0, bank[th][:], ALU.add, ALU.mult).then_inc(bank_free[th], 1)
                    freed(dve, a["u"][th])
                    if br == "c":
                        sh = a["share"][th]
                        full(dve, sh)
                        then(v.tensor_tensor(z, z, bank[sh[0]][:], ALU.mult))
                        dve.sem_inc(bank_free[sh[0]], 1)
                    v.tensor_tensor(tm[:, 2 * th + 1, :], z, Y[br][:, c, ts], ALU.mult).then_inc(z_mul, 1)
                elif kind == "z_split":
                    br, c, th = a["br"], a["c"], a["th"]
                    ts = slice(th * HALF, (th + 1) * HALF)
                    dve.wait_ge(high_ready, a["hs"] + 1)
                    low_of(YL[br][:, c, ts], tm[:, 2 * th + 1, :], YH[br][:, c, ts])
                elif kind == "w":
                    br, c, th = a["br"], a["c"], a["th"]
                    ts = slice(th * HALF, (th + 1) * HALF)
                    full(dve, a["u"][th])
                    freed(dve, a["gate"][th])
                    gate, so_far = tm[:, 2 * (c % 2) + th, :], ms[:, c % 2, ts]
                    if br == "c":
                        if c >= 2:
                            dve.wait_ge(m_stored[c % 2], 16 * (c // 2))
                        v.scalar_tensor_tensor(so_far, gate, 1.0, bank[th][:], ALU.add, ALU.mult).then_inc(bank_free[th], 1)
                    else:
                        v.scalar_tensor_tensor(gate, gate, 1.0, bank[th][:], ALU.add, ALU.mult).then_inc(bank_free[th], 1)
                        freed(dve, a["u"][th])
                        dve.wait_ge(m_loaded[c % 2], 16 * ((KC // 2 if br == "b" else 0) + c // 2 + 1))
                        v.tensor_tensor(mT[:, c, ts] if br == "b" else so_far, so_far, gate, ALU.add).then_inc(mixed, 1)
                elif kind == "m_split":
                    for cc in a["chunks"]:
                        m_split_low(cc)
                elif kind == "final":
                    for cc in range(KC):
                        if cc >= KC - 2:
                            m_split_low(cc)
                        split_low(a["first"] + cc + 1)
                    split_low(a["first"] + 2 * KC)
                    dve.wait_ge(xo_in, 16 * TB)
                    for b in range(TB):
                        dve.wait_ge(o_full, b + 1)
                        v.tensor_tensor(xo[b][:, 0:HALF], banks8[b], xo[b][:, 0:HALF], ALU.add).then_inc(o_free, 1)
                    for b in range(TB):
                        dve.wait_ge(o_full, TB + b + 1)
                        v.tensor_tensor(xo[b][:, HALF:D], banks8[b], xo[b][:, HALF:D], ALU.add).then_inc(res_ready, 1)
                        dve.wait_ge(o_ssq, b + 1)
                        v.tensor_scalar(rstd[:, 0, b:b + 1], ssq[:, b:b + 1], 1.0 / D, EPS, ALU.mult,
                                        ALU.add).then_inc(o_var, 1)
                        dve.wait_ge(o_sd, b + 1)
                        then(v.reciprocal(rstd[:, 2, b:b + 1], rstd[:, 1, b:b + 1]))
                        if b == 0:
                            dve.wait_ge(fg_in, 16)
                        v.scalar_tensor_tensor(xo[b], xo[b], rstd[:, 2, b:b + 1], fg, ALU.mult, ALU.mult).then_inc(out_ready, 1)


_INS = ["x", "norm_g", "w_in", "b_forget", "g_cq", "w_uq", "w_uq_idx", "g_ckv", "w_ukv", "w_a", "w_b", "w_c", "w_o",
        "final_g"]
_OUTS = [((1, T, D), "float32")]


def kernel(**inputs):
    import numpy as _np
    import concourse.bacc as _bacc
    from concourse import mybir as _mybir
    from concourse.bass_utils import run_bass_kernel_spmd as _run

    nc = _bacc.Bacc("TRN2", target_bir_lowering=False, num_devices=1)
    arrays, args = {}, []
    for name in _INS:
        a = _np.ascontiguousarray(inputs[name])
        arrays[f"in_{name}_dram"] = a
        args.append(nc.dram_tensor(f"in_{name}_dram", a.shape, _mybir.dt.from_np(a.dtype), kind="ExternalInput").ap())
    for i, (shape, dtype) in enumerate(_OUTS):
        dt = _mybir.dt.from_np(_np.dtype(dtype))
        args.append(nc.dram_tensor(f"out_{i}_dram", shape, dt, kind="ExternalOutput").ap())
    hybrid_layer_kernel(nc, *args)
    r = _run(nc, [arrays], core_ids=[0])
    return r.results[0]["out_0_dram"]
```

```python
from contextlib import ExitStack

import numpy as np

import concourse.bass as bass
from concourse import mybir

P = 128
D = 1024
T = 1024
KC = D // P
TB = T // P
HALF = 512
HD = 64
A_HEADS, B_HEADS, C_HEADS, IDX_HEADS = 8, 8, 12, 8
IDX_DIM = 32
TOPK = 256
ROUNDS = TOPK // 8
EPS = 1e-6
SCALE = HD ** -0.5
C_GROUPS = ((128, 1), (512, 4), (2048, 16))
NEG = -1e30
CAUSAL = -1e38
TAKEN = -3e38
SELECT_US = {"c": (0.9, 1.2), "c_merge": (0.3, 0.0), "a": (0.0, 2.0)}

WIDTHS = (("qa", 512), ("ka", 512), ("va", 512), ("fa", 8), ("za", 512), ("cq", 256), ("ckv", 128), ("kidx", 32),
          ("widx", 8), ("zb", 512), ("qc", 768), ("kc", 768), ("vc", 768), ("zc", 768), ("ga", D), ("gb", D), ("gc", D))
COL, at = {}, 0
for _n, _w in WIDTHS:
    COL[_n] = at
    at += _w

F32, F32R, BF16 = mybir.dt.float32, mybir.dt.float32r, mybir.dt.bfloat16
ALU = mybir.AluOpType
ACTF = mybir.ActivationFunctionType

RAW = 3
SPL = 3
PTS = {"a": 4, "b": 2, "c": 4}
LOW = 32
ROWS = LOW + C_HEADS
NCH = {"a": 4, "b": 4, "c": 6}


def c_slope(h):
    return float(np.float32(2.0 ** (-8.0 * (h + 1) / C_HEADS)))


def build_plan():
    plan, uses, blocks = [], [0] * 4, []
    count = {"ring": 0, "tp": 0, "hs": 0, "S": 0, "unit": 0, "z": 0, "bp": 0, "qk": 0}
    tiles, unit_of_tp, units_seen = {}, [], []

    def use(b):
        uses[b] += 1
        return b, uses[b] - 1

    def ring():
        count["ring"] += 1
        return use(2 + count["ring"] % 2)

    def nxt(name, n=1):
        count[name] += n
        return count[name] - n

    def step(kind, **kw):
        plan.append((kind, kw))
        return kw

    later, defer = [], [False]

    def flush_later():
        while later:
            later.pop(0)()

    def tile_pieces(kind, c, src, chunks=KC, **kw):
        u = [use(0), use(1)]
        tiles[kind, c] = u

        def read(th):
            name = kind[0] if kind[0] in "zgw" and len(kind) == 2 else kind
            if name == "z":
                share = ring()
                step("share", br=kw["br"], c=c, th=th, u=share)
                step("z", c=c, u=u, th=th, zn=nxt("z"), share=share, **kw)
                if th:
                    for t in range(2):
                        step("z_split", c=c, th=t, zn=count["z"] - 2 + t, hs=nxt("hs"), br=kw["br"])
            else:
                if name in ("qa", "ka"):
                    kw["n"] = nxt("qk")
                step(name, c=c, u=u, th=th, **kw)

        for base in range(0, chunks, 4):
            nk = min(4, chunks - base)
            last = base + nk == chunks
            blocks.append(dict(kind=kind, nk=nk, c=c, base=base, last=last, done=u[1]))
            n = len(blocks) - 1
            for th in range(2):
                step("block", n=n, base=base, nk=nk, u=u[th], th=th, first=base == 0, last=last, src=src)
                if last:
                    later.append(lambda th=th: read(th))
                    if not defer[0]:
                        flush_later()
                yield

    def tile(*args, **kw):
        for _ in tile_pieces(*args, **kw):
            pass

    fill, owed = [], [0.0]

    def pump(pieces):
        owed[0] += pieces
        while owed[0] >= 1 and fill:
            owed[0] -= 1
            flush_later()
            try:
                next(fill[0])
            except StopIteration:
                fill.pop(0)
                owed[0] += 1
        if not fill:
            owed[0] = 0.0

    def flush():
        while fill:
            pump(1)
        flush_later()

    def softmax_run(units, before, rate):
        n = len(units)
        defer[0] = True
        for s in range(n + 3):
            for f in before.get(s, []):
                f()
            if s < n:
                units[s].update(S=nxt("S"), unit=nxt("unit"))
                units_seen.append(units[s])
                plan.append(("logits", units[s]))
            if 1 <= s <= n:
                plan.append(("exp", units[s - 1]))
            pump(rate)
            if s >= 3:
                units[s - 3]["pv"] = ring()
                plan.append(("pv", units[s - 3]))
            if 2 <= s <= n + 1:
                x = units[s - 2]
                chunks = x["W"] // P
                x["groups"] = []
                for c0 in range(0, chunks, 4):
                    x["groups"].append(dict(use=ring(), tp=nxt("tp"), c0=c0, nc=min(4, chunks - c0)))
                    if x["br"] == "b":
                        x["groups"][-1]["bp"] = nxt("bp")
                    unit_of_tp.append(x)
                plan.append(("turn", x))
            flush_later()
        defer[0] = False

    def attend(br, after):
        units, before = [], {}
        for ch in range(NCH[br]):
            def v_turns(ch=ch):
                flush()
                for half in range(2):
                    tiles["V" + br, ch, half] = ring()
                    step("v_turn", br=br, ch=ch, half=half, use=tiles["V" + br, ch, half])
                fill.extend(qkv(br, ch + 1) if ch + 1 < NCH[br] else after())
            at = len(units)
            before.setdefault(at, []).append(v_turns)
            for hh in range(2):
                if br == "a":
                    def bcast(h=2 * ch + hh):
                        tiles["negc", h] = [ring(), ring()]
                        step("c_bcast", h=h, u=tiles["negc", h])
                    before.setdefault(max(0, len(units) - 1), []).append(bcast)
                for b in range(TB):
                    W = {0: P * min(b + 1, 2), 1: P * (b % 2 + 1), 2: P}[ch // 2] if br == "c" else P * (b + 1)
                    units.append(dict(br=br, ch=ch, hh=hh, b=b, W=W))
        softmax_run(units, before, 0.8)
        flush()

    def qkv(br, ch):
        return [tile_pieces(w + br, ch, "h") for w in "qkv"]

    def share_turns(br):
        for half in range(2):
            step("share_turn", br=br, half=half, use=ring(), hs=nxt("hs"))

    def merge(br):
        n = NCH[br]
        for c in range(n):
            yield from tile_pieces("z" + br, c, "h", br=br)
        yield from tile_pieces("g" + br, 0, "h", br=br)
        for c in range(KC):
            if c + 1 < KC:
                yield from tile_pieces("g" + br, c + 1, "h", br=br)
            if br == "b" and c == KC - 2:
                step("m_split", chunks=range(4))
            yield from tile_pieces("w" + br, c, "y", chunks=n, br=br, gate=tiles["g" + br, c])
            if br == "b" and c == KC - 2:
                step("m_split", chunks=range(4, KC - 2))

    step("phase", name="x")
    for th in range(2):
        for kc in range(KC):
            step("x_turn", kc=kc, th=th, use=use(kc % 4), hs=nxt("hs"))
    step("phase", name="small")
    tile("cq", 0, "h")
    tile("cq", 1, "h")
    fill.extend([tile_pieces("ckv", 2, "h"), tile_pieces("small", 0, "h")] + qkv("c", 0))
    for name, first, n in (("cq", 0, 2), ("ckv", 2, 1)):
        step("rms_sum", name=name, first_chunk=first, n=n, u=[ring(), ring()])
        pump(4)
        step("rms_norm", name=name, first_chunk=first, n=n, hs=nxt("hs", 2 * n))
    step("forget")
    step("natural", u=[ring(), ring()])
    pump(4)
    step("phase", name="index")
    step("b_k", u=[ring(), ring()], hs=nxt("hs", 2))
    step("b_v", u=[ring()])
    low = {}
    for h in range(IDX_HEADS + 1):
        def project(kind, th):
            if h < IDX_HEADS:
                step(kind, h=h, th=th, u=ring(), hs=nxt("hs"))
                if kind == "i_q":
                    low[h] = count["hs"]
        beside = [lambda: project("i_q", 0), lambda: project("i_q", 1), lambda: pump(1), lambda: project("b_q", 0),
                  lambda: project("b_q", 1), lambda: None]
        for i, other in zip(range(2, TB), beside):
            if h:
                step("i_dots", h=h - 1, i=i, S=nxt("S"), n=(h - 1) * 6 + i - 2, low=low[h - 1])
            other()
    step("phase", name="c")
    attend("c", lambda: qkv("a", 0))
    step("phase", name="c_stats")
    for g in range(3):
        for half in range(2):
            step("stat_turn", g=g, half=half, use=ring())
    fill.append(merge("c"))
    pump(1)
    step("stat_back", use=ring())
    pump(1)
    share_turns("c")
    step("phase", name="c_merge")
    flush()
    step("phase", name="a")
    attend("a", lambda: [])
    step("phase", name="b")
    share_turns("a")
    fill.append(merge("a"))
    pump(3)
    softmax_run([dict(br="b", ch=h // 2, hh=h % 2, b=b, W=(b + 1) * P, h=h)
                 for h in range(B_HEADS) for b in range(TB)], {}, 0.95)
    flush()
    step("phase", name="b_merge")
    fill.append(merge("b"))
    pump(2)
    share_turns("b")
    flush()
    step("phase", name="o")
    first_wo = len(blocks)
    for half in range(2):
        for cc in range(KC):
            blocks.append(dict(kind="wo", nk=4, c=cc, half=half))
    step("final", first=first_wo, uses=list(uses), S=count["S"])
    return plan, blocks, dict(unit_of_tp=unit_of_tp, units=units_seen, tiles=tiles, first_wo=first_wo)


def hybrid_layer_kernel(nc, x, norm_g, w_in, b_forget, g_cq, w_uq, w_uq_idx, g_ckv, w_ukv, w_a, w_b, w_c, w_o, final_g,
                        out):
    plan, blocks, info = build_plan()
    tiles, units = info["tiles"], info["units"]
    with ExitStack() as ctx:
        def sb(name, shape, dt=F32, es=ctx):
            return es.enter_context(nc.sbuf_tensor(name, shape, dt))

        def psum(name, cols):
            return ctx.enter_context(nc.psum_tensor(name, [P, cols], F32))

        def sem(name):
            return ctx.enter_context(nc.semaphore(name))

        hs = sb("hs", [P, 2, KC, T], F32R)
        w_raw = sb("w_raw", [P, RAW, 4, P])
        w_hl = sb("w_hl", [P, SPL, 2, 4, P], F32R)
        score = sb("score", [P, P * TB * (TB + 1) // 2])
        rowsT = sb("rowsT", [ROWS, T], F32R)
        sel = sb("sel", [ROWS, A_HEADS, HD], F32R)
        ident = sb("ident", [P, P])
        ident_b = sb("ident_b", [P, P], BF16)
        tri_b = sb("tri_b", [P, P], BF16)
        with ExitStack() as es:
            vb_low = sb("vb_low", [P, TB, HD], F32R, es)
        c_tables = sb("c_tables", [P, 9 * HD])
        band, pairs = c_tables[:, 0:2 * P], c_tables[:, 2 * P:3 * P]
        stat = c_tables[:, 3 * P:9 * HD].rearrange("p (g b a h) -> p g b a h", g=3, b=TB, a=2)
        gn = sb("gn", [P, KC])
        gq = sb("gq", [P, 3])
        bf = sb("bf", [A_HEADS, 1])
        wnat = sb("wnat", [P, TB, IDX_HEADS])
        den = wnat
        top8 = sb("top8", [P, 8])
        nmax = sb("nmax", [P, 8])
        ssq = sb("ssq", [P, TB])
        rstd = sb("rstd", [P, 3, TB])

        def at(kib, name, shape, dt=F32):
            with ExitStack() as es:
                if kib:
                    sb(name + "_below", [P, int(kib * 256)], F32, es)
                return sb(name, shape, dt, es)

        xn, junk = at(0, "xn", [P, TB, D]), at(36, "junk", [P, D])
        cq_hl, ckv_hl = at(0, "cq_hl", [P, 2, 2, T], F32R), at(16, "ckv_hl", [P, 2, T], F32R)
        ix_hl = at(52, "ix_hl", [P, 2, 2, IDX_HEADS, 4, IDX_DIM], F32R)
        uq_hl = at(68, "uq_hl", [P, 2, 2, B_HEADS, 2, HD], F32R)
        ukv_hl, kidx_hl = at(84, "ukv_hl", [P, 2, 3, HD], F32R), at(36, "kidx_hl", [P, T], F32R)
        c_raw = [at(k, f"c_raw{n}", [P, T]) for n, k in enumerate((28, 32, 48))]
        c_tmp, small = at(40, "c_tmp", [P, 2, T]), at(86, "small", [P, T])
        uq_raw, ix_raw = at(90, "uq_raw", [P, 2, B_HEADS, HD]), at(94, "ix_raw", [P, 2, IDX_HEADS, IDX_DIM])
        ukv_raw, ones = at(96, "ukv_raw", [P, 2, HD]), at(96.5, "ones", [P, P])
        iq_st, bq_st, relu_t = at(40, "iq_st", [P, 2, T], F32R), at(32, "bq_st", [P, T], F32R), at(86, "relu_t", [P, 2, T])
        v_st = at(48, "v_st", [P, 2, TB, HD], F32R)
        Y = {"c": at(0, "yc", [P, 6, T]), "a": at(0, "ya", [P, 4, T]), "b": at(64, "yb", [P, 4, T])}
        Q = {"c": [at(k, f"qc{k}", [P, T]) for k in (24, 36)],
             "a": [at(k, f"qa{k}", [P, 2, T], F32R) for k in (80, 16)]}
        K = {"c": [at(k, f"kc{k}", [P, T]) for k in (28, 40)],
             "a": [at(k, f"ka{k}", [P, 2, T], F32R) for k in (88, 56)]}
        V = {"c": [at(k, f"vc{k}", [P, TB, P]) for k in (32, 44)], "a": [at(k, f"va{k}", [P, TB, P]) for k in (68, 24)],
             "b": at(96, "vb", [P, TB, HD], F32R)}
        VT = {"c": at(48, "vtc", [P, T]), "a": at(72, "vta", [P, T])}
        PR = {"c": at(52, "pc", [P, 2, 2 * P]), "a": at(28, "pa", [P, 2, T]), "b": at(32, "pb", [P, 2, T])}
        PT = {"c": at(54, "ptc", [P, 4, 4, P]), "a": at(36, "pta", [P, 4, 4, P]), "b": at(40, "ptb", [P, 2, 2, 4, P], F32R)}
        bmc = at(62, "bmc", [P, 2, 2 * P])
        negc, selA = at(44, "negc", [P, 2, T]), at(52, "selA", [ROWS, A_HEADS, P], F32R)
        khb, qb, srow = at(80, "khb", [P, 2, T], F32R), at(88, "qb", [P, 2, T], F32R), at(76, "srow", [P, T])
        statT, natS = at(24, "statT", [8, 3, T]), at(36, "natS", [P, TB, 3, 2, 4])
        eS, wS, shareN = at(37, "eS", [P, 3, TB, 4]), at(38, "wS", [P, 3, TB, 4]), at(39, "shareN", [P, TB, 3, 4])
        mxS = at(40, "mxS", [P, TB, 4])
        shareC, selC = at(64, "shareC", [ROWS, T], F32R), at(68, "selC", [ROWS, C_HEADS, HD], F32R)
        YH = {"c": at(0, "ych", [P, 6, T], F32R), "a": at(0, "yah", [P, 4, T], F32R), "b": at(64, "ybh", [P, 4, T], F32R)}
        YL = {"c": at(24, "ycl", [P, 6, T], F32R), "a": at(16, "yal", [P, 4, T], F32R), "b": at(0, "ybl", [P, 4, T], F32R)}
        tm = at(48, "tm", [P, 4, HALF])
        ms = at(56, "ms", [P, 2, T])
        mT = at(16, "mT", [P, KC, T])
        wo_hl = [at(64, "wo0", [P, 2, KC, HALF], F32R), at(16, "wo1", [P, 2, KC, HALF], F32R)]
        xo_a, xo_b = at(48, "xo_a", [P, 4, D]), at(0, "xo_b", [P, 4, D])
        xo = [(xo_a if b < 4 else xo_b)[:, b % 4, :] for b in range(TB)]
        fg, junk_o = score[:, 0:D], score[:, D:2 * D]

        bank = [psum(f"bank{i}", HALF) for i in range(4)]
        slot = [psum(f"slot{i}", T) for i in range(2)]
        banks8 = [bank[0][:], bank[1][:], bank[2][:], bank[3][:], slot[0][:, 0:HALF], slot[0][:, HALF:T],
                  slot[1][:, 0:HALF], slot[1][:, HALF:T]]

        qb_dram = nc.dram_tensor("qb_scratch", [B_HEADS, P, T], F32R, kind="Internal").ap()
        kb_dram = nc.dram_tensor("kb_scratch", [P, 2, T], F32R, kind="Internal").ap()
        vb_dram = nc.dram_tensor("vb_scratch", [P, 2, TB, HD], F32R, kind="Internal").ap()
        m_dram = nc.dram_tensor("merged_scratch", [KC, P, T], F32, kind="Internal").ap()

        consts_in, fg_in, xo_in = sem("consts_in"), sem("fg_in"), sem("xo_in")
        x_in = [sem(f"x_in{i}") for i in range(TB)]
        m_stored, m_loaded = [sem(f"m_stored{i}") for i in range(2)], [sem(f"m_loaded{i}") for i in range(2)]
        pw_in = sem("pw_in")
        raw_in = [sem(f"raw_in{i}") for i in range(RAW)]
        w_high, w_low, w_used = sem("w_high"), sem("w_low"), sem("w_used")
        bank_full = [sem(f"bank_full{i}") for i in range(4)]
        bank_free = [sem(f"bank_free{i}") for i in range(4)]
        slot_full, slot_free, logit_ready = sem("slot_full"), sem("slot_free"), sem("logit_ready")
        high_ready, low_ready = sem("high_ready"), sem("low_ready")
        pool_consts, pool_causal, pool_srow = sem("pool_consts"), sem("pool_causal"), sem("pool_srow")
        ones_ready, ssq_ready, var_ready, root_ready, x_scaled = (sem(n) for n in
            ("ones_ready", "ssq_ready", "var_ready", "root_ready", "x_scaled"))
        pw_high, pw_low = sem("pw_high"), sem("pw_low")
        rms_sq, rms_var, rms_root, rms_y = sem("rms_sq"), sem("rms_var"), sem("rms_root"), sem("rms_y")
        forget_log, cum_ready, kidx_high, kidx_low = sem("forget_log"), sem("cum_ready"), sem("kidx_high"), sem("kidx_low")
        rows_zero, cum_high, cum_low = sem("rows_zero"), sem("cum_high"), sem("cum_low")
        qk_high = sem("qk_high")
        v_high, p_high = sem("v_high"), sem("p_high")
        kv_spilled, q_spilled = sem("kv_spilled"), sem("q_spilled")
        relu_used, score_done = sem("relu_used"), sem("score_done")
        bias_ready, sel_ready = sem("bias_ready"), sem("sel_ready")
        share_diff, share_exp, share_ready = sem("share_diff"), sem("share_exp"), sem("share_ready")
        z_tanh, z_mul, mixed = sem("z_tanh"), sem("z_mul"), sem("mixed")
        kv_in, qb_in = sem("kv_in"), [sem(f"qb_in{i}") for i in range(2)]
        m_high, m_low, o_full, o_free, res_ready = (sem(n) for n in ("m_high", "m_low", "o_full", "o_free", "res_ready"))
        o_ssq, o_var, o_root, out_ready, stored = (sem(n) for n in ("o_ssq", "o_var", "o_root", "out_ready", "stored"))
        act_chain, dve_chain = sem("act_chain"), sem("dve_chain")
        ended = {e: sem(f"ended_{e}") for e in ("pe", "act", "dve", "pool")}

        def full(eng, u):
            eng.wait_ge(bank_full[u[0]], u[1] + 1)

        def freed(eng, u):
            eng.wait_ge(bank_free[u[0]], u[1] + 1)

        def claim(pe, u):
            if u[1]:
                pe.wait_ge(bank_free[u[0]], u[1])

        def phase_end(eng, name, k):
            if name == "pool":
                eng.sem_inc(ended[name], 1)
            else:
                eng.drain().then_inc(ended[name], 1)
            if name != "pe":
                for other in ended:
                    if other != name:
                        eng.wait_ge(ended[other], k)

        def block_done(eng, n):
            if blocks[n]["last"]:
                full(eng, blocks[n]["done"])
            else:
                eng.wait_ge(w_used, sum(not b["last"] for b in blocks[:n + 1]))

        loads, arrived = [], [0] * RAW
        for n, b in enumerate(blocks):
            rows = slice(b.get("base", 0) * P, (b.get("base", 0) + b["nk"]) * P)
            kind, c = b["kind"], b["c"]

            def cols(w, col, width=P):
                return w[rows, col:col + width].rearrange("(k p) c -> p k c", p=P)
            if kind == "wo":
                src = [(None, w_o[0][c * P:(c + 1) * P, b["half"] * HALF:(b["half"] + 1) * HALF])]
            elif kind == "small":
                src = [(0, cols(w_in[0], COL["fa"], 32)), (32, cols(w_in[0], COL["widx"], 32)),
                       (64, cols(w_in[0], COL["kidx"], 32)), (96, cols(w_in[0], COL["kidx"], 32))]
            elif kind in ("wa", "wb", "wc"):
                src = [(0, cols({"wa": w_a, "wb": w_b, "wc": w_c}[kind][0], c * P))]
            else:
                src = [(0, cols(w_in[0], COL[kind] + (c if kind != "ckv" else 0) * P))]
            arrived[n % RAW] += 16 * len(src)
            loads.append((src, arrived[n % RAW]))

        def v_tokens(br, ch, t, b):
            g = ch // 2 if br == "c" else 0
            if g == 1:
                return t.rearrange("q (x r) -> q r x", r=4)[:, b // 2, (b % 2) * P:(b % 2 + 1) * P]
            return t[:, b * P:(b + 1) * P]

        def score_of(i):
            o = P * i * (i + 1) // 2
            return score[:, o:o + P * (i + 1)]

        def logit_bias(u):
            if u["br"] == "a":
                return negc[:, u["hh"], 0:u["W"]]
            if u["br"] == "b":
                return score_of(u["b"])
            return bmc[:, u["hh"], 0:P] if u["ch"] // 2 == 2 else bmc[:, u["hh"], 2 * P - u["W"]:2 * P]

        def stats_of(u):
            if u["br"] == "c":
                h4 = 2 * (u["ch"] % 2) + u["hh"]
                return stat[:, u["ch"] // 2, u["b"], 0, h4:h4 + 1], stat[:, u["ch"] // 2, u["b"], 1, h4:h4 + 1]
            k, h = u["unit"] % 8, 2 * u["ch"] + u["hh"]
            return nmax[:, k:k + 1], den[:, u["b"], h:h + 1]

        steps = {}
        for kind, a in plan:
            steps.setdefault(kind, []).append(a)
        last_low = {"w" + br: max(z["hs"] for z in steps["z_split"] if z["br"] == br) + 1 for br in "cab"}
        split_of = {(z["br"], z["c"], z["th"]): z["hs"] for z in steps["z_split"]}
        mix_base = {"a": 0, "b": 2 * KC}
        b_low = max(r["hs"] for r in steps["rms_norm"]) + 2
        last_S, last_pv, last_unit = {}, {}, {}
        for u in units:
            last_S[u["br"], u["ch"]] = u["S"]
            last_pv[u["br"], u["ch"]] = u["pv"]
            last_unit[u["br"], 2 * u["ch"] + u["hh"]] = u["unit"]
        units_c = [u for u in units if u["br"] == "c"]
        stat_uses = [a["use"] for a in steps["stat_turn"]]
        share_uses = {br: [a["use"] for a in steps["share_turn"] if a["br"] == br] for br in "cab"}
        shares = {"c": shareC, "a": rowsT, "b": rowsT}

        def turned_room(eng, grp):
            pts = PTS[info["unit_of_tp"][grp["tp"]]["br"]]
            if grp["tp"] >= pts:
                full(eng, info["unit_of_tp"][grp["tp"] - pts]["pv"])

        block = ctx.enter_context(nc.Block())

        @block.sync
        def _(sp):
            with nc.allow_non_contiguous_dma(reason="parameters, one value per partition"):
                sp.dma_start(gn[:], norm_g[0].rearrange("(k p) -> p k", p=P)).then_inc(consts_in, 16)
                sp.dma_start(gq[:, 0:2], g_cq[0].rearrange("(k p) -> p k", p=P)).then_inc(consts_in, 16)
                sp.dma_start(gq[:, 2:3], g_ckv[0].rearrange("(k p) -> p k", p=P)).then_inc(consts_in, 16)
                sp.dma_start(bf[:], b_forget[0].rearrange("(h o) -> h o", o=1)).then_inc(consts_in, 16)
            for i in range(TB):
                sp.dma_start(xn[:, i, :], x[0, i * P:(i + 1) * P, :]).then_inc(x_in[i], 16)
            sp.dma_start(uq_raw[:].rearrange("p k h d -> p k (h d)"),
                         w_uq[0].rearrange("(k p) n -> p k n", p=P)).then_inc(pw_in, 16)
            sp.dma_start(ix_raw[:].rearrange("p k h d -> p k (h d)"),
                         w_uq_idx[0].rearrange("(k p) n -> p k n", p=P)).then_inc(pw_in, 16)
            sp.dma_start(ukv_raw[:].rearrange("p a d -> p (a d)"), w_ukv[0]).then_inc(pw_in, 16)
            for n, (src, _) in enumerate(loads):
                if n >= RAW:
                    sp.wait_ge(w_low, n - RAW + 1)
                for col, ap in src:
                    if col is None:
                        dst = w_raw[:, n % RAW].rearrange("p k c -> p (k c)")
                    else:
                        dst = w_raw[:, n % RAW, 0:blocks[n]["nk"], col:col + ap.shape[2]]
                    sp.dma_start(dst, ap).then_inc(raw_in[n % RAW], 16)
            for b in range(TB):
                sp.wait_ge(out_ready, b + 1)
                sp.dma_start(out[0, b * P:(b + 1) * P, :], xo[b]).then_inc(stored, 16)
            sp.wait_ge(stored, 16 * TB)

        @block.gpsimd
        def _(pool):
            g = nc.gpsimd
            chain = [0]

            def then(ins):
                chain[0] += 1
                ins.then_inc(pool_consts, 1)
                pool.wait_ge(pool_consts, chain[0])

            then(g.memset(ident[:], 0.0))
            then(g.affine_select(ident[:], ident[:], [[-1, P]], ALU.not_equal, 1.0, base=0, channel_multiplier=1))
            then(g.memset(ident_b[:], 0.0))
            then(g.affine_select(ident_b[:], ident_b[:], [[-1, P]], ALU.not_equal, 1.0, base=0, channel_multiplier=1))
            then(g.memset(tri_b[:], 0.0))
            then(g.affine_select(tri_b[:], tri_b[:], [[-1, P]], ALU.is_ge, NEG, base=0, channel_multiplier=1))
            then(g.iota(band, [[1, 2 * P]], base=-P, channel_multiplier=-1, allow_small_or_imprecise_dtypes=True))
            then(g.affine_select(band, band, [[-1, 2 * P]], ALU.is_ge, NEG, base=P, channel_multiplier=1))
            then(g.affine_select(band, band, [[1, 2 * P]], ALU.is_ge, NEG, base=0, channel_multiplier=-1))
            then(g.memset(pairs, NEG))
            for a in range(2):
                sub = pairs[HD * a:HD * a + HD, HD * a:HD * a + HD]
                then(g.iota(sub, [[1, HD]], base=0, channel_multiplier=-1, allow_small_or_imprecise_dtypes=True))
                then(g.affine_select(sub, sub, [[-1, HD]], ALU.is_ge, NEG, base=0, channel_multiplier=1))
            for i in range(2):
                m = score_of(i)
                then(g.iota(m, [[1, P * (i + 1)]], base=-P * i, channel_multiplier=-1,
                            allow_small_or_imprecise_dtypes=True))
                then(g.affine_select(m, m, [[-1, P * (i + 1)]], ALU.is_ge, NEG, base=P * i, channel_multiplier=1))
            def load_first_sums(branches):
                for c in range(2):
                    pool.wait_ge(m_stored[c], 16 * (KC // 2) * branches)
                    pool.dma_start(ms[:, c, :], m_dram[c]).then_inc(m_loaded[c], 16)

            k = 0
            for kind, a in plan:
                if kind == "phase":
                    k += 1
                    if a["name"] == "c":
                        pool.wait_ge(kv_spilled, 32)
                        pool.wait_ge(q_spilled, 16 * B_HEADS)
                        for i in range(2, TB):
                            pool.wait_ge(score_done, i - 1)
                            m = score_of(i)[:, P * i:P * (i + 1)]
                            g.affine_select(m, m, [[-1, P]], ALU.is_ge, CAUSAL, base=0,
                                            channel_multiplier=1).then_inc(pool_causal, 1)
                    if k > 1:
                        phase_end(pool, "pool", k - 1)
                    if a["name"] == "c":
                        g.iota(srow[:], [[1, T]], base=0, channel_multiplier=-1,
                               allow_small_or_imprecise_dtypes=True).then_inc(pool_srow, 1)
                    if a["name"] == "b":
                        pool.dma_start(khb[:], kb_dram).then_inc(kv_in, 16)
                        pool.dma_start(V["b"][:], vb_dram[:, 0]).then_inc(kv_in, 16)
                        pool.dma_start(vb_low[:], vb_dram[:, 1]).then_inc(kv_in, 16)
                    if a["name"] == "b_merge":
                        load_first_sums(2)
                    if a["name"] == "o":
                        pool.dma_start(fg, final_g.rearrange("(o d) -> o d", o=1).to_broadcast([P, D])).then_inc(fg_in, 16)
                        for b in range(TB):
                            pool.dma_start(xo[b], x[0, b * P:(b + 1) * P, :]).then_inc(xo_in, 16)
                            pool.wait_ge(xo_in, 16 * (b + 1))
                elif kind == "rms_sum" and a["name"] == "cq":
                    pool.wait_ge(pw_high, 1)
                    for r in range(2):
                        ins = g.tensor_tensor(uq_hl[:, 1, :, :, r, :], uq_raw[:], uq_hl[:, 0, :, :, r, :].bitcast(F32),
                                          ALU.subtract)
                    ins.then_inc(pw_low, 1)
                    for r in range(4):
                        ins = g.tensor_tensor(ix_hl[:, 1, :, :, r, :], ix_raw[:], ix_hl[:, 0, :, :, r, :].bitcast(F32),
                                          ALU.subtract)
                    ins.then_inc(pw_low, 1)
                    for r, s in ((0, 0), (1, 0), (2, 1)):
                        ins = g.tensor_tensor(ukv_hl[:, 1, r, :], ukv_raw[:, s, :], ukv_hl[:, 0, r, :].bitcast(F32),
                                          ALU.subtract)
                    ins.then_inc(pw_low, 1)
                elif kind == "b_k":
                    pool.wait_ge(low_ready, a["hs"] + 2)
                    pool.dma_start(kb_dram, iq_st[:]).then_inc(kv_spilled, 16)
                elif kind == "b_v":
                    freed(pool, a["u"][0])
                    pool.dma_start(vb_dram, v_st[:]).then_inc(kv_spilled, 16)
                elif kind == "b_q" and a["th"]:
                    pool.wait_ge(low_ready, a["hs"] + 1)
                    pool.dma_start(qb_dram[a["h"]], bq_st[:]).then_inc(q_spilled, 16)
                elif kind == "logits" and a["br"] == "b" and a["b"] == 0:
                    for h in ([0, 1] if a["h"] == 0 else [a["h"] + 1] if a["h"] + 1 < B_HEADS else []):
                        if h >= 2:
                            pool.wait_ge(slot_full, a["S"])
                        pool.dma_start(qb[:, h % 2, :], qb_dram[h]).then_inc(qb_in[h % 2], 16)
                    if a["h"] == 0:
                        load_first_sums(1)
                elif kind == "w" and a["th"]:
                    br, c = a["br"], a["c"]
                    if br == "c":
                        for u in a["u"]:
                            freed(pool, u)
                    else:
                        pool.wait_ge(mixed, mix_base[br] + 2 * c + 2)
                    if br != "b":
                        pool.dma_start(m_dram[c], ms[:, c % 2, :]).then_inc(m_stored[c % 2], 16)
                    if br != "c" and c + 2 < KC:
                        if br == "a":
                            pool.wait_ge(m_stored[c % 2], 16 * (KC // 2 + c // 2 + 1))
                        pool.dma_start(ms[:, c % 2, :], m_dram[c + 2]).then_inc(m_loaded[c % 2], 16)

        @block.tensor
        def _(pe):
            def split_product(out_, wh, wl, mh, ml, start, stop):
                pe.matmul(out_, wh, mh, start=start, stop=False)
                pe.matmul(out_, wh, ml, start=False, stop=False)
                return pe.matmul(out_, wl, mh, start=False, stop=stop)

            k = 0
            for kind, a in plan:
                if kind == "phase":
                    k += 1
                    if k > 1:
                        phase_end(pe, "pe", k - 1)
                elif kind == "x_turn":
                    if a["kc"] == 0:
                        pe.wait_ge(x_scaled, 4 * a["th"] + 4)
                        pe.wait_ge(pool_consts, 2)
                    claim(pe, a["use"])
                    for j in range(4):
                        ins = pe.transpose(bank[a["use"][0]][:, j * P:(j + 1) * P],
                                           xn[:, 4 * a["th"] + j, a["kc"] * P:(a["kc"] + 1) * P], ident[:])
                    ins.then_inc(bank_full[a["use"][0]], 1)
                elif kind == "block":
                    n, b, th = a["n"], blocks[a["n"]], a["th"]
                    pe.wait_ge(w_low, n + 1)
                    if a["first"]:
                        if a["src"] == "h":
                            pe.wait_ge(low_ready, 2 * KC)
                        elif b["c"] == 0:
                            pe.wait_ge(low_ready, last_low[b["kind"]])
                        claim(pe, a["u"])
                    br, w = b["kind"][1], w_hl[:, n % SPL]
                    ts = slice(th * HALF, (th + 1) * HALF)
                    for kk in range(a["nk"]):
                        c = a["base"] + kk
                        mh, ml = ((hs[:, 0, c, ts], hs[:, 1, c, ts]) if a["src"] == "h" else
                                  (YH[br][:, c, ts], YL[br][:, c, ts]))
                        ins = split_product(bank[th][:], w[:, 0, kk, :], w[:, 1, kk, :], mh, ml,
                                            a["first"] and kk == 0, a["last"] and kk == a["nk"] - 1)
                    if a["last"]:
                        ins.then_inc(bank_full[th], 1)
                    elif th == 1:
                        ins.then_inc(w_used, 1)
                elif kind == "rms_sum":
                    pe.wait_ge(rms_sq, 1 if a["name"] == "cq" else 2)
                    pe.wait_ge(ones_ready, 1)
                    for th, u in enumerate(a["u"]):
                        claim(pe, u)
                        for c in range(a["n"]):
                            ins = pe.matmul(bank[u[0]][:], ones[:], c_tmp[:, c, th * HALF:(th + 1) * HALF],
                                            start=c == 0, stop=c == a["n"] - 1)
                        ins.then_inc(bank_full[u[0]], 1)
                elif kind == "natural":
                    for u in tiles["small", 0]:
                        freed(pe, u)
                    for half, u in enumerate(a["u"]):
                        claim(pe, u)
                        for j in range(4):
                            i = 4 * half + j
                            ins = pe.transpose(bank[u[0]][:, j * P:(j + 1) * P], small[:, i * P:(i + 1) * P], ident[:])
                        ins.then_inc(bank_full[u[0]], 1)
                elif kind == "b_k":
                    pe.wait_ge(pw_low, 3)
                    pe.wait_ge(low_ready, b_low)
                    for th, u in enumerate(a["u"]):
                        claim(pe, u)
                        ts = slice(th * HALF, (th + 1) * HALF)
                        split_product(bank[u[0]][:], ukv_hl[:, 0, 0:2, :], ukv_hl[:, 1, 0:2, :], ckv_hl[:, 0, ts],
                                      ckv_hl[:, 1, ts], True, True).then_inc(bank_full[u[0]], 1)
                elif kind == "b_v":
                    u = a["u"][0]
                    claim(pe, u)
                    for b in range(TB):
                        tk = slice(b * P, (b + 1) * P)
                        ins = split_product(bank[u[0]][:, b * HD:(b + 1) * HD], ckv_hl[:, 0, tk], ckv_hl[:, 1, tk],
                                            ukv_hl[:, 0, 2, :], ukv_hl[:, 1, 2, :], True, True)
                    ins.then_inc(bank_full[u[0]], 1)
                elif kind in ("b_q", "i_q"):
                    w, u, th = (uq_hl if kind == "b_q" else ix_hl), a["u"], a["th"]
                    claim(pe, u)
                    ts = slice(th * HALF, (th + 1) * HALF)
                    for c in range(2):
                        ins = split_product(bank[u[0]][:], w[:, 0, c, a["h"]], w[:, 1, c, a["h"]],
                                            cq_hl[:, 0, c, ts], cq_hl[:, 1, c, ts], c == 0, c == 1)
                    ins.then_inc(bank_full[u[0]], 1)
                elif kind == "i_dots":
                    if a["i"] == 2:
                        pe.wait_ge(low_ready, a["low"])
                        pe.wait_ge(kidx_low, 1)
                    if a["S"] >= 2:
                        pe.wait_ge(slot_free, a["S"] - 1)
                    W = (a["i"] + 1) * P
                    for c0 in range(0, W, HALF):
                        c1 = min(W, c0 + HALF)
                        ins = pe.matmul(slot[a["S"] % 2][:, c0:c1], iq_st[:, a["h"] % 2, a["i"] * P:(a["i"] + 1) * P],
                                        kidx_hl[:, c0:c1], start=True, stop=True)
                    ins.then_inc(slot_full, 1)
                elif kind == "v_turn":
                    br = a["br"]
                    for u in tiles["v" + br, a["ch"]]:
                        freed(pe, u)
                    claim(pe, a["use"])
                    for j in range(4):
                        ins = pe.transpose(bank[a["use"][0]][:, j * P:(j + 1) * P],
                                           v_tokens(br, a["ch"], VT[br][:], 4 * a["half"] + j), ident[:])
                    ins.then_inc(bank_full[a["use"][0]], 1)
                elif kind == "c_bcast":
                    pe.wait_ge(cum_low, 1)
                    pe.wait_ge(sel_ready, 3)
                    for th, u in enumerate(a["u"]):
                        claim(pe, u)
                        pe.matmul(bank[u[0]][:], selA[:, a["h"], :], rowsT[:, th * HALF:(th + 1) * HALF],
                                  start=True, stop=True).then_inc(bank_full[u[0]], 1)
                elif kind == "logits":
                    br, W = a["br"], a["W"]
                    if br != "b" and a["b"] == 0 and a["hh"] == 0:
                        for w in "qk":
                            for u in tiles[w + br, a["ch"]]:
                                freed(pe, u)
                    if br == "b" and a["b"] == 0:
                        pe.wait_ge(kv_in, 48)
                        pe.wait_ge(qb_in[a["h"] % 2], 16 * (a["h"] // 2 + 1))
                    if a["S"] >= 2:
                        pe.wait_ge(slot_free, a["S"] - 1)
                    o = slot[a["S"] % 2]
                    if br == "b":
                        q = qb[:, a["h"] % 2, a["b"] * P:(a["b"] + 1) * P]
                        for c0 in range(0, W, HALF):
                            c1 = min(W, c0 + HALF)
                            pe.matmul(o[:, c0:c1], q, khb[:, 0, c0:c1], start=True, stop=False)
                            ins = pe.matmul(o[:, c0:c1], q, khb[:, 1, c0:c1], start=False, stop=True)
                    else:
                        rows = slice(HD * a["hh"], HD * a["hh"] + HD)
                        qt, kt = Q[br][a["ch"] % 2], K[br][a["ch"] % 2]
                        if br == "c":
                            q = v_tokens(br, a["ch"], qt[rows, :], a["b"])
                        g = a["ch"] // 2 if br == "c" else 0
                        if br == "c" and g == 0:
                            keys = kt[rows, (a["b"] + 1) * P - W:(a["b"] + 1) * P]
                        elif g == 1:
                            keys = kt[rows, :].rearrange("q (x r) -> q r x", r=4)[:, a["b"] // 2, 0:W]
                        elif g == 2:
                            keys = v_tokens(br, a["ch"], kt[rows, :], a["b"])
                        if br == "c":
                            ins = pe.matmul(o[:, 0:W], q, keys, start=True, stop=True)
                        else:
                            for c0 in range(0, W, HALF):
                                c1 = min(W, c0 + HALF)
                                tq = slice(a["b"] * P, (a["b"] + 1) * P)
                                split_product(o[:, c0:c1], qt[rows, 0, tq], qt[rows, 1, tq], kt[rows, 0, c0:c1],
                                              kt[rows, 1, c0:c1], True, c1 < W)
                            ins = pe.matmul(o[:, W - P:W], ident_b[:], tri_b[:], start=False, stop=True)
                    ins.then_inc(slot_full, 1)
                elif kind == "turn":
                    pe.wait_ge(slot_free, a["S"] + 1)
                    pr = PR[a["br"]][:, a["unit"] % 2]
                    for grp in a["groups"]:
                        claim(pe, grp["use"])
                        for j in range(grp["nc"]):
                            c = grp["c0"] + j
                            ins = pe.transpose(bank[grp["use"][0]][:, j * P:(j + 1) * P], pr[:, c * P:(c + 1) * P], ident[:])
                        ins.then_inc(bank_full[grp["use"][0]], 1)
                elif kind == "pv":
                    for grp in a["groups"]:
                        freed(pe, grp["use"])
                    if a["br"] != "b":
                        freed(pe, tiles["V" + a["br"], a["ch"], 1])
                    claim(pe, a["pv"])
                    n = a["W"] // P
                    first = a["b"] + 1 - n
                    if a["br"] == "c" and a["ch"] // 2 == 1:
                        first = a["b"] // 2 * 2
                    for grp in a["groups"]:
                        for j in range(grp["nc"]):
                            c = grp["c0"] + j
                            o, pt = bank[a["pv"][0]][0:HD, 0:P], PT[a["br"]][:, grp["tp"] % PTS[a["br"]]]
                            if a["br"] == "b":
                                ins = split_product(o, V["b"][:, c, :], vb_low[:, c, :], pt[:, 0, j, :], pt[:, 1, j, :],
                                                    c == 0, c == n - 1)
                            else:
                                v = V[a["br"]][a["ch"] % 2][:, first + c, HD * a["hh"]:HD * a["hh"] + HD]
                                ins = pe.matmul(o, v, pt[:, j, :], start=c == 0, stop=c == n - 1)
                    ins.then_inc(bank_full[a["pv"][0]], 1)
                elif kind == "stat_turn":
                    claim(pe, a["use"])
                    if a["g"] == 0 and a["half"] == 0:
                        pe.wait_ge(slot_free, units_c[-1]["S"] + 1)
                    for j in range(4):
                        b = 4 * a["half"] + j
                        ins = pe.transpose(bank[a["use"][0]][0:8, j * P:(j + 1) * P],
                                           stat[:, a["g"], b].rearrange("p a h -> p (a h)"), ident[:])
                    ins.then_inc(bank_full[a["use"][0]], 1)
                elif kind == "stat_back":
                    for u in stat_uses:
                        freed(pe, u)
                    claim(pe, a["use"])
                    for i in range(TB):
                        for g in range(3):
                            o = (i * 3 + g) * 8
                            ins = pe.transpose(bank[a["use"][0]][:, o:o + 8], statT[:, g, i * P:(i + 1) * P], ident[0:8, 0:8])
                    ins.then_inc(bank_full[a["use"][0]], 1)
                elif kind == "share_turn":
                    n = C_HEADS if a["br"] == "c" else A_HEADS
                    pe.wait_ge(share_ready, 1 + "cab".index(a["br"]))
                    claim(pe, a["use"])
                    for j in range(4):
                        i = 4 * a["half"] + j
                        src = (shareN[:, i].rearrange("p g h -> p (g h)") if a["br"] == "c" else
                               den[:, i, :])
                        ins = pe.transpose(bank[a["use"][0]][0:n, j * P:(j + 1) * P], src, ident[:])
                    ins.then_inc(bank_full[a["use"][0]], 1)
                elif kind == "share":
                    z = a["br"]
                    for u in share_uses[z]:
                        freed(pe, u)
                    pe.wait_ge(sel_ready, 2 if z == "c" else 1)
                    u, th, s = a["u"], a["th"], (selC if z == "c" else sel)
                    claim(pe, u)
                    pe.matmul(bank[u[0]][:], s[:, 2 * a["c"]:2 * a["c"] + 2, :].rearrange("p h d -> p (h d)"),
                              shares[z][:, th * HALF:(th + 1) * HALF], start=True, stop=True).then_inc(bank_full[u[0]], 1)
                elif kind == "final":
                    for b in range(4):
                        pe.wait_ge(bank_free[b], a["uses"][b])
                    pe.wait_ge(slot_free, a["S"])
                    for half in range(2):
                        if half == 0:
                            order = [(cc, tb) for cc in range(KC) for tb in range(TB)]
                        else:
                            order = [(cc, tb) for tb in range(TB) for cc in range(KC)]
                        for cc, tb in order:
                            if half == 0 and tb == 0:
                                pe.wait_ge(m_low, cc + 1)
                                pe.wait_ge(w_low, a["first"] + cc + 1)
                            if half == 1 and cc == 0:
                                pe.wait_ge(o_free, tb + 1)
                                if tb == 0:
                                    pe.wait_ge(w_low, a["first"] + 2 * KC)
                            tk = slice(tb * P, (tb + 1) * P)
                            w = wo_hl[half]
                            ins = split_product(banks8[tb], hs[:, 0, cc, tk], hs[:, 1, cc, tk], w[:, 0, cc, :], w[:, 1, cc, :],
                                                cc == 0, cc == KC - 1)
                            if cc == KC - 1:
                                ins.then_inc(o_full, 1)

        @block.scalar
        def _(act):
            A = nc.scalar.activation
            chain = [0]
            done = [0]

            def then(ins):
                chain[0] += 1
                ins.then_inc(act_chain, 1)
                act.wait_ge(act_chain, chain[0])

            def split_high(upto):
                while done[0] < min(upto, len(blocks)):
                    n = done[0]
                    b = blocks[n]
                    done[0] += 1
                    act.wait_ge(raw_in[n % RAW], loads[n][1])
                    if b["kind"] == "wo":
                        dst = wo_hl[b["half"]][:, 0, b["c"], :]
                        src = w_raw[:, n % RAW].rearrange("p k c -> p (k c)")
                    else:
                        if n >= SPL:
                            block_done(act, n - SPL)
                        dst, src = w_hl[:, n % SPL, 0, 0:b["nk"], :], w_raw[:, n % RAW, 0:b["nk"], :]
                    A(dst, src, ACTF.Copy).then_inc(w_high, 1)

            k = 0
            for kind, a in plan:
                if kind == "phase":
                    k += 1
                    if k > 1:
                        phase_end(act, "act", k - 1)
                    if a["name"] == "x":
                        for th in range(2):
                            for i in range(4 * th, 4 * th + 4):
                                act.wait_ge(x_in[i], 16)
                                then(A(junk[:], xn[:, i, :], ACTF.Square, accum_out=ssq[:, i:i + 1]))
                            act.sem_inc(ssq_ready, 1)
                            act.wait_ge(var_ready, th + 1)
                            hb = slice(4 * th, 4 * th + 4)
                            A(rstd[:, 1, hb], rstd[:, 0, hb], ACTF.Sqrt).then_inc(root_ready, 1)
                        split_high(SPL)
                elif kind == "x_turn":
                    full(act, a["use"])
                    A(hs[:, 0, a["kc"], a["th"] * HALF:(a["th"] + 1) * HALF], bank[a["use"][0]][:], ACTF.Copy,
                      scale=gn[:, a["kc"]:a["kc"] + 1]).then_inc(high_ready, 1)
                elif kind == "block":
                    if a["th"] == 0:
                        split_high(min(a["n"] + SPL, info["first_wo"]))
                elif kind in ("cq", "ckv", "small"):
                    th = a["th"]
                    full(act, a["u"][th])
                    dst = small[:] if kind == "small" else c_raw[a["c"]][:]
                    A(dst[:, th * HALF:(th + 1) * HALF], bank[th][:], ACTF.Copy).then_inc(bank_free[th], 1)
                elif kind == "rms_sum":
                    for c in range(a["n"]):
                        ch = a["first_chunk"] + c
                        for u in tiles["cq" if ch < 2 else "ckv", ch]:
                            freed(act, u)
                        if a["name"] == "ckv" and c == 0:
                            act.wait_ge(rms_y, 2)
                        ins = A(c_tmp[:, c, :], c_raw[ch][:], ACTF.Square)
                    ins.then_inc(rms_sq, 1)
                    for th in range(2):
                        kk = 2 * (a["name"] == "ckv") + th
                        act.wait_ge(rms_var, kk + 1)
                        v = c_tmp[:, 0, th * HALF:(th + 1) * HALF]
                        A(v, v, ACTF.Sqrt).then_inc(rms_root, 1)
                    if a["name"] == "cq":
                        act.wait_ge(pw_in, 48)
                        for r in range(2):
                            A(uq_hl[:, 0, :, :, r, :], uq_raw[:], ACTF.Copy)
                        for r in range(4):
                            ins = A(ix_hl[:, 0, :, :, r, :], ix_raw[:], ACTF.Copy)
                        for r, s in ((0, 0), (1, 0), (2, 1)):
                            ins = A(ukv_hl[:, 0, r, :], ukv_raw[:, s, :], ACTF.Copy)
                        ins.then_inc(pw_high, 1)
                elif kind == "rms_norm":
                    for c in range(a["n"]):
                        ch = a["first_chunk"] + c
                        act.wait_ge(rms_y, ch + 1)
                        dst = ckv_hl[:, 0, :] if ch == 2 else cq_hl[:, 0, ch, :]
                        for th in range(2):
                            ts = slice(th * HALF, (th + 1) * HALF)
                            A(dst[:, ts], c_raw[ch][:, ts], ACTF.Copy).then_inc(high_ready, 1)
                elif kind == "forget":
                    act.wait_ge(rms_y, 3)
                    act.wait_ge(consts_in, 64)
                    for u in tiles["small", 0]:
                        freed(act, u)
                    e = c_tmp[0:A_HEADS, 0, :]
                    then(A(e, small[0:A_HEADS, :], ACTF.Abs, bias=bf[:]))
                    then(A(e, e, ACTF.Exp, scale=-1.0))
                    A(e, e, ACTF.Ln, bias=1.0).then_inc(forget_log, 1)
                    act.wait_ge(cum_ready, 1)
                    act.wait_ge(rows_zero, 1)
                    A(rowsT[0:A_HEADS, :], c_raw[0][0:A_HEADS, :], ACTF.Copy).then_inc(cum_high, 1)
                    A(kidx_hl[0:32, :], small[64:96, :], ACTF.Copy)
                    A(kidx_hl[32:64, :], small[64:96, :], ACTF.Copy)
                    A(kidx_hl[64:128, :], small[64:128, :], ACTF.Copy).then_inc(kidx_high, 1)
                elif kind == "b_k":
                    for th, u in enumerate(a["u"]):
                        full(act, u)
                        A(iq_st[:, 0, th * HALF:(th + 1) * HALF], bank[u[0]][:], ACTF.Copy).then_inc(high_ready, 1)
                elif kind == "b_v":
                    u = a["u"][0]
                    full(act, u)
                    A(v_st[:, 0].rearrange("p b d -> p (b d)"), bank[u[0]][:], ACTF.Copy).then_inc(v_high, 1)
                elif kind in ("b_q", "i_q"):
                    h = a["h"]
                    th, u = a["th"], a["u"]
                    if kind == "b_q":
                        if h and th == 0:
                            act.wait_ge(q_spilled, 16 * h)
                        dst, scale = bq_st[:], SCALE * 2.0 ** (h + 1)
                    else:
                        if h < 2:
                            act.wait_ge(kv_spilled, 32)
                        else:
                            act.wait_ge(slot_full, 6 * (h - 1))
                        dst, scale = iq_st[:, h % 2, :], 1.0
                    full(act, u)
                    A(dst[:, th * HALF:(th + 1) * HALF], bank[u[0]][:], ACTF.Copy, scale=scale).then_inc(high_ready, 1)
                elif kind == "i_dots":
                    act.wait_ge(slot_full, a["S"] + 1)
                    if a["n"] >= 2:
                        act.wait_ge(relu_used, a["n"] - 1)
                    W = (a["i"] + 1) * P
                    A(relu_t[:, a["n"] % 2, 0:W], slot[a["S"] % 2][:, 0:W], ACTF.Relu).then_inc(slot_free, 1)
                elif kind in ("qc", "qa", "kc", "ka", "vc", "va"):
                    br, what, th = kind[1], kind[0], a["th"]
                    dst = {"q": Q, "k": K}[what][br][a["c"] % 2] if what != "v" else VT[br]
                    if what == "v" and a["c"] and th == 0:
                        full(act, tiles["V" + br, a["c"] - 1, 1])
                    elif what != "v" and a["c"] >= 2 and th == 0:
                        act.wait_ge(slot_full, last_S[br, a["c"] - 2] + 1)
                    full(act, a["u"][th])
                    if kind in ("qa", "ka"):
                        if kind == "ka" and a["c"] == 1 and th == 0:
                            for s in range(2):
                                act.wait_ge(m_stored[s], 16 * (KC // 2))
                        A(dst[:, 0, th * HALF:(th + 1) * HALF], bank[th][:], ACTF.Copy,
                          scale=SCALE if what == "q" else 1.0).then_inc(qk_high, 1)
                        continue
                    d, src = dst[:, th * HALF:(th + 1) * HALF], bank[th][:]
                    if br == "c" and a["c"] // 2 == 2:
                        d = dst[:].rearrange("p (c u) -> p u c", c=16)[:, 32 * th:32 * th + 32, :]
                        src = src.rearrange("p (u c) -> p u c", c=16)
                    A(d, src, ACTF.Copy, scale=SCALE if what == "q" else 1.0).then_inc(bank_free[th], 1)
                elif kind == "v_turn":
                    br = a["br"]
                    if a["ch"] >= 2 and a["half"] == 0:
                        full(act, last_pv[br, a["ch"] - 2])
                    full(act, a["use"])
                    A(V[br][a["ch"] % 2][:, 4 * a["half"]:4 * a["half"] + 4, :].rearrange("p b c -> p (b c)"), bank[a["use"][0]][:],
                      ACTF.Copy).then_inc(bank_free[a["use"][0]], 1)
                elif kind == "c_bcast":
                    if a["h"] >= 2:
                        act.wait_ge(logit_ready, last_unit["a", a["h"] - 2] + 1)
                    for th, u in enumerate(a["u"]):
                        full(act, u)
                        A(negc[:, a["h"] % 2, th * HALF:(th + 1) * HALF], bank[u[0]][:], ACTF.Copy,
                          scale=-1.0).then_inc(bank_free[u[0]], 1)
                elif kind == "logits":
                    if a["br"] == "c" and a["b"] == 0:
                        h, g = 2 * a["ch"] + a["hh"], a["ch"] // 2
                        if h >= 2:
                            act.wait_ge(logit_ready, last_unit["c", h - 2] + 1)
                        m = band if g < 2 else pairs
                        if h == 0:
                            act.wait_ge(pool_consts, 14)
                        A(bmc[:, a["hh"], 0:m.shape[1]], m, ACTF.Copy,
                          scale=float(np.float32(c_slope(h)) * np.float32(C_GROUPS[g][1]))).then_inc(bias_ready, 1)
                elif kind == "exp":
                    act.wait_ge(logit_ready, a["unit"] + 1)
                    if a["unit"] >= 2:
                        full(act, units[a["unit"] - 2]["groups"][-1]["use"])
                    mx, dn = stats_of(a)
                    A(PR[a["br"]][:, a["unit"] % 2, 0:a["W"]], slot[a["S"] % 2][:, 0:a["W"]], ACTF.Exp, bias=mx,
                      scale=-1.0, accum_out=dn).then_inc(slot_free, 1)
                elif kind == "turn":
                    for grp in a["groups"]:
                        b, n = grp["use"][0], grp["nc"]
                        full(act, grp["use"])
                        turned_room(act, grp)
                        if a["br"] == "b":
                            A(PT["b"][:, grp["tp"] % 2, 0, 0:n, :].rearrange("p c q -> p (c q)"), bank[b][:, 0:n * P],
                              ACTF.Copy).then_inc(p_high, 1)
                        else:
                            A(PT[a["br"]][:, grp["tp"] % 4, 0:n, :].rearrange("p c q -> p (c q)"), bank[b][:, 0:n * P],
                              ACTF.Copy).then_inc(bank_free[b], 1)
                elif kind == "pv":
                    br, ch, b = a["br"], a["ch"], a["b"]
                    full(act, a["pv"])
                    y = Y[br][HD * a["hh"]:HD * a["hh"] + HD, ch, :]
                    src = bank[a["pv"][0]][0:HD, 0:P]
                    if br == "c" and ch // 2 == 2:
                        y = y.rearrange("q (u c) -> q c u", c=16)[:, 2 * b:2 * b + 2, :]
                        src = src.rearrange("q (c u) -> q c u", c=2)
                    else:
                        y = v_tokens(br, ch, y, b)
                    A(y, src, ACTF.Copy).then_inc(bank_free[a["pv"][0]], 1)
                elif kind == "stat_turn":
                    full(act, a["use"])
                    g, half = a["g"], a["half"]
                    y, src = statT[:, g, :], bank[a["use"][0]][0:8, :]
                    if g == 0:
                        y = y[:, half * HALF:(half + 1) * HALF]
                    elif g == 1:
                        y = y.rearrange("q (x r) -> q r x", r=4)[:, 2 * half:2 * half + 2, :]
                        src = src.rearrange("q (r x) -> q r x", r=2)
                    else:
                        y = y.rearrange("q (u c) -> q c u", c=16)[:, 8 * half:8 * half + 8, :]
                        src = src.rearrange("q (c u) -> q c u", c=8)
                    A(y, src, ACTF.Copy).then_inc(bank_free[a["use"][0]], 1)
                elif kind == "stat_back":
                    full(act, a["use"])
                    A(natS[:].rearrange("p i g a h -> p (i g a h)"), bank[a["use"][0]][:, 0:TB * 24],
                      ACTF.Copy).then_inc(bank_free[a["use"][0]], 1)
                    act.wait_ge(share_diff, 1)
                    A(eS[:], eS[:], ACTF.Exp).then_inc(share_exp, 1)
                elif kind == "share_turn":
                    full(act, a["use"])
                    act.wait_ge(rows_zero, 2 if a["br"] == "c" else 1)
                    n = C_HEADS if a["br"] == "c" else A_HEADS
                    A(shares[a["br"]][0:n, a["half"] * HALF:(a["half"] + 1) * HALF], bank[a["use"][0]][0:n, :],
                      ACTF.Copy).then_inc(high_ready, 1)
                elif kind == "z":
                    br, c, th = a["br"], a["c"], a["th"]
                    full(act, a["u"][th])
                    if c:
                        act.wait_ge(low_ready, split_of[br, c - 1, th] + 1)
                    A(tm[:, 2 * th, :], bank[th][:], ACTF.Tanh, scale=0.5).then_inc(z_tanh, 1)
                elif kind == "z_split":
                    th = a["th"]
                    act.wait_ge(z_mul, a["zn"] + 1)
                    A(YH[a["br"]][:, a["c"], th * HALF:(th + 1) * HALF], tm[:, 2 * th + 1, :], ACTF.Copy).then_inc(high_ready, 1)
                elif kind == "g":
                    br, c, th = a["br"], a["c"], a["th"]
                    full(act, a["u"][th])
                    if c < 2:
                        act.wait_ge(low_ready, last_low["w" + br])
                    elif br == "c":
                        freed(act, tiles["w" + br, c - 2][th])
                    else:
                        act.wait_ge(mixed, mix_base[br] + 2 * (c - 2) + th + 1)
                    A(tm[:, 2 * (c % 2) + th, :], bank[th][:], ACTF.Tanh, scale=0.5).then_inc(bank_free[th], 1)
                elif kind == "m_split":
                    for u in tiles["gb", KC - 1]:
                        full(act, u)
                    for cc in a["chunks"]:
                        act.wait_ge(mixed, mix_base["b"] + 2 * cc + 2)
                        A(hs[:, 0, cc, :], mT[:, cc, :], ACTF.Copy, scale=0.25).then_inc(m_high, 1)
                elif kind == "final":
                    for cc in range(KC):
                        if cc >= KC - 2:
                            A(hs[:, 0, cc, :], mT[:, cc, :], ACTF.Copy, scale=0.25).then_inc(m_high, 1)
                        split_high(a["first"] + cc + 1)
                    act.wait_ge(m_low, KC)
                    split_high(a["first"] + 2 * KC)
                    for b in range(TB):
                        act.wait_ge(res_ready, b + 1)
                        A(junk_o, xo[b], ACTF.Square, accum_out=ssq[:, b:b + 1]).then_inc(o_ssq, 1)
                        act.wait_ge(o_var, b + 1)
                        A(rstd[:, 1, b:b + 1], rstd[:, 0, b:b + 1], ACTF.Sqrt).then_inc(o_root, 1)

        @block.vector
        def _(dve):
            v = nc.vector
            chain = [0]
            done = [0]

            def then(ins):
                chain[0] += 1
                ins.then_inc(dve_chain, 1)
                dve.wait_ge(dve_chain, chain[0])

            def split_low(upto):
                while done[0] < min(upto, len(blocks)):
                    n = done[0]
                    b = blocks[n]
                    done[0] += 1
                    dve.wait_ge(w_high, n + 1)
                    if b["kind"] == "wo":
                        hi, lo = wo_hl[b["half"]][:, 0, b["c"], :], wo_hl[b["half"]][:, 1, b["c"], :]
                        src = w_raw[:, n % RAW].rearrange("p k c -> p (k c)")
                    else:
                        hi, lo = w_hl[:, n % SPL, 0, 0:b["nk"], :], w_hl[:, n % SPL, 1, 0:b["nk"], :]
                        src = w_raw[:, n % RAW, 0:b["nk"], :]
                    v.tensor_tensor(lo, src, hi.bitcast(F32), ALU.subtract).then_inc(w_low, 1)

            rounds = [(i, r) for i in range(2, TB) for r in range(ROUNDS)]
            credit, at_round = [0.0], [0]

            def select(us):
                credit[0] += us
                while at_round[0] < len(rounds):
                    i, r = rounds[at_round[0]]
                    cost = 2 * P * (i + 1) / 960 + 0.2
                    if credit[0] < cost:
                        return
                    credit[0] -= cost
                    at_round[0] += 1
                    if r == 0:
                        dve.wait_ge(pool_causal, i - 1)
                    then(v.max(top8[:], score_of(i)))
                    then(v.match_replace(score_of(i), top8[:], score_of(i), TAKEN))
                    if r == ROUNDS - 1:
                        then(v.tensor_scalar(score_of(i), score_of(i), 0.66 * TAKEN, NEG, ALU.is_ge, ALU.mult))
                        dve.wait_ge(pool_srow, 1)
                        then(v.scalar_tensor_tensor(score_of(i), score_of(i), float(-P * i), srow[:, 0:P * (i + 1)],
                                                    ALU.add, ALU.add))

            def low_of(dst, src, hi):
                v.tensor_tensor(dst, src, hi.bitcast(F32), ALU.subtract).then_inc(low_ready, 1)

            def zero_rows(rows):
                v.tensor_scalar(rows[:].rearrange("p (i t) -> p i t", t=P), ident[0:ROWS, :].unsqueeze(1).to_broadcast(
                    [ROWS, TB, P]), 0.0, None, ALU.mult).then_inc(rows_zero, 1)

            def spread(to, heads):
                d = to.shape[2]
                then(v.tensor_copy(to[:], ident[0:ROWS, 0:heads].unsqueeze(2).to_broadcast([ROWS, heads, d])))
                v.tensor_copy(to[LOW:LOW + heads], ident[LOW:LOW + heads, LOW:LOW + heads].unsqueeze(2).to_broadcast(
                    [heads, heads, d])).then_inc(sel_ready, 1)

            def m_split_low(cc):
                dve.wait_ge(m_high, cc + 1)
                v.scalar_tensor_tensor(hs[:, 1, cc, :], mT[:, cc, :], 0.25, hs[:, 0, cc, :].bitcast(F32), ALU.mult,
                                       ALU.subtract).then_inc(m_low, 1)

            rate = (0.0, 0.0)
            k = 0
            for kind, a in plan:
                if kind == "phase":
                    k += 1
                    if a["name"] == "b":
                        select(1e9)
                    if k > 1:
                        phase_end(dve, "dve", k - 1)
                    if a["name"] == "x":
                        v.memset(ones[:], 1.0).then_inc(ones_ready, 1)
                        dve.wait_ge(pool_consts, 2)
                        zero_rows(rowsT)
                        spread(sel, A_HEADS)
                        for th in range(2):
                            hb = slice(4 * th, 4 * th + 4)
                            dve.wait_ge(ssq_ready, th + 1)
                            v.tensor_scalar(rstd[:, 0, hb], ssq[:, hb], 1.0 / D, EPS, ALU.mult, ALU.add).then_inc(var_ready, 1)
                            dve.wait_ge(root_ready, th + 1)
                            then(v.reciprocal(rstd[:, 2, hb], rstd[:, 1, hb]))
                            for i in range(4 * th, 4 * th + 4):
                                v.tensor_scalar(xn[:, i, :], xn[:, i, :], rstd[:, 2, i:i + 1], None,
                                                ALU.mult).then_inc(x_scaled, 1)
                        dve.wait_ge(consts_in, 64)
                    rate = SELECT_US.get(a["name"], (0.0, 0.0))
                    if a["name"] == "a":
                        spread(selA, A_HEADS)
                    if a["name"] == "c_stats":
                        zero_rows(shareC)
                        spread(selC, C_HEADS)
                    if a["name"] == "b":
                        dve.wait_ge(pool_consts, 18)
                elif kind == "x_turn":
                    dve.wait_ge(high_ready, a["hs"] + 1)
                    ts = slice(a["th"] * HALF, (a["th"] + 1) * HALF)
                    b = a["use"][0]
                    v.scalar_tensor_tensor(hs[:, 1, a["kc"], ts], bank[b][:], gn[:, a["kc"]:a["kc"] + 1],
                                           hs[:, 0, a["kc"], ts].bitcast(F32), ALU.mult,
                                           ALU.subtract).then_inc(bank_free[b], 1)
                    if a["hs"] == 2 * KC - 1:
                        for x_turn in steps["x_turn"]:
                            freed(dve, x_turn["use"])
                        dve.sem_inc(low_ready, 2 * KC)
                elif kind == "block":
                    if a["th"] == 0:
                        split_low(min(a["n"] + SPL, info["first_wo"]))
                    select(rate[0])
                elif kind == "rms_sum":
                    width = P * a["n"]
                    for th, u in enumerate(a["u"]):
                        full(dve, u)
                        v.tensor_scalar(c_tmp[:, 0, th * HALF:(th + 1) * HALF], bank[u[0]][:], 1.0 / width, EPS, ALU.mult,
                                        ALU.add).then_inc(rms_var, 1)
                    n0 = 2 * (a["name"] == "ckv")
                    dve.wait_ge(rms_root, n0 + 2)
                    then(v.reciprocal(c_tmp[:, 0, :], c_tmp[:, 0, :]))
                    for th, u in enumerate(a["u"]):
                        dve.wait_ge(rms_var, n0 + th + 1)
                        dve.sem_inc(bank_free[u[0]], 1)
                elif kind == "rms_norm":
                    for c in range(a["n"]):
                        ch = a["first_chunk"] + c
                        v.scalar_tensor_tensor(c_raw[ch][:], c_raw[ch][:], gq[:, ch:ch + 1], c_tmp[:, 0, :], ALU.mult,
                                               ALU.mult).then_inc(rms_y, 1)
                    dve.wait_ge(rms_y, a["first_chunk"] + a["n"])
                    for c in range(a["n"]):
                        ch = a["first_chunk"] + c
                        hl = ckv_hl if ch == 2 else cq_hl[:, :, ch, :]
                        for th in range(2):
                            ts = slice(th * HALF, (th + 1) * HALF)
                            dve.wait_ge(high_ready, a["hs"] + 2 * c + th + 1)
                            low_of(hl[:, 1, ts], c_raw[ch][:, ts], hl[:, 0, ts])
                elif kind == "forget":
                    mn = c_tmp[0:A_HEADS, 1, :]
                    then(v.tensor_scalar(mn, small[0:A_HEADS, :], bf[:], 0.0, ALU.add, ALU.min))
                    dve.wait_ge(forget_log, 1)
                    v.tensor_tensor_scan(c_raw[0][0:A_HEADS, :], mn, c_tmp[0:A_HEADS, 0, :], 0.0, ALU.add,
                                         ALU.subtract).then_inc(cum_ready, 1)
                    dve.wait_ge(cum_high, 1)
                    v.tensor_tensor(rowsT[LOW:LOW + A_HEADS, :], c_raw[0][0:A_HEADS, :], rowsT[0:A_HEADS, :].bitcast(F32),
                                    ALU.subtract).then_inc(cum_low, 1)
                    dve.wait_ge(kidx_high, 1)
                    v.tensor_tensor(kidx_hl[64:128, :], small[64:128, :], kidx_hl[64:128, :].bitcast(F32),
                                    ALU.subtract).then_inc(kidx_low, 1)
                elif kind == "natural":
                    for half, u in enumerate(a["u"]):
                        full(dve, u)
                        v.tensor_copy(wnat[:, 4 * half:4 * half + 4, :],
                                      bank[u[0]][:].rearrange("p (j c) -> p j c", j=4)[:, :, 32:32 + IDX_HEADS]
                                      ).then_inc(bank_free[u[0]], 1)
                elif kind in ("qa", "ka"):
                    th, ts = a["th"], slice(a["th"] * HALF, (a["th"] + 1) * HALF)
                    t = (Q if kind == "qa" else K)["a"][a["c"] % 2]
                    dve.wait_ge(qk_high, a["n"] + 1)
                    v.scalar_tensor_tensor(t[:, 1, ts], bank[th][:], SCALE if kind == "qa" else 1.0, t[:, 0, ts].bitcast(F32),
                                           ALU.mult, ALU.subtract).then_inc(bank_free[th], 1)
                elif kind == "b_v":
                    dve.wait_ge(v_high, 1)
                    b = a["u"][0][0]
                    v.tensor_tensor(v_st[:, 1].rearrange("p b d -> p (b d)"), bank[b][:],
                                    v_st[:, 0].bitcast(F32).rearrange("p b d -> p (b d)"), ALU.subtract).then_inc(bank_free[b], 1)
                elif kind == "b_k":
                    for th, u in enumerate(a["u"]):
                        ts = slice(th * HALF, (th + 1) * HALF)
                        dve.wait_ge(high_ready, a["hs"] + th + 1)
                        low_of(iq_st[:, 1, ts], bank[u[0]][:], iq_st[:, 0, ts])
                    for th, u in enumerate(a["u"]):
                        dve.wait_ge(low_ready, a["hs"] + th + 1)
                        dve.sem_inc(bank_free[u[0]], 1)
                elif kind in ("b_q", "i_q"):
                    q_t = bq_st[:] if kind == "b_q" else iq_st[:, a["h"] % 2, :]
                    spans = ((64, 128),) if kind == "b_q" else ((32, 64), (96, 128))
                    scale = SCALE * 2.0 ** (a["h"] + 1) if kind == "b_q" else 1.0
                    th, u = a["th"], a["u"]
                    ts = slice(th * HALF, (th + 1) * HALF)
                    dve.wait_ge(high_ready, a["hs"] + 1)
                    for p0, p1 in spans:
                        ins = v.scalar_tensor_tensor(q_t[p0:p1, ts], bank[u[0]][p0:p1, :], scale,
                                                     q_t[p0:p1, ts].bitcast(F32), ALU.mult, ALU.subtract)
                    ins.then_inc(low_ready, 1)
                    dve.wait_ge(low_ready, a["hs"] + 1)
                    dve.sem_inc(bank_free[u[0]], 1)
                elif kind == "i_dots":
                    W, i = (a["i"] + 1) * P, a["i"]
                    dve.wait_ge(slot_free, a["S"] + 1)
                    w = wnat[:, i, a["h"]:a["h"] + 1]
                    if a["h"] == 0:
                        v.tensor_scalar(score_of(i), relu_t[:, a["n"] % 2, 0:W], w, None, ALU.mult).then_inc(relu_used, 1)
                    else:
                        dve.wait_ge(relu_used, a["n"] - 5)
                        v.scalar_tensor_tensor(score_of(i), relu_t[:, a["n"] % 2, 0:W], w, score_of(i), ALU.mult,
                                               ALU.add).then_inc(relu_used, 1)
                    if a["h"] == IDX_HEADS - 1:
                        dve.wait_ge(relu_used, a["n"] + 1)
                        dve.sem_inc(score_done, 1)
                elif kind == "logits":
                    dve.wait_ge(slot_full, a["S"] + 1)
                    if a["br"] == "a" and a["b"] == 0:
                        for u in tiles["negc", 2 * a["ch"] + a["hh"]]:
                            freed(dve, u)
                    if a["br"] == "c":
                        dve.wait_ge(bias_ready, 2 * a["ch"] + a["hh"] + 1)
                    o = slot[a["S"] % 2][:, 0:a["W"]]
                    slope = 2.0 ** (-(a["h"] + 1)) if a["br"] == "b" else 1.0
                    v.tensor_tensor_reduce(o, o, logit_bias(a), -slope, 0.0, ALU.add, ALU.min,
                                           stats_of(a)[0]).then_inc(logit_ready, 1)
                elif kind == "turn":
                    for grp in a["groups"]:
                        b, n = grp["use"][0], grp["nc"]
                        if a["br"] == "b":
                            dve.wait_ge(p_high, grp["bp"] + 1)
                            hi, lo = (PT["b"][:, grp["tp"] % 2, part, 0:n, :].rearrange("p c q -> p (c q)") for part in range(2))
                            v.tensor_tensor(lo, bank[b][:, 0:n * P], hi.bitcast(F32), ALU.subtract).then_inc(bank_free[b], 1)
                    select(rate[1])
                elif kind == "stat_back":
                    freed(dve, a["use"])
                    nm = [natS[:, :, g, 0, :] for g in range(3)]
                    dn = [natS[:, :, g, 1, :] for g in range(3)]
                    then(v.tensor_tensor(mxS[:], nm[0], nm[1], ALU.min))
                    then(v.tensor_tensor(mxS[:], mxS[:], nm[2], ALU.min))
                    for g in range(3):
                        ins = v.tensor_tensor(eS[:, g], mxS[:], nm[g], ALU.subtract)
                    ins.then_inc(share_diff, 1)
                    dve.wait_ge(share_exp, 1)
                    for g in range(3):
                        then(v.tensor_tensor(wS[:, g], eS[:, g], dn[g], ALU.mult))
                    then(v.tensor_tensor(wS[:, 0], wS[:, 0], wS[:, 1], ALU.add))
                    then(v.tensor_tensor(wS[:, 0], wS[:, 0], wS[:, 2], ALU.add))
                    then(v.reciprocal(wS[:, 1], wS[:, 0]))
                    for g in range(3):
                        then(v.tensor_tensor(shareN[:, :, g, :], eS[:, g], wS[:, 1], ALU.mult))
                    dve.sem_inc(share_ready, 1)
                elif kind == "share_turn":
                    br, u = a["br"], a["use"]
                    n, rows, ts = C_HEADS if br == "c" else A_HEADS, shares[br], slice(a["half"] * HALF, (a["half"] + 1) * HALF)
                    if br != "c" and a["half"] == 0:
                        dve.wait_ge(slot_free, last_S[br, NCH[br] - 1] + 1)
                        v.reciprocal(den[:], den[:]).then_inc(share_ready, 1)
                    dve.wait_ge(high_ready, a["hs"] + 1)
                    low_of(rows[LOW:LOW + n, ts], bank[u[0]][0:n, :], rows[0:n, ts])
                    dve.wait_ge(low_ready, a["hs"] + 1)
                    dve.sem_inc(bank_free[u[0]], 1)
                elif kind == "z":
                    br, c, th = a["br"], a["c"], a["th"]
                    ts = slice(th * HALF, (th + 1) * HALF)
                    z = tm[:, 2 * th, :]
                    dve.wait_ge(z_tanh, a["zn"] + 1)
                    v.scalar_tensor_tensor(z, z, 1.0, bank[th][:], ALU.add, ALU.mult).then_inc(bank_free[th], 1)
                    freed(dve, a["u"][th])
                    sh = a["share"]
                    full(dve, sh)
                    then(v.tensor_tensor(z, z, bank[sh[0]][:], ALU.mult))
                    dve.sem_inc(bank_free[sh[0]], 1)
                    v.tensor_tensor(tm[:, 2 * th + 1, :], z, Y[br][:, c, ts], ALU.mult).then_inc(z_mul, 1)
                elif kind == "z_split":
                    br, c, th = a["br"], a["c"], a["th"]
                    ts = slice(th * HALF, (th + 1) * HALF)
                    dve.wait_ge(high_ready, a["hs"] + 1)
                    low_of(YL[br][:, c, ts], tm[:, 2 * th + 1, :], YH[br][:, c, ts])
                elif kind == "w":
                    br, c, th = a["br"], a["c"], a["th"]
                    ts = slice(th * HALF, (th + 1) * HALF)
                    full(dve, a["u"][th])
                    freed(dve, a["gate"][th])
                    gate, so_far = tm[:, 2 * (c % 2) + th, :], ms[:, c % 2, ts]
                    if br == "c":
                        if c >= 2:
                            dve.wait_ge(m_stored[c % 2], 16 * (c // 2))
                        v.scalar_tensor_tensor(so_far, gate, 1.0, bank[th][:], ALU.add, ALU.mult).then_inc(bank_free[th], 1)
                    else:
                        v.scalar_tensor_tensor(gate, gate, 1.0, bank[th][:], ALU.add, ALU.mult).then_inc(bank_free[th], 1)
                        freed(dve, a["u"][th])
                        dve.wait_ge(m_loaded[c % 2], 16 * ((KC // 2 if br == "b" else 0) + c // 2 + 1))
                        v.tensor_tensor(mT[:, c, ts] if br == "b" else so_far, so_far, gate, ALU.add).then_inc(mixed, 1)
                elif kind == "m_split":
                    for cc in a["chunks"]:
                        m_split_low(cc)
                elif kind == "final":
                    for cc in range(KC):
                        if cc >= KC - 2:
                            m_split_low(cc)
                        split_low(a["first"] + cc + 1)
                    split_low(a["first"] + 2 * KC)
                    dve.wait_ge(xo_in, 16 * TB)
                    for b in range(TB):
                        dve.wait_ge(o_full, b + 1)
                        v.tensor_tensor(xo[b][:, 0:HALF], banks8[b], xo[b][:, 0:HALF], ALU.add).then_inc(o_free, 1)
                    for b in range(TB):
                        dve.wait_ge(o_full, TB + b + 1)
                        v.tensor_tensor(xo[b][:, HALF:D], banks8[b], xo[b][:, HALF:D], ALU.add).then_inc(res_ready, 1)
                        dve.wait_ge(o_ssq, b + 1)
                        v.tensor_scalar(rstd[:, 0, b:b + 1], ssq[:, b:b + 1], 1.0 / D, EPS, ALU.mult,
                                        ALU.add).then_inc(o_var, 1)
                        dve.wait_ge(o_root, b + 1)
                        then(v.reciprocal(rstd[:, 2, b:b + 1], rstd[:, 1, b:b + 1]))
                        if b == 0:
                            dve.wait_ge(fg_in, 16)
                        v.scalar_tensor_tensor(xo[b], xo[b], rstd[:, 2, b:b + 1], fg, ALU.mult, ALU.mult).then_inc(out_ready, 1)


_INS = ["x", "norm_g", "w_in", "b_forget", "g_cq", "w_uq", "w_uq_idx", "g_ckv", "w_ukv", "w_a", "w_b", "w_c", "w_o",
        "final_g"]
_OUTS = [((1, T, D), "float32")]


def kernel(**inputs):
    import numpy as _np
    import concourse.bacc as _bacc
    from concourse import mybir as _mybir
    from concourse.bass_utils import run_bass_kernel_spmd as _run

    nc = _bacc.Bacc("TRN2", target_bir_lowering=False, num_devices=1)
    arrays, args = {}, []
    for name in _INS:
        a = _np.ascontiguousarray(inputs[name])
        arrays[f"in_{name}_dram"] = a
        args.append(nc.dram_tensor(f"in_{name}_dram", a.shape, _mybir.dt.from_np(a.dtype), kind="ExternalInput").ap())
    for i, (shape, dtype) in enumerate(_OUTS):
        dt = _mybir.dt.from_np(_np.dtype(dtype))
        args.append(nc.dram_tensor(f"out_{i}_dram", shape, dt, kind="ExternalOutput").ap())
    hybrid_layer_kernel(nc, *args)
    r = _run(nc, [arrays], core_ids=[0])
    return r.results[0]["out_0_dram"]
```
